# Optimizing a Trainium2 kernel written in Bass

```python
import math
import jax, jax.numpy as jnp
from jax import lax
import numpy as np

D_MODEL = 1024
BATCH = 1
SEQ = 512
DEPTH = 1

CHUNK = 64
N_META = 16
Q_BLOCK = 128

ATT_HEADS = 8
ATT_HEAD_DIM = 64
ATT_WIDTH = ATT_HEADS * ATT_HEAD_DIM

SSM_WIDTH = 512
SSM_GROUP = 16
SSM_GROUPS = SSM_WIDTH // SSM_GROUP
SSM_STATE = 64

N_BRANCHES = 2
IN_COLS = 3 * ATT_WIDTH + ATT_HEADS + SSM_WIDTH + N_BRANCHES * D_MODEL
SPLIT_IDX = [ATT_WIDTH, 2 * ATT_WIDTH, 3 * ATT_WIDTH, 3 * ATT_WIDTH + ATT_HEADS,
             3 * ATT_WIDTH + ATT_HEADS + SSM_WIDTH]

PEER_HEADS = 8
N_KEYS = 128
N_EXPERTS = N_KEYS * N_KEYS
PEER_TOPK = 16
KEY_DIM = 256
HALF_KEY = KEY_DIM // 2

RMS_EPS = 1e-6
NEG_INF = -1e30

kernel_name = "hybrid_fox_s5_peer_block"

def _rmsnorm(x, g):
    xf = x.astype(jnp.float32)
    y = xf * lax.rsqrt(jnp.mean(xf * xf, axis=-1, keepdims=True) + RMS_EPS)
    return (y * g.astype(jnp.float32)).astype(x.dtype)

def _forgetting_attention(q, k, v, log_f):
    B, L, H, dh = q.shape
    nb = L // Q_BLOCK
    cum = jnp.cumsum(log_f, axis=1)
    cum_k = cum.transpose(0, 2, 1)
    qf = q.astype(jnp.float32) * (dh ** -0.5)
    kf = k.astype(jnp.float32)
    vf = v.astype(jnp.float32)
    q_blocks = qf.reshape(B, nb, Q_BLOCK, H, dh).transpose(1, 0, 2, 3, 4)
    c_blocks = cum.reshape(B, nb, Q_BLOCK, H).transpose(1, 0, 3, 2)
    key_pos = jnp.arange(L)

    def one_block(args):
        qb, cb, blk = args
        s = jnp.einsum('bqhd,bkhd->bhqk', qb, kf)
        s = s + cb[..., :, None] - cum_k[:, :, None, :]
        q_pos = blk * Q_BLOCK + jnp.arange(Q_BLOCK)
        mask = key_pos[None, :] <= q_pos[:, None]
        s = jnp.where(mask, s, NEG_INF)
        p = jax.nn.softmax(s, axis=-1)
        return jnp.einsum('bhqk,bkhd->bqhd', p, vf)

    out = lax.map(one_block, (q_blocks, c_blocks, jnp.arange(nb)))
    return out.transpose(1, 0, 2, 3, 4).reshape(B, L, H * dh)

def _s5_scan(u, a_re, a_im, log_dt, b_re, b_im, c_re, c_im, d_skip):
    B, L, _ = u.shape
    uf = u.astype(jnp.float32).reshape(B, L, SSM_GROUPS, SSM_GROUP)
    ar = a_re.astype(jnp.float32)
    ai = a_im.astype(jnp.float32)
    dt = jnp.exp(log_dt.astype(jnp.float32))[:, None]
    mag = jnp.exp(ar * dt)
    abar_r = mag * jnp.cos(ai * dt)
    abar_i = mag * jnp.sin(ai * dt)
    num_r = abar_r - 1.0
    num_i = abar_i
    den = ar * ar + ai * ai
    coef_r = (num_r * ar + num_i * ai) / den
    coef_i = (num_i * ar - num_r * ai) / den
    br = b_re.astype(jnp.float32)
    bi = b_im.astype(jnp.float32)
    bbar_r = coef_r[..., None] * br - coef_i[..., None] * bi
    bbar_i = coef_r[..., None] * bi + coef_i[..., None] * br
    bu_r = jnp.einsum('blgc,gpc->blgp', uf, bbar_r)
    bu_i = jnp.einsum('blgc,gpc->blgp', uf, bbar_i)
    a_r = jnp.broadcast_to(abar_r, bu_r.shape)
    a_i = jnp.broadcast_to(abar_i, bu_i.shape)

    def combine(e1, e2):
        a1r, a1i, b1r, b1i = e1
        a2r, a2i, b2r, b2i = e2
        return (a2r * a1r - a2i * a1i,
                a2r * a1i + a2i * a1r,
                a2r * b1r - a2i * b1i + b2r,
                a2r * b1i + a2i * b1r + b2i)

    _, _, xs_r, xs_i = lax.associative_scan(combine, (a_r, a_i, bu_r, bu_i), axis=1)
    y = (jnp.einsum('blgp,gcp->blgc', xs_r, c_re.astype(jnp.float32))
         - jnp.einsum('blgp,gcp->blgc', xs_i, c_im.astype(jnp.float32))
         + d_skip.astype(jnp.float32) * uf)
    return y.reshape(B, L, SSM_WIDTH)

def _hybrid_mixer(hn, w_in, b_forget, b_gate, w_att_branch,
                  a_re, a_im, log_dt, b_re, b_im, c_re, c_im, d_skip,
                  w_glu_val, w_glu_gate, w_out):
    B, L, D = hn.shape
    proj = hn @ w_in
    q, k, v, f, u, gate = jnp.split(proj, SPLIT_IDX, axis=-1)
    log_f = jax.nn.log_sigmoid((f + b_forget).astype(jnp.float32))
    att = _forgetting_attention(q.reshape(B, L, ATT_HEADS, ATT_HEAD_DIM),
                                k.reshape(B, L, ATT_HEADS, ATT_HEAD_DIM),
                                v.reshape(B, L, ATT_HEADS, ATT_HEAD_DIM), log_f)
    branch_att = att.astype(hn.dtype) @ w_att_branch
    y = _s5_scan(u, a_re, a_im, log_dt, b_re, b_im, c_re, c_im, d_skip)
    z = jax.nn.gelu(y, approximate=False).astype(hn.dtype)
    branch_ssm = (z @ w_glu_val) * jax.nn.sigmoid(z @ w_glu_gate)
    g = jax.nn.sigmoid((gate + b_gate).astype(jnp.float32)).astype(hn.dtype)
    g = g.reshape(B, L, N_BRANCHES, D)
    merged = g[:, :, 0, :] * branch_att + g[:, :, 1, :] * branch_ssm
    return merged @ w_out

def _peer(hn, w_query, sub_keys, expert_u, expert_v):
    B, L, D = hn.shape
    nb = L // Q_BLOCK
    blocks = hn.reshape(B, nb, Q_BLOCK, D).transpose(1, 0, 2, 3)
    keys = sub_keys.astype(jnp.float32)

    def one_block(xb):
        qry = (xb @ w_query).reshape(B, Q_BLOCK, PEER_HEADS, 2, HALF_KEY).astype(jnp.float32)
        s = jnp.einsum('bqhjd,hjnd->bqhjn', qry, keys)
        v1, i1 = lax.top_k(s[..., 0, :], PEER_TOPK)
        v2, i2 = lax.top_k(s[..., 1, :], PEER_TOPK)
        cand = (v1[..., :, None] + v2[..., None, :]).reshape(B, Q_BLOCK, PEER_HEADS, PEER_TOPK * PEER_TOPK)
        best, pos = lax.top_k(cand, PEER_TOPK)
        e1 = jnp.take_along_axis(i1, pos // PEER_TOPK, axis=-1)
        e2 = jnp.take_along_axis(i2, pos % PEER_TOPK, axis=-1)
        idx = e1 * N_KEYS + e2
        gate = jax.nn.softmax(best, axis=-1)
        u_sel = expert_u[idx]
        act = jax.nn.gelu(jnp.einsum('bqhkd,bqd->bqhk', u_sel, xb).astype(jnp.float32), approximate=False)
        w = (gate * act).astype(xb.dtype)
        return jnp.einsum('bqhk,bqhkd->bqd', w, expert_v[idx])

    out = lax.map(one_block, blocks)
    return out.transpose(1, 0, 2, 3).reshape(B, L, D)

def setup_inputs(seed: int = 0) -> dict:
    key = jax.random.key(seed)
    ks = jax.random.split(key, 24)
    D = D_MODEL
    f32 = jnp.float32

    def nrm(k, shape, scale):
        return jax.random.normal(k, shape, f32) * scale

    x = jax.random.normal(ks[0], (BATCH, SEQ, D), f32)
    meta_tokens = nrm(ks[1], (N_META, D), 1.0)
    mix_norm_g = 1.0 + nrm(ks[2], (DEPTH, D), 0.02)
    w_in = nrm(ks[3], (DEPTH, D, IN_COLS), D ** -0.5)
    b_forget = jax.random.uniform(ks[4], (DEPTH, ATT_HEADS), f32, 1.0, 4.0)
    b_gate = nrm(ks[5], (DEPTH, N_BRANCHES * D), 0.01)
    w_att_branch = nrm(ks[6], (DEPTH, ATT_WIDTH, D), ATT_WIDTH ** -0.5)
    n_idx = jnp.arange(SSM_STATE, dtype=f32)
    ssm_a_re = -0.5 + nrm(ks[7], (DEPTH, SSM_GROUPS, SSM_STATE), 0.01)
    ssm_a_im = math.pi * n_idx + nrm(ks[8], (DEPTH, SSM_GROUPS, SSM_STATE), 0.01)
    ssm_log_dt = jax.random.uniform(ks[9], (DEPTH, SSM_GROUPS), f32, math.log(1e-3), math.log(1e-1))
    ssm_b_re = nrm(ks[10], (DEPTH, SSM_GROUPS, SSM_STATE, SSM_GROUP), (2 * SSM_GROUP) ** -0.5)
    ssm_b_im = nrm(ks[11], (DEPTH, SSM_GROUPS, SSM_STATE, SSM_GROUP), (2 * SSM_GROUP) ** -0.5)
    ssm_c_re = nrm(ks[12], (DEPTH, SSM_GROUPS, SSM_GROUP, SSM_STATE), (2 * SSM_STATE) ** -0.5)
    ssm_c_im = nrm(ks[13], (DEPTH, SSM_GROUPS, SSM_GROUP, SSM_STATE), (2 * SSM_STATE) ** -0.5)
    ssm_d = nrm(ks[14], (DEPTH, SSM_GROUPS, SSM_GROUP), 1.0)
    w_glu_val = nrm(ks[15], (DEPTH, SSM_WIDTH, D), SSM_WIDTH ** -0.5)
    w_glu_gate = nrm(ks[16], (DEPTH, SSM_WIDTH, D), SSM_WIDTH ** -0.5)
    w_out = nrm(ks[17], (DEPTH, D, D), D ** -0.5)
    ffn_norm_g = 1.0 + nrm(ks[18], (DEPTH, D), 0.02)
    w_query = nrm(ks[19], (DEPTH, D, PEER_HEADS * KEY_DIM), D ** -0.5)
    sub_keys = nrm(ks[20], (DEPTH, PEER_HEADS, 2, N_KEYS, HALF_KEY), HALF_KEY ** -0.5)
    expert_u = nrm(ks[21], (DEPTH, N_EXPERTS, D), D ** -0.5)
    expert_v = nrm(ks[22], (DEPTH, N_EXPERTS, D), PEER_HEADS ** -0.5)
    out_norm_g = 1.0 + nrm(ks[23], (D,), 0.02)
    return {"x": x, "meta_tokens": meta_tokens, "mix_norm_g": mix_norm_g, "w_in": w_in,
            "b_forget": b_forget, "b_gate": b_gate, "w_att_branch": w_att_branch,
            "ssm_a_re": ssm_a_re, "ssm_a_im": ssm_a_im, "ssm_log_dt": ssm_log_dt,
            "ssm_b_re": ssm_b_re, "ssm_b_im": ssm_b_im, "ssm_c_re": ssm_c_re, "ssm_c_im": ssm_c_im,
            "ssm_d": ssm_d, "w_glu_val": w_glu_val, "w_glu_gate": w_glu_gate, "w_out": w_out,
            "ffn_norm_g": ffn_norm_g, "w_query": w_query, "sub_keys": sub_keys,
            "expert_u": expert_u, "expert_v": expert_v, "out_norm_g": out_norm_g}

def reference(x, meta_tokens, mix_norm_g, w_in, b_forget, b_gate, w_att_branch,
              ssm_a_re, ssm_a_im, ssm_log_dt, ssm_b_re, ssm_b_im, ssm_c_re, ssm_c_im,
              ssm_d, w_glu_val, w_glu_gate, w_out, ffn_norm_g, w_query, sub_keys,
              expert_u, expert_v, out_norm_g):
    B, S, D = x.shape
    L = S + N_META
    L_pad = ((L + Q_BLOCK - 1) // Q_BLOCK) * Q_BLOCK
    meta = jnp.broadcast_to(meta_tokens.astype(x.dtype)[None], (B, N_META, D))
    pad = jnp.zeros((B, L_pad - L, D), x.dtype)
    h = jnp.concatenate([meta, x, pad], axis=1)
    for layer in range(DEPTH):
        hn = _rmsnorm(h, mix_norm_g[layer])
        h = h + _hybrid_mixer(hn, w_in[layer], b_forget[layer], b_gate[layer], w_att_branch[layer],
                              ssm_a_re[layer], ssm_a_im[layer], ssm_log_dt[layer],
                              ssm_b_re[layer], ssm_b_im[layer], ssm_c_re[layer], ssm_c_im[layer],
                              ssm_d[layer], w_glu_val[layer], w_glu_gate[layer], w_out[layer])
        hn = _rmsnorm(h, ffn_norm_g[layer])
        h = h + _peer(hn, w_query[layer], sub_keys[layer], expert_u[layer], expert_v[layer])
    h = _rmsnorm(h, out_norm_g)
    return h[:, N_META:N_META + S, :]


_drawn_inputs = setup_inputs


def setup_inputs(seed=0):
    import zlib

    import numpy as np

    out = dict(_drawn_inputs(seed))
    spreads = {}
    factors = {'mix_norm_g': 3.231,
     'b_gate': 22.58,
     'ssm_a_re': 64.0,
     'ssm_b_re': 3.129,
     'ssm_b_im': 3.166,
     'ssm_c_re': 3.152,
     'ssm_c_im': 3.245,
     'out_norm_g': 8.475,
     'ffn_norm_g': 4.663}
    for name, (base, spread) in spreads.items():
        noise = np.random.default_rng([zlib.crc32(name.encode()), seed]).standard_normal(out[name].shape)
        drawn = base * np.exp(spread * noise) if base else spread * noise
        out[name] = __import__('jax').numpy.asarray(drawn.astype(out[name].dtype))
    for name, factor in factors.items():
        out[name] = (out[name] * factor).astype(out[name].dtype)
    return out
```

```python
from contextlib import ExitStack
import math

import concourse.bass as bass
from concourse import mybir

ALU = mybir.AluOpType
ACT = mybir.ActivationFunctionType
AX = mybir.AxisListType
F32 = mybir.dt.float32
BF16 = mybir.dt.bfloat16
U32 = mybir.dt.uint32

P = 128
D = 1024
DC = D // P
META = 16
SEQ = 512
L = META + SEQ
TT = SEQ // P
HEADS = 8
DH = 64
AW = HEADS * DH
AC = AW // P
SW = 512
SC = SW // P
GROUPS = 32
GCH = 16
ST = 64
NT = GROUPS * ST // P
PH = 8
HK = 2 * PH
NKEY = 128
TOPK = 16
HALF = SEQ // 2
EPS = 1e-6
NEG = -1e30
X0 = 512 - META
TWO_PI_HI = 6.28125
TWO_PI_LO = 2.0 * math.pi - 6.28125
ROUND = 1.5 * 2.0 ** 23

G_WORDS = P * HALF
RING = 8
SLOT = 1024
O_COS, O_SIN = 0, NT * L
O_WOUT, O_SCORE = 0, 8192
O_KT = 2 * NT * L
O_QT = O_KT + AC * L
O_MERGED = O_KT
O_VX = O_QT + AC * SEQ
O_VM = O_VX + TT * AW
O_ATT = O_VM + AW
O_WV = O_ATT + AC * SEQ
O_Z = O_WV
O_KEYS = O_Z + SC * SEQ
O_P = O_KEYS
O_PT = O_P + 2 * L
O_U = O_WV + DC * AW
O_SMALL = O_U + SC * L
TEMP = 4160


def hybrid_program(nc, x, meta, g_mix, g_ffn, g_out, w_u, w_k, w_q, w_v, w_f, w_g, b_f, b_g, w_att, w_val,
                   w_gg, w_out, a_re, a_im, log_dt, b_re, b_im, c_re, c_im, d_skip, w_query, keys,
                   expert_u, expert_v, out):
    order = [("hn", i) for i in range(TT + 1)]
    order += [("B", 0), ("B", 1)]
    order += [("u", c) for c in range(SC)] + [("k", c) for c in range(AC)] + [("q", c) for c in range(AC)]
    order += [("f", 0)] + [("v", i) for i in range(TT + 1)]
    for i in range(NT):
        order += [("bu_re", i), ("bu_im", i)]
        if i >= 1:
            order += [("y", i - 1)]
    order += [("y", NT - 1)]
    for j in range(TT):
        for hp in range(AC):
            order += [("S", j, 2 * hp), ("S", j, 2 * hp + 1), ("PT", j, 2 * hp), ("PT", j, 2 * hp + 1), ("O", j, hp)]
    for c in range(DC):
        order += [("g0", c), ("att", c), ("g1", c), ("gg", c), ("val", c)]
    for i in range(TT):
        order += [("wout", i), ("hn2", i)]
    for n in range(HK):
        order += [("qry", n), ("sc", n)]
    for i in range(TT):
        order += [("idx", i)]
    place = {name: (n % 4, n // 4) for n, name in enumerate(order)}
    uses = [sum(1 for v in place.values() if v[0] == p) for p in range(4)]

    with ExitStack() as ctx:
        sb = lambda name, shape, dt=F32: ctx.enter_context(nc.sbuf_tensor(name, shape, dt))
        sem = lambda name: ctx.enter_context(nc.semaphore(name))
        gate_all = sb("gate_all", [P, G_WORDS])
        hnT = sb("hnT", [P, DC, L])
        ring = sb("ring", [P, RING, SLOT])
        temp = sb("temp", [P, TEMP])
        chosen = sb("chosen", [P, 3, SEQ])
        cd = sb("cd", [P, 2, NT, 32])
        ident = sb("ident", [P, P])
        iota = sb("iota", [P, P])
        identb = sb("identb", [P, P], BF16)
        maskb = sb("maskb", [P, P], BF16)
        zerob = sb("zerob", [P, 512], BF16)
        gmix = sb("gmix", [P, DC])
        gffn = sb("gffn", [P, DC])
        bgate = sb("bgate", [P, 2 * DC])
        dsk = sb("dsk", [P, SC])
        bfg = sb("bfg", [HEADS, 1])
        wf = sb("wf", [P, DC, HEADS])
        st = sb("st", [P, 64])
        h1_dram = nc.dram_tensor("h1_dram", [TT, P, D], F32, kind="Internal").ap()
        pairs = [ctx.enter_context(nc.psum_tensor(f"pair{p}", [P, 1024], F32)) for p in range(4)]

        def region(off, *shape):
            n = 1
            for s in shape:
                n *= s
            v = gate_all[:, off:off + n]
            if len(shape) == 1:
                return v
            if len(shape) == 2:
                return v.rearrange("p (a b) -> p a b", a=shape[0])
            if len(shape) == 3:
                return v.rearrange("p (a b c) -> p a b c", a=shape[0], b=shape[1])
            return v.rearrange("p (a b c d) -> p a b c d", a=shape[0], b=shape[1], c=shape[2])

        ecos, esin = region(O_COS, NT, L), region(O_SIN, NT, L)
        wout = region(O_WOUT, DC, D)
        score = region(O_SCORE, TT, HK, NKEY)
        kT, qT = region(O_KT, AC, L), region(O_QT, AC, SEQ)
        merged = region(O_MERGED, DC, SEQ)
        vx, vm = region(O_VX, TT, AW), region(O_VM, AW)
        attT, wv = region(O_ATT, AC, SEQ), region(O_WV, DC, AW)
        zT, keysT = region(O_Z, SC, SEQ), region(O_KEYS, HK, NKEY)
        prob, probT = region(O_P, 2, L), region(O_PT, 5, P)
        uT = region(O_U, SC, L)
        fgate = region(O_ATT, 2, L)
        small = region(O_SMALL, 34, NT)
        G = region(0, P, HALF)
        braw = region(O_ATT, 4, NT, GCH)
        bd = region(O_ATT + 4 * NT * GCH, 2, NT, 32)
        bprod = chosen[:, 0, :].rearrange("p (a b c) -> p a b c", a=2, b=NT)
        bT = chosen[:, 1:3, :].rearrange("p a (q s) -> p a q s", q=4)
        ptmp = ring[:, RING - 1, :]
        ncum = ring[0:HEADS, RING - 2, 0:L]
        act = temp[:, 0:2 * HALF].rearrange("p (a t) -> p a t", a=2)
        wgt = temp[:, 512:512 + 2 * HALF].rearrange("p (a t) -> p a t", a=2)
        oh1 = temp[:, 1024:2048].rearrange("p (a t) -> p a t", a=8)
        oh2 = temp[:, 2048:3072].rearrange("p (a t) -> p a t", a=8)
        h1s = temp[:, 3072:4096]
        gout = cd[:].rearrange("p a b c -> p (a b c)")

        loaded = sem("params_loaded")
        x_landed = [sem(f"x_landed{i}") for i in range(2)]
        wv_landed = sem("wv_landed")
        wout_landed = sem("wout_landed")
        keys_landed = sem("keys_landed")
        ring_landed = [sem(f"ring_landed{i}") for i in range(RING)]
        psum_filled = [sem(f"psum_filled{p}") for p in range(4)]
        psum_drained = [sem(f"psum_drained{p}") for p in range(4)]
        pool_step, dve_step, act_step = sem("pool_step"), sem("dve_step"), sem("act_step")
        consts_ready = sem("consts_ready")
        squares_summed = sem("squares_summed")
        mean_ready = sem("mean_ready")
        root_ready = sem("root_ready")
        hn_ready = sem("hn_ready")
        dt_ready, mag_ready, adt_ready, angle_ready, sincos_ready = (
            sem("dt_ready"), sem("mag_ready"), sem("adt_ready"), sem("angle_ready"), sem("sincos_ready"))
        table_ready = sem("table_ready")
        bd_ready = sem("bd_ready")
        f_shifted, f_logged, ncum_ready = sem("f_shifted"), sem("f_logged"), sem("ncum_ready")
        state_ready = sem("state_ready")
        state_used = sem("state_used")
        y_ready, z_ready = sem("y_ready"), sem("z_ready")
        rowmax_ready, exp_ready, prob_ready = sem("rowmax_ready"), sem("exp_ready"), sem("prob_ready")
        gates_ready = sem("gates_ready")
        h1_ready, h1_stored, h1_landed = sem("h1_ready"), sem("h1_stored"), sem("h1_landed")
        chosen_ready = sem("chosen_ready")
        merged_ready = sem("merged_ready")
        pv_half = sem("pv_half")
        gates_raw, gates_exp = sem("gates_raw"), sem("gates_exp")
        onehot_ready, onehot_free = sem("onehot_ready"), sem("onehot_free")
        gmat_filled, gmat_free = sem("gmat_filled"), sem("gmat_free")
        u_product, v_slot_free = sem("u_product"), sem("v_slot_free")
        gelu_done = sem("gelu_done")
        w_ready = sem("w_ready")
        acc_ready, acc_drained = sem("acc_ready"), sem("acc_drained")
        gout_landed = sem("gout_landed")
        out_ready, out_stored = sem("out_ready"), sem("out_stored")
        h2_ready, h2_squared = sem("h2_ready"), sem("h2_squared")

        negmax, rowsum, rinv, epsc = st[:, 48:50], st[:, 50:52], st[:, 52:54], st[:, 63:64]
        dve_consts = sem("dve_consts")
        topv, topi = region(0, HK, TOPK), region(256, HK, TOPK).bitcast(U32)
        topf, work, work2 = region(512, HK, TOPK), region(768, NKEY), region(896, NKEY)
        cand, cwork = region(1024, PH, TOPK * TOPK), region(3072, TOPK * TOPK)
        best, posu = region(3328, PH, TOPK), region(3456, PH, TOPK).bitcast(U32)
        hiu, lou = region(3584, PH, TOPK).bitcast(U32), region(3712, PH, TOPK).bitcast(U32)
        hif, lof = region(3840, PH, TOPK), region(3968, PH, TOPK)
        pick = region(4096, PH, TOPK, TOPK)
        norm, gexp = region(6144, PH), region(6160, PH, TOPK)

        def vacant(eng, name):
            p, k = place[name]
            if k:
                eng.wait_ge(psum_drained[p], k)

        def filled(eng, name):
            p, k = place[name]
            eng.wait_ge(psum_filled[p], k + 1)

        def drained(eng, name):
            p, k = place[name]
            eng.wait_ge(psum_drained[p], k + 1)

        pair = lambda name: pairs[place[name][0]][:, :]
        full_sem = lambda name: psum_filled[place[name][0]]
        free_sem = lambda name: psum_drained[place[name][0]]

        wloads = [("u", c, w_u[c]) for c in range(SC)] + [("k", c, w_k[c]) for c in range(AC)]
        wloads += [("q", c, w_q[c]) for c in range(AC)]
        for c in range(DC):
            wloads += [("g0", c, w_g[c]), ("att", c, w_att[c]), ("g1", c, w_g[DC + c]), ("gg", c, w_gg[c]),
                       ("val", c, w_val[c])]
        wloads += [("qry", n, w_query[n]) for n in range(HK)]
        NW = 6
        wslot = {(a, b): (n % NW, 16 * (n // NW + 1)) for n, (a, b, _) in enumerate(wloads)}
        ring_base = [16 * sum(1 for s, _ in wslot.values() if s == i) for i in range(RING)]

        def weights(name):
            return ring[:, wslot[name][0], :].rearrange("p (k m) -> p k m", m=P)

        NLOAD = 15
        block = ctx.enter_context(nc.Block())

        @block.sync
        def _(sp):
            def load_x(n, i):
                if i == 0:
                    sp.dma_start(temp[0:META, 0:D], meta).then_inc(x_landed[n % 2], 16)
                else:
                    o = (n % 2) * D
                    sp.dma_start(temp[:, o:o + D], x[(i - 1) * P:i * P, :]).then_inc(x_landed[n % 2], 16)
            load_x(0, 0)
            load_x(1, 1)
            small_loads = [(gmix[:], g_mix), (gffn[:], g_ffn), (bgate[:], b_g), (dsk[:], d_skip), (bfg[:], b_f),
                           (wf[:], w_f), (small[:, 0, :], a_re), (small[:, 1, :], a_im), (small[:, 2, :], log_dt),
                           (braw[:, 0], b_re), (braw[:, 1], b_im), (braw[:, 2], c_re), (braw[:, 3], c_im)]
            assert len(small_loads) == 13
            for dst, src in small_loads:
                sp.dma_start(dst, src).then_inc(loaded, 16)

            def load_w(n):
                a, b, src = wloads[n]
                s = n % NW
                if n >= NW:
                    filled(sp, wloads[n - NW][:2])
                size = src.shape[1]
                sp.dma_start(ring[:, s, 0:size], src).then_inc(ring_landed[s], 16)
            for n in range(NW):
                load_w(n)
            sp.dma_start(wv, w_v).then_inc(wv_landed, 16)
            for i in range(2, TT + 1):
                sp.wait_ge(hn_ready, i - 1)
                load_x(i, i)
            for n in range(NW, 12):
                load_w(n)
            for n in range(12, 18):
                load_w(n)
            sp.wait_ge(state_ready, NT)
            sp.dma_start(wout, w_out).then_inc(wout_landed, 16)
            for n in range(18, 12 + 5 * DC + 4):
                load_w(n)
                if n == 30:
                    drained(sp, ("O", TT - 1, AC - 1))
                    sp.dma_start(keysT, keys).then_inc(keys_landed, 16)
            for i in range(TT):
                if i < 2:
                    sp.wait_ge(merged_ready, DC)
                else:
                    sp.wait_ge(h1_stored, 16 * (i - 1))
                    drained(sp, ("hn2", i - 2))
                o = (i % 2) * D
                sp.dma_start(temp[:, o:o + D], x[i * P:(i + 1) * P, :]).then_inc(x_landed[i % 2], 16)
                sp.wait_ge(h1_ready, i + 1)
                sp.dma_start(h1_dram[i], temp[:, o:o + D]).then_inc(h1_stored, 16)
            for n in range(12 + 5 * DC + 4, len(wloads)):
                load_w(n)
            sp.dma_start(gout, g_out.partition_broadcast(P)).then_inc(gout_landed, 16)
            filled(sp, ("qry", HK - 1))

            for hf in range(2):
                with sp.Fori(0, P // 4) as it:
                    for s in range(4):
                        n = it * 4 + s + hf * P
                        blk = bass.ds(it * 4 + s, 1)
                        sp.wait_ge(v_slot_free, n + 1)
                        sp.dma_start(ring[:, s, :], expert_u[blk].rearrange("a p n -> p (a n)"))\
                          .then_inc(ring_landed[s], 16)
                        sp.dma_start(ring[:, 4 + s, :], expert_v[blk].rearrange("a p n -> p (a n)"))\
                          .then_inc(ring_landed[4 + s], 16)

        @block.gpsimd
        def _(pool):
            steps = [0]

            def chain(ins):
                steps[0] += 1
                ins.then_inc(pool_step, 1)
                pool.wait_ge(pool_step, steps[0])
            chain(pool.memset(ident[:], 0.0))
            chain(pool.affine_select(out=ident[:], in_=ident[:], compare_op=ALU.not_equal, fill=1.0, base=0,
                                     pattern=[[-1, P]], channel_multiplier=1))
            chain(pool.tensor_copy(identb[:], ident[:]))
            chain(pool.memset(maskb[:], 0.0))
            chain(pool.affine_select(out=maskb[:], in_=maskb[:], compare_op=ALU.is_ge, fill=NEG, base=0,
                                     pattern=[[-1, P]], channel_multiplier=1))
            chain(pool.iota(iota[:], [[1, P]], base=0, channel_multiplier=0, allow_small_or_imprecise_dtypes=True))
            chain(pool.memset(zerob[:], 0.0))
            pool.memset(cd[:], 0.0).then_inc(consts_ready, 1)
            pool.memset(ecos[:, :, 0:1], 1.0)
            chain(pool.memset(esin[:, :, 0:1], 0.0))
            pool.wait_ge(sincos_ready, 1)
            ec, es = small[:, 10, :], small[:, 11, :]
            turn = [(small[:, 28, :], small[:, 29, :]), (small[:, 30, :], small[:, 31, :])]
            t1, t2 = small[:, 32, :], small[:, 33, :]
            n, lvl = 1, 0
            while n < L:
                m = min(n, L - n)
                cn, sn = turn[lvl % 2] if lvl else (ec, es)
                cn2, sn2 = turn[(lvl + 1) % 2]
                per = max(1, min(NT, SLOT // m))
                for a in range(0, NT, per):
                    b = a + per
                    tmp = ptmp[:, 0:per * m].rearrange("p (a b) -> p a b", a=per)
                    bc = cn[:, a:b].unsqueeze(2).to_broadcast([P, per, m])
                    bs = sn[:, a:b].unsqueeze(2).to_broadcast([P, per, m])
                    src_c, src_s = ecos[:, a:b, 0:m], esin[:, a:b, 0:m]
                    dst_c, dst_s = ecos[:, a:b, n:n + m], esin[:, a:b, n:n + m]
                    chain(pool.tensor_tensor(dst_c, src_c, bc, ALU.mult))
                    chain(pool.tensor_tensor(tmp, src_s, bs, ALU.mult))
                    chain(pool.tensor_tensor(dst_c, dst_c, tmp, ALU.subtract))
                    chain(pool.tensor_tensor(dst_s, src_s, bc, ALU.mult))
                    chain(pool.tensor_tensor(tmp, src_c, bs, ALU.mult))
                    chain(pool.tensor_tensor(dst_s, dst_s, tmp, ALU.add))
                chain(pool.tensor_tensor(t1, cn, cn, ALU.mult))
                chain(pool.tensor_tensor(t2, sn, sn, ALU.mult))
                chain(pool.tensor_tensor(cn2, t1, t2, ALU.subtract))
                chain(pool.tensor_tensor(t1, cn, sn, ALU.mult))
                chain(pool.tensor_tensor(sn2, t1, t1, ALU.add))
                n *= 2
                lvl += 1
            pool.memset(t1, 0.0).then_inc(table_ready, 1)
            pool.wait_ge(h1_stored, 16 * TT)
            for g in range(TT):
                if g == 0:
                    pool.wait_ge(onehot_free, 8)
                else:
                    pool.wait_ge(out_stored, 16 * g)
                pool.dma_start(h1s, h1_dram[g]).then_inc(h1_landed, 16)
                pool.wait_ge(out_ready, g + 1)
                pool.dma_start(out[g * P:(g + 1) * P, :], h1s).then_inc(out_stored, 16)
            pool.wait_ge(out_stored, 16 * TT)

        @block.tensor
        def _(pe):
            pe.wait_ge(consts_ready, 1)

            def transposes(name, i, src, rows):
                vacant(pe, name)
                for c in range(DC):
                    mm = pe.transpose(pair(name)[:, c * P:c * P + rows], src[0:rows, c * P:(c + 1) * P], ident[0:rows, 0:rows])
                mm.then_inc(full_sem(name), 1)

            for i in range(TT + 1):
                pe.wait_ge(hn_ready, i + 1)
                o = 2 * D + (i % 2) * D
                transposes(("hn", i), i, temp[:, o:o + D], META if i == 0 else P)
            pe.wait_ge(bd_ready, 1)
            for a in range(2):
                vacant(pe, ("B", a))
                for q in range(4):
                    mm = pe.transpose(pair(("B", a))[:, q * P:(q + 1) * P],
                                      bd[:, a, 4 * q:4 * q + 4, :].rearrange("p a b -> p (a b)"), ident[:])
                mm.then_inc(full_sem(("B", a)), 1)
            for i in range(TT + 1):
                drained(pe, ("hn", i))

            def project(name, rhs, kc, cols):
                vacant(pe, name)
                s, v = wslot[name]
                pe.wait_ge(ring_landed[s], v)
                w = weights(name)
                for (dst, lo, hi) in cols:
                    for c in range(kc):
                        mm = pe.matmul(pair(name)[:, dst:dst + hi - lo], w[:, c, :], rhs[:, c, lo:hi],
                                       start=(c == 0), stop=(c == kc - 1))
                mm.then_inc(full_sem(name), 1)

            both = [(X0, 0, META), (512, META, L)]
            for c in range(SC):
                project(("u", c), hnT, DC, both)
            for c in range(AC):
                project(("k", c), hnT, DC, both)
            for c in range(AC):
                project(("q", c), hnT, DC, [(0, META, L)])
            vacant(pe, ("f", 0))
            pe.wait_ge(loaded, 13 * 16)
            for dst, lo, hi in both:
                for c in range(DC):
                    mm = pe.matmul(pair(("f", 0))[0:HEADS, dst:dst + hi - lo], wf[:, c, :], hnT[:, c, lo:hi],
                                   start=(c == 0), stop=(c == DC - 1))
            mm.then_inc(full_sem(("f", 0)), 1)
            pe.wait_ge(wv_landed, 16)
            for i in range(TT + 1):
                vacant(pe, ("v", i))
                lo, n = (0, META) if i == 0 else (META + (i - 1) * P, P)
                for c in range(DC):
                    mm = pe.matmul(pair(("v", i))[0:n, 0:AW], hnT[:, c, lo:lo + n], wv[:, c, :],
                                   start=(c == 0), stop=(c == DC - 1))
                mm.then_inc(full_sem(("v", i)), 1)

            for a in range(2):
                drained(pe, ("B", a))
            for c in range(SC):
                drained(pe, ("u", c))

            def c_times_x(i):
                name = ("y", i)
                vacant(pe, name)
                pe.wait_ge(state_ready, i + 1)
                q = 32 * (i % 4)
                for a in range(2):
                    o = 4 * L + (2 * (i % 2) + a) * 512
                    mm = pe.matmul(pair(name)[q:q + 32, 0:SEQ], cd[:, a, i, :], temp[:, o:o + SEQ],
                                   start=(a == 0), stop=(a == 1))
                mm.then_inc(full_sem(name), 1)

            for i in range(NT):
                q = 32 * (i % 4)
                for a, kind in enumerate(("bu_re", "bu_im")):
                    name = (kind, i)
                    vacant(pe, name)
                    for dst, lo, hi in both:
                        mm = pe.matmul(pair(name)[:, dst:dst + hi - lo], bT[q:q + 32, a, i // 4, :],
                                       uT[q:q + 32, i // 4, lo:hi], start=True, stop=True)
                    mm.then_inc(full_sem(name), 1)
                if i >= 1:
                    c_times_x(i - 1)
            c_times_x(NT - 1)

            pe.wait_ge(ncum_ready, 1)
            for c in range(AC):
                drained(pe, ("k", c))
                drained(pe, ("q", c))
            for i in range(TT + 1):
                drained(pe, ("v", i))
            for j in range(TT):
                keys_x = (j + 1) * P
                for hp in range(AC):
                    for h in (2 * hp, 2 * hp + 1):
                        name = ("S", j, h)
                        vacant(pe, name)
                        b = 64 * (h % 2)
                        q = qT[b:b + 64, hp, j * P:(j + 1) * P]
                        eh = ident[0:HEADS, h:h + 1].to_broadcast([HEADS, P])
                        S = pair(name)
                        pe.matmul(S[:, X0:512], q, kT[b:b + 64, hp, 0:META], start=True, stop=False)
                        pe.matmul(S[:, X0:512], eh, ncum[:, 0:META], start=False, stop=True)
                        pe.matmul(S[:, 512:512 + keys_x], q, kT[b:b + 64, hp, META:META + keys_x], start=True, stop=False)
                        pe.matmul(S[:, 512:512 + keys_x], eh, ncum[:, META:META + keys_x], start=False, stop=False)
                        pe.matmul(S[:, 512 + keys_x - P:512 + keys_x], identb[:], maskb[:], start=False, stop=True)\
                          .then_inc(full_sem(name), 1)
                    for h in (2 * hp, 2 * hp + 1):
                        name = ("PT", j, h)
                        vacant(pe, name)
                        pe.wait_ge(prob_ready, j * HEADS + h + 1)
                        pe.transpose(pair(name)[0:META, 4 * P:5 * P], prob[:, h % 2, 0:META], ident[:])
                        for s in range(j + 1):
                            mm = pe.transpose(pair(name)[:, s * P:(s + 1) * P],
                                              prob[:, h % 2, META + s * P:META + (s + 1) * P], ident[:])
                        mm.then_inc(full_sem(name), 1)
                        o = ("O", j, hp)
                        if h % 2 == 0:
                            vacant(pe, o)
                        drained(pe, name)
                        b = 64 * (h % 2)
                        O = pair(o)[b:b + 64, 0:P]
                        pe.matmul(O, vm[0:META, h * DH:(h + 1) * DH], probT[0:META, 4, :], start=True, stop=False)
                        for s in range(j + 1):
                            mm = pe.matmul(O, vx[:, s, h * DH:(h + 1) * DH], probT[:, s, :], start=False, stop=(s == j))
                        if h % 2 == 0:
                            mm.then_inc(pv_half, 1)
                        else:
                            mm.then_inc(full_sem(o), 1)

            pe.wait_ge(z_ready, SC)
            for hp in range(AC):
                drained(pe, ("O", TT - 1, hp))
            x_cols = [(0, META, L)]
            t_cols = [(0, 0, SEQ)]
            for c in range(DC):
                project(("g0", c), hnT, DC, x_cols)
                project(("att", c), attT, AC, t_cols)
                project(("g1", c), hnT, DC, x_cols)
                project(("gg", c), zT, SC, t_cols)
                project(("val", c), zT, SC, t_cols)
            pe.wait_ge(wout_landed, 16)
            pe.wait_ge(merged_ready, DC)
            for i in range(TT):
                name = ("wout", i)
                vacant(pe, name)
                for hf in range(2):
                    for c in range(DC):
                        mm = pe.matmul(pair(name)[:, hf * 512:(hf + 1) * 512], merged[:, c, i * P:(i + 1) * P],
                                       wout[:, c, hf * 512:(hf + 1) * 512], start=(c == 0), stop=(c == DC - 1))
                mm.then_inc(full_sem(name), 1)
                pe.wait_ge(hn_ready, TT + 2 + i)
                o = 2 * D + (i % 2) * D
                transposes(("hn2", i), i, temp[:, o:o + D], P)

            for i in range(TT):
                drained(pe, ("hn2", i))
            pe.wait_ge(keys_landed, 16)
            for n in range(HK):
                project(("qry", n), hnT, DC, t_cols)
                name = ("sc", n)
                vacant(pe, name)
                drained(pe, ("qry", n))
                for i in range(TT):
                    mm = pe.matmul(pair(name)[:, i * P:(i + 1) * P], temp[:, (n % 2) * 512 + i * P:(n % 2) * 512 + (i + 1) * P],
                                   keysT[:, n, :], start=True, stop=True)
                mm.then_inc(full_sem(name), 1)
            for i in range(TT):
                name = ("idx", i)
                vacant(pe, name)
                pe.wait_ge(chosen_ready, i + 1)
                for a in range(3):
                    mm = pe.transpose(pair(name)[:, a * P:(a + 1) * P], temp[:, (i % 2) * 384 + a * P + 2048:(i % 2) * 384 + (a + 1) * P + 2048], ident[:])
                mm.then_inc(full_sem(name), 1)

            for p in range(4):
                pe.wait_ge(psum_drained[p], uses[p])
            pe.sem_inc(onehot_free, 8)
            pe.sem_inc(v_slot_free, 4)

            def open_and_close(start):
                for p in range(2):
                    for b in range(2):
                        mm = pe.matmul(pairs[p][:, b * 512:(b + 1) * 512], zerob[:, 0:P], zerob[:], start=start,
                                       stop=not start, skip_group_check=True)
                return mm

            for hf in range(2):
                def u_part(s, n, k):
                    pe.wait_ge(ring_landed[s], k + ring_base[s] + hf * (P // 4) * 16)
                    for c in range(DC):
                        mm = pe.matmul(pairs[2 + s % 2][:, 0:HALF], ring[:, s, c * P:(c + 1) * P],
                                       hnT[:, c, hf * HALF:(hf + 1) * HALF], start=(c == 0), stop=(c == DC - 1))
                    mm.then_inc(u_product, 1)

                def v_part(s, n, k):
                    pe.wait_ge(ring_landed[4 + s], k + ring_base[4 + s] + hf * (P // 4) * 16)
                    pe.wait_ge(w_ready, n + 1)
                    for i in range(2):
                        for b in range(2):
                            mm = pe.matmul(pairs[i][:, b * 512:(b + 1) * 512], wgt[:, s % 2, i * P:(i + 1) * P],
                                           ring[:, 4 + s, b * 512:(b + 1) * 512], start=False, stop=False,
                                           skip_group_check=True)
                    mm.then_inc(v_slot_free, 1)

                with pe.Fori(0, HALF // 16) as it:
                    for s in range(4):
                        g = it * 4 + s + hf * (HALF // 4)
                        pe.wait_ge(gmat_free, g + 1)
                        for t in range(4):
                            pe.wait_ge(onehot_ready, g * 4 + t + 1)
                            k = (s % 2) * 4 + t
                            pe.matmul(pairs[2 + s // 2][:, (s % 2) * 512 + t * P:(s % 2) * 512 + (t + 1) * P],
                                      oh2[:, k, :], oh1[:, k, :], start=True, stop=True).then_inc(onehot_free, 1)
                pe.wait_ge(gmat_free, 4 + (hf + 1) * HALF // 4)
                if hf:
                    pe.wait_ge(acc_drained, 2)
                open_and_close(True)
                u_part(0, hf * P, 16)
                with pe.Fori(0, P // 4 - 1) as it:
                    for s in range(4):
                        n = it * 4 + s + hf * P
                        pe.wait_ge(gelu_done, n + 1)
                        u_part((s + 1) % 4, n + 1, it * 16 + (16 if s < 3 else 32))
                        v_part(s, n, it * 16 + 16)
                for s in range(4):
                    n = P - 4 + s + hf * P
                    if s < 3:
                        pe.wait_ge(gelu_done, n + 1)
                        u_part(s + 1, n + 1, (P // 4) * 16)
                    v_part(s, n, (P // 4) * 16)
                open_and_close(False).then_inc(acc_ready, 1)

        @block.scalar
        def _(ac):
            def final(g):
                ac.wait_ge(h2_ready, g + 1)
                ac.activation(pairs[g % 2][:, :], h1s, ACT.Square, accum_out=st[:, 9 + g:10 + g]).then_inc(acc_drained, 1)
                ac.wait_ge(acc_drained, g + 1)
                ac.activation(st[:, 25 + g:26 + g], st[:, 9 + g:10 + g], ACT.Sqrt, bias=epsc,
                              scale=1.0 / D).then_inc(root_ready, 1)

            def rms(tile, src, rows, junk):
                ac.activation(junk, src, ACT.Square, accum_out=st[0:rows, tile:tile + 1]).then_inc(act_step, 1)
                steps[0] += 1
                ac.wait_ge(act_step, steps[0])
                ac.activation(st[0:rows, 16 + tile:17 + tile], st[0:rows, tile:tile + 1], ACT.Sqrt,
                              bias=epsc[0:rows, :], scale=1.0 / D).then_inc(root_ready, 1)
            steps = [0]
            ac.wait_ge(dve_consts, 1)
            ac.wait_ge(loaded, 13 * 16)
            ac.activation(small[:, 3, :], small[:, 2, :], ACT.Exp).then_inc(dt_ready, 1)
            ac.wait_ge(adt_ready, 1)
            ac.activation(small[:, 5, :], small[:, 4, :], ACT.Exp).then_inc(mag_ready, 1)
            ac.wait_ge(angle_ready, 1)
            ac.activation(small[:, 11, :], small[:, 8, :], ACT.Sin)
            ac.activation(small[:, 10, :], small[:, 9, :], ACT.Sin).then_inc(sincos_ready, 1)
            for i in range(TT + 1):
                rows = META if i == 0 else P
                ac.wait_ge(x_landed[i % 2], 16 * (i // 2 + 1))
                if i >= 2:
                    filled(ac, ("hn", i - 2))
                o = (i % 2) * D
                rms(i, temp[0:rows, o:o + D], rows, temp[0:rows, 2 * D + o:3 * D + o])

            def evac(name, dst, cols, scale=1.0, rows=P):
                filled(ac, name)
                ac.activation(dst, pair(name)[0:rows, cols[0]:cols[1]], ACT.Copy, scale=scale).then_inc(free_sem(name), 1)

            ac.wait_ge(bd_ready, 1)
            for a in range(2):
                evac(("B", a), bT[:, a].rearrange("p q s -> p (q s)"), (0, 512))
            for c in range(SC):
                evac(("u", c), uT[:, c, :], (X0, X0 + L))
            for c in range(AC):
                evac(("k", c), kT[:, c, :], (X0, X0 + L))
            for c in range(AC):
                evac(("q", c), qT[:, c, :], (0, SEQ), scale=DH ** -0.5)
            ac.wait_ge(f_shifted, 1)
            ac.activation(fgate[0:HEADS, 1, :], fgate[0:HEADS, 1, :], ACT.Exp).then_inc(act_step, 1)
            steps[0] += 1
            ac.wait_ge(act_step, steps[0])
            ac.activation(fgate[0:HEADS, 1, :], fgate[0:HEADS, 1, :], ACT.Ln, bias=1.0).then_inc(f_logged, 1)
            evac(("v", 0), vm[0:META, :], (0, AW), rows=META)
            for i in range(1, TT + 1):
                evac(("v", i), vx[:, i - 1, :], (0, AW))
            for c in range(SC):
                ac.wait_ge(y_ready, 4 * (c + 1))
                ac.activation(zT[:, c, :], zT[:, c, :], ACT.Gelu).then_inc(z_ready, 1)
            ac.wait_ge(ncum_ready, 1)
            for j in range(TT):
                n = META + (j + 1) * P
                for hp in range(AC):
                    for h in (2 * hp, 2 * hp + 1):
                        k = j * HEADS + h
                        ac.wait_ge(rowmax_ready, k + 1)
                        if k >= 2:
                            filled(ac, ("PT", (k - 2) // HEADS, (k - 2) % HEADS))
                        name = ("S", j, h)
                        ac.activation(prob[:, h % 2, 0:n], pair(name)[:, X0:X0 + n], ACT.Exp, bias=negmax[:, h % 2:h % 2 + 1],
                                      accum_out=rowsum[:, h % 2:h % 2 + 1]).then_inc(exp_ready, 1)
                    for h in (2 * hp, 2 * hp + 1):
                        k = j * HEADS + h
                        name = ("PT", j, h)
                        filled(ac, name)
                        if h % 2:
                            ac.wait_ge(pv_half, k // 2 + 1)
                        elif k:
                            filled(ac, ("O", (k - 1) // HEADS, (k - 1) % HEADS // 2))
                        ac.activation(probT[0:META, 4, :], pair(name)[0:META, 4 * P:5 * P], ACT.Copy)
                        ac.activation(probT[:, 0:j + 1, :].rearrange("p a b -> p (a b)"), pair(name)[:, 0:(j + 1) * P],
                                      ACT.Copy).then_inc(free_sem(name), 1)
            for c in range(DC):
                base = (c % 2) * 2048
                if c >= 2:
                    ac.wait_ge(merged_ready, c - 1)
                for n, (kind, bias) in enumerate((("g0", bgate[:, c:c + 1]), ("g1", bgate[:, DC + c:DC + c + 1]), ("gg", 0.0))):
                    name = (kind, c)
                    filled(ac, name)
                    ac.activation(temp[:, base + n * 512:base + (n + 1) * 512], pair(name)[:, 0:SEQ], ACT.Sigmoid,
                                  bias=bias).then_inc(free_sem(name), 1)
            for i in range(TT):
                ac.wait_ge(h1_ready, i + 1)
                if i < 2:
                    ac.wait_ge(merged_ready, DC)
                else:
                    filled(ac, ("hn2", i - 2))
                o = (i % 2) * D
                rms(TT + 1 + i, temp[:, o:o + D], P, temp[:, 2 * D + o:3 * D + o])
            ac.wait_ge(h1_stored, 16 * TT)
            for i in range(TT):
                drained(ac, ("hn2", i))
            for n in range(HK):
                if n >= 2:
                    filled(ac, ("sc", n - 2))
                evac(("qry", n), temp[:, (n % 2) * 512:(n % 2 + 1) * 512], (0, SEQ))
            for i in range(TT):
                ac.wait_ge(gates_raw, i + 1)
                ac.activation(gexp, gexp, ACT.Exp).then_inc(gates_exp, 1)
                name = ("idx", i)
                filled(ac, name)
                ac.activation(chosen[:, :, i * P:(i + 1) * P], pair(name)[:, 0:3 * P].rearrange("p (a t) -> p a t", a=3),
                              ACT.Copy).then_inc(free_sem(name), 1)
            ac.sem_inc(gmat_free, 4)
            ac.sem_inc(gelu_done, 1)
            for hf in range(2):
                if hf:
                    ac.wait_ge(w_ready, P)
                with ac.Fori(0, HALF // 16) as it:
                    for s in range(4):
                        g = it * 4 + s + hf * (HALF // 4)
                        ac.wait_ge(onehot_free, g * 4 + 12)
                        ac.activation(G[:, :, bass.ds(it * 16 + s * 4, 4)],
                                      pairs[2 + s // 2][:, (s % 2) * 512:(s % 2 + 1) * 512].rearrange("p (t e) -> p e t", t=4),
                                      ACT.Copy).then_inc(gmat_free, 1)
                if hf:
                    for i in range(2):
                        final(i)
                with ac.Fori(0, P // 4) as it:
                    for s in range(4):
                        n = it * 4 + s + hf * P
                        ac.wait_ge(u_product, n + 1)
                        ac.activation(act[:, s % 2, :], pairs[2 + s % 2][:, 0:HALF], ACT.Gelu).then_inc(gelu_done, 1)
            for i in range(2, 4):
                final(i)

        @block.vector
        def _(dve):
            steps = [0]

            def chain(ins):
                steps[0] += 1
                ins.then_inc(dve_step, 1)
                dve.wait_ge(dve_step, steps[0])

            def mul(out, a, b):
                return dve.tensor_tensor(out, a, b, ALU.mult)

            dve.memset(bd.rearrange("p a n c -> p (a n c)"), 0.0)
            dve.memset(epsc, EPS).then_inc(dve_consts, 1)
            dve.wait_ge(dve_consts, 1)
            dve.wait_ge(loaded, 13 * 16)
            S = lambda k: small[:, k, :]
            are, aim, dt, adt, mag, th, kk, ang, cosarg, cosv, sinv = (S(0), S(1), S(3), S(4), S(5), S(6), S(7), S(8),
                                                                      S(9), S(10), S(11))
            abr, abi, numr, den, tm, rden, cr, ci = S(12), S(13), S(14), S(15), S(16), S(17), S(18), S(19)
            dve.wait_ge(dt_ready, 1)
            mul(adt, are, dt).then_inc(adt_ready, 1)
            chain(mul(th, aim, dt))
            chain(dve.tensor_scalar(kk, th, 1.0 / (2 * math.pi), ROUND, ALU.mult, ALU.add))
            chain(dve.tensor_scalar(kk, kk, -ROUND, None, ALU.add))
            chain(dve.scalar_tensor_tensor(out=ang, in0=kk, scalar=-TWO_PI_HI, in1=th, op0=ALU.mult, op1=ALU.add))
            chain(dve.scalar_tensor_tensor(out=ang, in0=kk, scalar=-TWO_PI_LO, in1=ang, op0=ALU.mult, op1=ALU.add))
            chain(dve.tensor_scalar(ang, ang, 3.1415925, -3.1415925, ALU.min, ALU.max))
            chain(dve.scalar_tensor_tensor(out=cosarg, in0=ang, scalar=-1.0, in1=ang, op0=ALU.mult, op1=ALU.min))
            dve.tensor_scalar(cosarg, cosarg, math.pi / 2, None, ALU.add).then_inc(angle_ready, 1)
            dve.wait_ge(sincos_ready, 1)
            dve.wait_ge(mag_ready, 1)
            mul(abr, mag, cosv)
            chain(mul(abi, mag, sinv))
            chain(dve.tensor_scalar(numr, abr, -1.0, None, ALU.add))
            mul(den, are, are)
            chain(mul(tm, aim, aim))
            chain(dve.tensor_tensor(den, den, tm, ALU.add))
            chain(dve.reciprocal(rden, den))
            mul(cr, numr, are)
            chain(mul(tm, abi, aim))
            chain(dve.tensor_tensor(cr, cr, tm, ALU.add))
            chain(mul(cr, cr, rden))
            mul(ci, abi, are)
            chain(mul(tm, numr, aim))
            chain(dve.tensor_tensor(ci, ci, tm, ALU.subtract))
            chain(mul(ci, ci, rden))
            crb = cr.unsqueeze(2).to_broadcast([P, NT, GCH])
            cib = ci.unsqueeze(2).to_broadcast([P, NT, GCH])
            for a, (p, q, op) in enumerate((((crb, 0), (cib, 1), ALU.subtract), ((crb, 1), (cib, 0), ALU.add))):
                mul(bprod[:, 0], braw[:, p[1]], p[0])
                chain(mul(bprod[:, 1], braw[:, q[1]], q[0]))
                dve.tensor_tensor(bd[0:64, a, :, 0:GCH], bprod[0:64, 0], bprod[0:64, 1], op)
                ins = dve.tensor_tensor(bd[64:P, a, :, GCH:32], bprod[64:P, 0], bprod[64:P, 1], op)
                chain(ins) if a == 0 else ins.then_inc(bd_ready, 1)
            dve.wait_ge(consts_ready, 1)
            for g in range(2):
                r = slice(64 * g, 64 * g + 64)
                dve.tensor_copy(cd[r, 0, :, GCH * g:GCH * (g + 1)], braw[r, 2])
                dve.tensor_scalar(cd[r, 1, :, GCH * g:GCH * (g + 1)], braw[r, 3], -1.0, None, ALU.mult)

            def normalise(tile, src, dst, rows):
                dve.wait_ge(root_ready, tile + 1)
                chain(dve.reciprocal(st[0:rows, 32 + tile:33 + tile], st[0:rows, 16 + tile:17 + tile]))
                dve.tensor_scalar(dst, src, st[0:rows, 32 + tile:33 + tile], None, ALU.mult).then_inc(hn_ready, 1)

            def to_features(name, dst, rows, gain):
                filled(dve, name)
                mul(dst, pair(name).rearrange("p (c t) -> p c t", c=DC)[:, :, 0:rows],
                    gain[:, :].unsqueeze(2).to_broadcast([P, DC, rows])).then_inc(free_sem(name), 1)

            for i in range(TT + 1):
                rows = META if i == 0 else P
                o = (i % 2) * D
                normalise(i, temp[0:rows, o:o + D], temp[0:rows, 2 * D + o:3 * D + o], rows)
                lo = 0 if i == 0 else META + (i - 1) * P
                to_features(("hn", i), hnT[:, :, lo:lo + rows], rows, gmix)

            fx, fe = fgate[0:HEADS, 0, :], fgate[0:HEADS, 1, :]
            name = ("f", 0)
            filled(dve, name)
            dve.tensor_scalar(fx, pair(name)[0:HEADS, X0:X0 + L], bfg[:, 0:1], None, ALU.add).then_inc(free_sem(name), 1)
            drained(dve, name)
            dve.scalar_tensor_tensor(out=fe, in0=fx, scalar=-1.0, in1=fx, op0=ALU.mult, op1=ALU.min).then_inc(f_shifted, 1)
            dve.wait_ge(f_logged, 1)
            chain(dve.scalar_tensor_tensor(out=fe, in0=fx, scalar=0.0, in1=fe, op0=ALU.min, op1=ALU.subtract))
            chain(dve.tensor_scalar(fe, fe, -1.0, None, ALU.mult))
            chain(dve.memset(fx, 0.0))
            dve.tensor_tensor_scan(ncum, fe, fx, 0.0, ALU.add, ALU.add).then_inc(ncum_ready, 1)

            dve.wait_ge(table_ready, 1)
            m1, m2, m3, m4 = (temp[:, k * L:(k + 1) * L] for k in range(4))

            def gain_and_skip(i):
                name = ("y", i)
                filled(dve, name)
                q = 32 * (i % 4)
                dve.scalar_tensor_tensor(out=zT[q:q + 32, i // 4, :], in0=uT[q:q + 32, i // 4, META:L],
                                         scalar=dsk[q:q + 32, i // 4:i // 4 + 1], in1=pair(name)[q:q + 32, 0:SEQ],
                                         op0=ALU.mult, op1=ALU.add).then_inc(free_sem(name), 1)

            for i in range(NT):
                c, s = ecos[:, i, :], esin[:, i, :]
                re, im = ("bu_re", i), ("bu_im", i)
                filled(dve, re)
                bre, bim = pair(re)[:, X0:X0 + L], pair(im)[:, X0:X0 + L]
                mul(m1, bre, c)
                mul(m4, bre, s).then_inc(free_sem(re), 1)
                filled(dve, im)
                mul(m2, bim, s)
                mul(m3, bim, c).then_inc(free_sem(im), 1)
                drained(dve, re)
                drained(dve, im)
                dve.tensor_tensor(m1, m1, m2, ALU.add)
                chain(dve.tensor_tensor(m3, m3, m4, ALU.subtract))
                decay = mag[:, i:i + 1].to_broadcast([P, L])
                dve.tensor_tensor_scan(m2, decay, m1, 0.0, ALU.mult, ALU.add)
                chain(dve.tensor_tensor_scan(m4, decay, m3, 0.0, ALU.mult, ALU.add))
                xs = [temp[:, 4 * L + (2 * (i % 2) + a) * 512:4 * L + (2 * (i % 2) + a + 1) * 512] for a in range(2)]
                cx, sx, yr, yi = c[:, META:L], s[:, META:L], m2[:, META:L], m4[:, META:L]
                mul(m1[:, 0:SEQ], yr, cx)
                chain(mul(m3[:, 0:SEQ], yi, sx))
                if i >= 2:
                    filled(dve, ("y", i - 2))
                chain(dve.tensor_tensor(xs[0], m1[:, 0:SEQ], m3[:, 0:SEQ], ALU.subtract))
                mul(m1[:, 0:SEQ], yr, sx)
                chain(mul(m3[:, 0:SEQ], yi, cx))
                dve.tensor_tensor(xs[1], m1[:, 0:SEQ], m3[:, 0:SEQ], ALU.add).then_inc(state_ready, 1)
                dve.wait_ge(state_ready, i + 1)
                if i >= 1:
                    gain_and_skip(i - 1)
            gain_and_skip(NT - 1)
            for i in range(NT):
                drained(dve, ("y", i))
            dve.engine_nop().then_inc(y_ready, 4 * SC)

            for j in range(TT):
                n = META + (j + 1) * P
                for hp in range(AC):
                    for h in (2 * hp, 2 * hp + 1):
                        name = ("S", j, h)
                        filled(dve, name)
                        dve.tensor_reduce(negmax[:, h % 2:h % 2 + 1], pair(name)[:, X0:X0 + n], AX.X, ALU.max,
                                          negate=True).then_inc(rowmax_ready, 1)
                    for h in (2 * hp, 2 * hp + 1):
                        name = ("S", j, h)
                        dve.wait_ge(exp_ready, j * HEADS + h + 1)
                        dve.reciprocal(rinv[:, h % 2:h % 2 + 1], rowsum[:, h % 2:h % 2 + 1]).then_inc(free_sem(name), 1)
                        drained(dve, name)
                        dve.tensor_scalar(prob[:, h % 2, 0:n], prob[:, h % 2, 0:n], rinv[:, h % 2:h % 2 + 1], None,
                                          ALU.mult).then_inc(prob_ready, 1)
                    name = ("O", j, hp)
                    filled(dve, name)
                    dve.tensor_copy(attT[:, hp, j * P:(j + 1) * P], pair(name)[:, 0:P]).then_inc(free_sem(name), 1)

            for c in range(DC):
                b = (c % 2) * 2048
                g0, g1, gg, t = (temp[:, b + k * 512:b + (k + 1) * 512] for k in range(4))
                name = ("att", c)
                filled(dve, name)
                drained(dve, ("g0", c))
                mul(merged[:, c, :], pair(name)[:, 0:SEQ], g0).then_inc(free_sem(name), 1)
                name = ("val", c)
                filled(dve, name)
                drained(dve, ("gg", c))
                mul(t, pair(name)[:, 0:SEQ], gg).then_inc(free_sem(name), 1)
                drained(dve, name)
                drained(dve, ("g1", c))
                chain(mul(t, t, g1))
                drained(dve, ("att", c))
                dve.tensor_tensor(merged[:, c, :], merged[:, c, :], t, ALU.add).then_inc(merged_ready, 1)

            for i in range(TT):
                name, o = ("wout", i), (i % 2) * D
                filled(dve, name)
                dve.wait_ge(x_landed[i % 2], 16 * ((TT + 2 - i % 2) // 2 + i // 2 + 1))
                h = temp[:, o:o + D]
                dve.tensor_tensor(h, h, pair(name), ALU.add).then_inc(h1_ready, 1)
                dve.wait_ge(h1_ready, i + 1)
                dve.engine_nop().then_inc(free_sem(name), 1)
                normalise(TT + 1 + i, h, temp[:, 2 * D + o:3 * D + o], P)
                to_features(("hn2", i), hnT[:, :, i * P:(i + 1) * P], P, gffn)

            for n in range(HK):
                name = ("sc", n)
                filled(dve, name)
                dve.tensor_copy(score[:, :, n, :], pair(name)[:, 0:SEQ].rearrange("p (i k) -> p i k", i=TT))\
                   .then_inc(free_sem(name), 1)

            def top16(vals, idx, src, scratch):
                chain(dve.max(vals[:, 0:8], src))
                dve.max_index(idx[:, 0:8], vals[:, 0:8], src)
                chain(dve.match_replace(scratch, vals[:, 0:8], src, -3.0e38))
                chain(dve.max(vals[:, 8:16], scratch))
                return dve.max_index(idx[:, 8:16], vals[:, 8:16], scratch)

            drained(dve, ("sc", HK - 1))
            for n in range(HK):
                drained(dve, ("sc", n))
            for i in range(TT):
                for n in range(HK):
                    chain(top16(topv[:, n, :], topi[:, n, :], score[:, i, n, :], work))
                chain(dve.tensor_copy(topf, topi))
                for h in range(PH):
                    a = topv[:, 2 * h, :].unsqueeze(2).to_broadcast([P, TOPK, TOPK])
                    b = topv[:, 2 * h + 1, :].unsqueeze(1).to_broadcast([P, TOPK, TOPK])
                    chain(dve.tensor_tensor(cand[:, h, :].rearrange("p (a b) -> p a b", a=TOPK), a, b, ALU.add))
                    chain(top16(best[:, h, :], posu[:, h, :], cand[:, h, :], cwork))
                base = 2048 + (i % 2) * 384
                if i >= 2:
                    filled(dve, ("idx", i - 2))
                dve.tensor_scalar(hiu, posu, 4, None, ALU.logical_shift_right)
                chain(dve.tensor_scalar(lou, posu, 15, None, ALU.bitwise_and))
                dve.tensor_copy(hif, hiu)
                chain(dve.tensor_copy(lof, lou))
                for a, place_f in enumerate((hif, lof)):
                    where = place_f.unsqueeze(3).to_broadcast([P, PH, TOPK, TOPK])
                    which = iota[:, 0:TOPK].unsqueeze(1).unsqueeze(1).to_broadcast([P, PH, TOPK, TOPK])
                    index = topf[:, a:HK:2, :].unsqueeze(2).to_broadcast([P, PH, TOPK, TOPK])
                    for h in range(PH):
                        dve.tensor_tensor(pick[:, h], where[:, h], which[:, h], ALU.is_equal)
                    chain(dve.engine_nop())
                    for h in range(PH):
                        mul(pick[:, h], pick[:, h], index[:, h])
                    chain(dve.engine_nop())
                    chain(dve.tensor_reduce(temp[:, base + a * P:base + (a + 1) * P], pick.rearrange("p h k j -> p (h k) j"),
                                            AX.X, ALU.add))
                dve.tensor_tensor(gexp, best, best[:, :, 0:1].to_broadcast([P, PH, TOPK]), ALU.subtract)\
                   .then_inc(gates_raw, 1)
                dve.wait_ge(gates_exp, i + 1)
                chain(dve.tensor_reduce(norm, gexp, AX.X, ALU.add))
                chain(dve.reciprocal(norm, norm))
                mul(temp[:, base + 2 * P:base + 3 * P].rearrange("p (h k) -> p h k", h=PH), gexp,
                    norm.unsqueeze(2).to_broadcast([P, PH, TOPK])).then_inc(chosen_ready, 1)

            for i in range(TT):
                drained(dve, ("idx", i))

            def final(g):
                dve.wait_ge(h1_landed, 16 * (g + 1))
                dve.wait_ge(acc_ready, g // 2 + 1)
                dve.tensor_tensor(h1s, h1s, pairs[g % 2][:, :], ALU.add).then_inc(h2_ready, 1)
                dve.wait_ge(root_ready, 10 + g)
                chain(dve.reciprocal(st[:, 41 + g:42 + g], st[:, 25 + g:26 + g]))
                dve.scalar_tensor_tensor(out=h1s, in0=h1s, scalar=st[:, 41 + g:42 + g], in1=gout, op0=ALU.mult,
                                         op1=ALU.mult).then_inc(out_ready, 1)

            dve.wait_ge(gout_landed, 16)
            for hf in range(2):
                with dve.Fori(0, HALF // 8) as it:
                    for k in range(8):
                        t = it * 8 + k + hf * HALF
                        dve.wait_ge(onehot_free, t + 1)
                        e1, e2, gate = (chosen[:, a, bass.ds(t, 1)] for a in range(3))
                        dve.tensor_scalar(oh2[:, k, :], iota[:], e2, None, ALU.is_equal)
                        dve.tensor_scalar(oh1[:, k, :], iota[:], e1, gate, ALU.is_equal, ALU.mult)\
                           .then_inc(onehot_ready, 1)
                if hf:
                    final(0)
                    final(1)
                dve.wait_ge(gmat_free, 4 + (hf + 1) * HALF // 4)
                with dve.Fori(0, P // 4) as it:
                    for s in range(4):
                        n = it * 4 + s + hf * P
                        dve.wait_ge(gelu_done, n + 2)
                        dve.tensor_tensor(wgt[:, s % 2, :], act[:, s % 2, :],
                                          G[:, bass.ds(it * 4 + s, 1), :].rearrange("p a t -> p (a t)"), ALU.mult)\
                           .then_inc(w_ready, 1)
            final(2)
            final(3)


def kernel(**inputs):
    import numpy as np
    import concourse.bacc as bacc
    from concourse.bass_utils import run_bass_kernel_spmd

    a = {k: np.asarray(v) for k, v in inputs.items()}

    def chunks(w):
        k, n = w.shape
        return w.reshape(k // P, P, n // P, P).transpose(2, 1, 0, 3).reshape(n // P, P, k)

    def rows(w):
        return w.reshape(w.shape[0] // P, P, -1).transpose(1, 0, 2)

    def states(w):
        return np.moveaxis(w.reshape((NT, 2 * ST) + w.shape[2:]), 1, 0)

    w_in = a["w_in"][0]
    s1, s2, s3 = AW, 2 * AW, 3 * AW
    s4, s5 = s3 + HEADS, s3 + HEADS + SW
    data = {
        "x": a["x"][0], "meta": a["meta_tokens"],
        "g_mix": a["mix_norm_g"].reshape(DC, P).T, "g_ffn": a["ffn_norm_g"].reshape(DC, P).T,
        "g_out": a["out_norm_g"],
        "w_u": chunks(w_in[:, s4:s5]), "w_k": chunks(w_in[:, s1:s2]), "w_q": chunks(w_in[:, 0:s1]),
        "w_v": rows(w_in[:, s2:s3]), "w_f": rows(w_in[:, s3:s4]), "w_g": chunks(w_in[:, s5:]),
        "b_f": a["b_forget"].reshape(HEADS, 1), "b_g": a["b_gate"].reshape(2 * DC, P).T,
        "w_att": chunks(a["w_att_branch"][0]), "w_val": chunks(a["w_glu_val"][0]), "w_gg": chunks(a["w_glu_gate"][0]),
        "w_out": rows(a["w_out"][0]),
        "a_re": states(a["ssm_a_re"][0]), "a_im": states(a["ssm_a_im"][0]),
        "log_dt": states(np.repeat(a["ssm_log_dt"][0][:, None], ST, axis=1)),
        "b_re": states(a["ssm_b_re"][0]), "b_im": states(a["ssm_b_im"][0]),
        "c_re": states(a["ssm_c_re"][0].transpose(0, 2, 1)), "c_im": states(a["ssm_c_im"][0].transpose(0, 2, 1)),
        "d_skip": a["ssm_d"].reshape(SC, P).T,
        "w_query": chunks(a["w_query"][0]),
        "keys": a["sub_keys"][0].reshape(HK, NKEY, P).transpose(2, 0, 1),
        "expert_u": a["expert_u"].reshape(P, P, DC, P).transpose(0, 3, 2, 1).reshape(P, P, D),
        "expert_v": a["expert_v"].reshape(P, P, D),
    }
    nc = bacc.Bacc("TRN2", target_bir_lowering=False, num_devices=1)
    arrays, args = {}, []
    for name, v in data.items():
        v = np.ascontiguousarray(v)
        arrays[f"in_{name}"] = v
        args.append(nc.dram_tensor(f"in_{name}", v.shape, mybir.dt.from_np(v.dtype), kind="ExternalInput").ap())
    args.append(nc.dram_tensor("out", (SEQ, D), F32, kind="ExternalOutput").ap())
    hybrid_program(nc, *args)
    r = run_bass_kernel_spmd(nc, [arrays], core_ids=[0])
    return r.results[0]["out"].reshape(1, SEQ, D)
```

```python
from contextlib import ExitStack
import math

import concourse.bass as bass
from concourse import mybir

ALU = mybir.AluOpType
ACT = mybir.ActivationFunctionType
AX = mybir.AxisListType
F32 = mybir.dt.float32
BF16 = mybir.dt.bfloat16
U32 = mybir.dt.uint32
F32R = mybir.dt.float32r

P = 128
D = 1024
DC = D // P
META = 16
SEQ = 512
L = META + SEQ
TT = SEQ // P
HEADS = 8
DH = 64
AW = HEADS * DH
AC = AW // P
SW = 512
SC = SW // P
GROUPS = 32
GCH = 16
ST = 64
NT = GROUPS * ST // P
PH = 8
HK = 2 * PH
NKEY = 128
TOPK = 16
HALF = SEQ // 2
EPS = 1e-6
NEG = -1e30
X0 = 512 - META
TWO_PI_HI = 6.28125
TWO_PI_LO = 2.0 * math.pi - 6.28125
ROUND = 1.5 * 2.0 ** 23

G_WORDS = P * HALF
RING = 8
SLOT = 1024
O_COS, O_SIN = 0, NT * L
O_WOUT, O_SCORE = NT * L, 0
O_KT = 2 * NT * L
O_QT = O_KT + AC * L
O_MERGED = O_KT
O_VX = O_QT + AC * SEQ
O_VM = O_VX + TT * AW
O_ATT = O_VM + AW
O_WV = O_ATT + AC * SEQ
O_Z = O_WV
O_KEYS = O_Z + SC * SEQ
O_P = O_KEYS
O_PT = O_P + 2 * L
O_TOPK = O_KT
O_U = O_WV + DC * AW
O_SMALL = O_U + SC * L
TEMP = 6 * L + 2 * SEQ


def hybrid_program(nc, x, meta, g_mix, g_ffn, g_out, w_u, w_k, w_q, w_v, w_f, w_g, b_f, b_g, w_att, w_val,
                   w_gg, w_out, a_re, a_im, log_dt, b_re, b_im, c_re, c_im, d_skip, w_query, keys,
                   expert_u, expert_v, out):
    order = [("hn", i) for i in range(TT + 1)]
    order += [("B", 0), ("B", 1)]
    order += [("u", c) for c in range(SC)] + [("f", 0)] + [("k", c) for c in range(AC)]
    order += [("q", c) for c in range(AC)] + [("v", i) for i in range(TT + 1)]
    alone = len(order)
    units = [(j, hp) for j in range(TT) for hp in range(AC)]
    order += [("bu_re", 0), ("bu_im", 0)]
    for i in range(NT + 1):
        if i >= 1:
            j, hp = units[i - 1]
            order += [("PT", j, 2 * hp), ("PT", j, 2 * hp + 1), ("O", j, hp)]
        if i < NT:
            j, hp = units[i]
            order += [("S", j, 2 * hp), ("S", j, 2 * hp + 1)]
        if i >= 1:
            order += [("gate", i - 1)]
        if i + 1 < NT:
            order += [("bu_re", i + 1), ("bu_im", i + 1)]
        if i >= 1:
            order += [("y", i - 1)]
    together = len(order)
    for c in range(DC):
        order += [("att", c), ("gg", c), ("val", c)]
    for i in range(TT):
        order += [("wout", i), ("hn2", i)]
    for n in range(HK):
        order += [("qry", n), ("sc", n)]
    order += [("idx", a) for a in range(3)]
    place, held, turns = {}, [0] * 4, 0
    for n, name in enumerate(order):
        if name[0] in ("bu_re", "bu_im"):
            p = 2 if name[0] == "bu_re" else 3
        elif alone <= n < together:
            p, turns = turns % 2, turns + 1
        else:
            p = n % 4
        place[name] = (p, held[p])
        held[p] += 1

    with ExitStack() as ctx:
        sb = lambda name, shape, dt=F32: ctx.enter_context(nc.sbuf_tensor(name, shape, dt))
        sem = lambda name: ctx.enter_context(nc.semaphore(name))
        gate_all = sb("gate_all", [P, G_WORDS])
        chosen = sb("chosen", [P, 3, SEQ])
        cd = sb("cd", [P, 2, NT, 32])
        ident = sb("ident", [P, P])
        iota = sb("iota", [P, P])
        identb = sb("identb", [P, P], BF16)
        maskb = sb("maskb", [P, P], BF16)
        zerob = sb("zerob", [P, 512], BF16)
        gmix = sb("gmix", [P, DC])
        gffn = sb("gffn", [P, DC])
        bgate = sb("bgate", [P, 2 * DC])
        dsk = sb("dsk", [P, SC])
        bfg = sb("bfg", [HEADS, 1])
        wf = sb("wf", [P, DC, HEADS])
        dskip = sb("dskip", [P, SC, 32])
        st = sb("st", [P, 64])
        second = sb("second", [P, 4])
        with ExitStack() as mixer:
            hnT = mixer.enter_context(nc.sbuf_tensor("hnT", [P, DC, L], F32))
            ring = mixer.enter_context(nc.sbuf_tensor("ring", [P, RING, SLOT], F32))
            temp = mixer.enter_context(nc.sbuf_tensor("temp", [P, TEMP], F32))
        raw = sb("raw", [P, 4, SLOT])
        h1s = sb("h1s", [P, D])
        act = sb("act", [P, 2, HALF])
        wfull = sb("wfull", [P, HALF])
        hn_hi, hn_lo = sb("hn_hi", [P, DC, HALF], F32R), sb("hn_lo", [P, DC, HALF], F32R)
        u_hi, u_lo = sb("u_hi", [P, 2, SLOT], F32R), sb("u_lo", [P, SLOT], F32R)
        v_hi, v_lo = sb("v_hi", [P, SLOT], F32R), sb("v_lo", [P, SLOT], F32R)
        w_hi, w_lo = sb("w_hi", [P, 2, HALF], F32R), sb("w_lo", [P, 2, HALF], F32R)
        oh1 = raw[:, 2, :].rearrange("p (a t) -> p a t", a=8)
        oh2 = raw[:, 3, :].rearrange("p (a t) -> p a t", a=8)
        hn_raw = raw[:, 0:2, :].rearrange("p a (c t) -> p (a c) t", t=HALF)
        hn2_dram = nc.dram_tensor("hn2_dram", [2, P, DC * HALF], F32, kind="Internal").ap()
        h1_dram = nc.dram_tensor("h1_dram", [TT, P, D], F32, kind="Internal").ap()
        pairs = [ctx.enter_context(nc.psum_tensor(f"pair{p}", [P, 1024], F32)) for p in range(4)]

        def region(off, *shape):
            n = 1
            for s in shape:
                n *= s
            v = gate_all[:, off:off + n]
            if len(shape) == 1:
                return v
            if len(shape) == 2:
                return v.rearrange("p (a b) -> p a b", a=shape[0])
            if len(shape) == 3:
                return v.rearrange("p (a b c) -> p a b c", a=shape[0], b=shape[1])
            return v.rearrange("p (a b c d) -> p a b c d", a=shape[0], b=shape[1], c=shape[2])

        ecos, esin = region(O_COS, NT, L), region(O_SIN, NT, L)
        wout = region(O_WOUT, DC, D)
        score = region(O_SCORE, HK, TT, NKEY)
        kT, qT = region(O_KT, AC, L), region(O_QT, AC, SEQ)
        merged = region(O_MERGED, DC, SEQ)
        vx, vm = region(O_VX, TT, AW), region(O_VM, AW)
        attT, wv = region(O_ATT, AC, SEQ), region(O_WV, DC, AW)
        zT, keysT = region(O_Z, SC, SEQ), region(O_KEYS, HK, NKEY)
        prob = region(O_P, 2, L)
        probT = [region(O_PT, 5, P), ring[:, 5, 0:5 * P].rearrange("p (a b) -> p a b", a=5)]
        gates = ecos[:, :, 0:SEQ]
        uT = region(O_U, SC, L)
        fgate = region(O_ATT, 2, L)
        small = region(O_SMALL, 34, NT)
        G = region(0, P, HALF)
        braw = region(O_ATT, 4, NT, GCH)
        bd = region(O_ATT + 4 * NT * GCH, 2, NT, 32)
        bprod = chosen[:, 0, :].rearrange("p (a b c) -> p a b c", a=2, b=NT)
        bT = chosen[:, 1:3, :].rearrange("p a (q s) -> p a q s", q=4)
        ptmp = ring[:, RING - 1, :]
        ncum = ring[0:HEADS, RING - 2, 0:L]
        xs = [temp[:, 6 * L + a * SEQ:6 * L + (a + 1) * SEQ] for a in range(2)]
        y_real = [[temp[:, (2 + 2 * b + a) * L:(3 + 2 * b + a) * L] for a in range(2)] for b in range(2)]
        gout = cd[:].rearrange("p a b c -> p (a b c)")

        loaded = sem("params_loaded")
        x_landed = [sem(f"x_landed{i}") for i in range(2)]
        wv_landed = sem("wv_landed")
        wout_landed = sem("wout_landed")
        keys_landed = sem("keys_landed")
        ring_landed = [sem(f"ring_landed{i}") for i in range(RING)]
        psum_filled = [sem(f"psum_filled{p}") for p in range(4)]
        psum_drained = [sem(f"psum_drained{p}") for p in range(4)]
        pool_step, dve_step, act_step = sem("pool_step"), sem("dve_step"), sem("act_step")
        consts_ready = sem("consts_ready")
        squares_summed = sem("squares_summed")
        mean_ready = sem("mean_ready")
        root_ready = sem("root_ready")
        hn_ready = sem("hn_ready")
        dt_ready, mag_ready, adt_ready, angle_ready, sincos_ready = (
            sem("dt_ready"), sem("mag_ready"), sem("adt_ready"), sem("angle_ready"), sem("sincos_ready"))
        table_ready = sem("table_ready")
        bd_ready, dskip_ready = sem("bd_ready"), sem("dskip_ready")
        f_shifted, f_logged, ncum_ready = sem("f_shifted"), sem("f_logged"), sem("ncum_ready")
        state_ready = sem("state_ready")
        state_used = sem("state_used")
        y_ready, z_ready = sem("y_ready"), sem("z_ready")
        rowmax_ready, exp_ready, prob_ready = sem("rowmax_ready"), sem("exp_ready"), sem("prob_ready")
        gates_ready = sem("gates_ready")
        h1_ready, h1_stored, h1_landed = sem("h1_ready"), sem("h1_stored"), sem("h1_landed")
        chosen_ready = sem("chosen_ready")
        merged_ready = sem("merged_ready")
        y_real_ready = sem("y_real_ready")
        places_ready, pick_done = sem("places_ready"), sem("pick_done")
        gate_sig = sem("gate_sigmoid_done")
        gates_raw, gates_exp = sem("gates_raw"), sem("gates_exp")
        oh1_ready, oh2_ready, onehot_free = sem("oh1_ready"), sem("oh2_ready"), sem("onehot_free")
        oh2b_ready, second_ready = sem("oh2_by_pool_ready"), sem("second_keys_ready")
        gmat_filled, gmat_free = sem("gmat_filled"), sem("gmat_free")
        u_product, v_product = sem("u_product"), sem("v_product")
        hn2_stored, hn2_landed, hn2_hi, hn2_split = (sem("hn2_stored"), sem("hn2_landed"), sem("hn2_hi_ready"),
                                                     sem("hn2_split"))
        u_landed = [sem(f"u_landed{i}") for i in range(2)]
        v_landed = [sem(f"v_landed{i}") for i in range(2)]
        u_hi_ready, u_split, v_hi_ready, v_split = (sem("u_hi_ready"), sem("u_split"), sem("v_hi_ready"),
                                                    sem("v_split"))
        w_full, w_rounded = sem("w_full"), sem("w_rounded")
        gelu_done = sem("gelu_done")
        w_ready = sem("w_ready")
        acc_ready, acc_drained = sem("acc_ready"), sem("acc_drained")
        gout_landed = sem("gout_landed")
        out_ready, out_stored = sem("out_ready"), sem("out_stored")
        h2_ready, h2_squared = sem("h2_ready"), sem("h2_squared")

        negmax, rowsum, rinv, epsc = st[:, 48:50], st[:, 50:52], st[:, 52:54], st[:, 63:64]
        dve_consts = sem("dve_consts")
        topv, topi = region(O_TOPK, HK, TT, TOPK), region(O_TOPK + 1024, HK, TT, TOPK).bitcast(U32)
        topf = region(O_TOPK + 2048, HK, TT, TOPK)
        work, cwork = region(O_TOPK + 3072, NKEY), region(O_TOPK + 3200, TOPK * TOPK)
        cand = region(O_TOPK + 3456, TOPK * TOPK)
        best, posu = region(O_TOPK + 3712, PH, TT, TOPK), region(O_TOPK + 4224, PH, TT, TOPK).bitcast(U32)
        partu = region(O_TOPK + 4736, 2, TT, TOPK).bitcast(U32)
        partf = region(O_TOPK + 4864, 2, TT, TOPK)
        norm = region(O_TOPK + 5120, PH * TT)
        gexp = region(O_TOPK + 5152, PH, TT, TOPK)
        pick = [region(O_TOPK + 5664 + k * 1024, TT, TOPK, TOPK) for k in range(2)]
        picked = temp[:, 2048:2048 + 3 * SEQ].rearrange("p (a i h k) -> p a i h k", a=3, i=TT, h=PH)

        def vacant(eng, name):
            p, k = place[name]
            if k:
                eng.wait_ge(psum_drained[p], k)

        def filled(eng, name):
            p, k = place[name]
            eng.wait_ge(psum_filled[p], k + 1)

        def drained(eng, name):
            p, k = place[name]
            eng.wait_ge(psum_drained[p], k + 1)

        pair = lambda name: pairs[place[name][0]][:, :]
        full_sem = lambda name: psum_filled[place[name][0]]
        free_sem = lambda name: psum_drained[place[name][0]]

        wloads = [("u", c, w_u[c]) for c in range(SC)] + [("k", c, w_k[c]) for c in range(AC)]
        wloads += [("q", c, w_q[c]) for c in range(AC)] + [("gate", n, w_g[n]) for n in range(2 * DC)]
        merge_from = len(wloads)
        for c in range(DC):
            wloads += [("att", c, w_att[c]), ("gg", c, w_gg[c]), ("val", c, w_val[c])]
        query_from = len(wloads)
        wloads += [("qry", n, w_query[n]) for n in range(HK)]
        NW = 5
        wslot = {(a, b): (n % NW, 16 * (n // NW + 1)) for n, (a, b, _) in enumerate(wloads)}

        def weights(name):
            return ring[:, wslot[name][0], :].rearrange("p (k m) -> p k m", m=P)

        NLOAD = 15
        block = ctx.enter_context(nc.Block())

        @block.sync
        def _(sp):
            def load_x(n, i):
                if i == 0:
                    sp.dma_start(temp[0:META, 0:D], meta).then_inc(x_landed[n % 2], 16)
                else:
                    o = (n % 2) * D
                    sp.dma_start(temp[:, o:o + D], x[(i - 1) * P:i * P, :]).then_inc(x_landed[n % 2], 16)
            load_x(0, 0)
            load_x(1, 1)
            small_loads = [(gmix[:], g_mix), (gffn[:], g_ffn), (bgate[:], b_g), (dsk[:], d_skip), (bfg[:], b_f),
                           (wf[:], w_f), (small[:, 0, :], a_re), (small[:, 1, :], a_im), (small[:, 2, :], log_dt),
                           (braw[:, 0], b_re), (braw[:, 1], b_im), (braw[:, 2], c_re), (braw[:, 3], c_im)]
            assert len(small_loads) == 13
            for dst, src in small_loads:
                sp.dma_start(dst, src).then_inc(loaded, 16)

            def load_w(n):
                a, b, src = wloads[n]
                s = n % NW
                if n >= NW:
                    filled(sp, wloads[n - NW][:2])
                size = src.shape[1]
                sp.dma_start(ring[:, s, 0:size], src).then_inc(ring_landed[s], 16)
            for n in range(NW):
                load_w(n)
            sp.dma_start(wv, w_v).then_inc(wv_landed, 16)
            for i in range(2, TT + 1):
                sp.wait_ge(hn_ready, i - 1)
                load_x(i, i)
            for n in range(NW, merge_from + NW - 2):
                load_w(n)
            sp.wait_ge(state_ready, NT)
            sp.dma_start(wout, w_out).then_inc(wout_landed, 16)
            for n in range(merge_from + NW - 2, query_from + 4):
                load_w(n)
                if n == merge_from + NW:
                    drained(sp, ("O", TT - 1, AC - 1))
                    sp.dma_start(keysT, keys).then_inc(keys_landed, 16)
            for i in range(TT):
                if i < 2:
                    sp.wait_ge(merged_ready, DC)
                else:
                    sp.wait_ge(h1_stored, 16 * (i - 1))
                    drained(sp, ("hn2", i - 2))
                o = (i % 2) * D
                sp.dma_start(temp[:, o:o + D], x[i * P:(i + 1) * P, :]).then_inc(x_landed[i % 2], 16)
                sp.wait_ge(h1_ready, i + 1)
                sp.dma_start(h1_dram[i], temp[:, o:o + D]).then_inc(h1_stored, 16)
            for n in range(query_from + 4, len(wloads)):
                load_w(n)
            sp.dma_start(gout, g_out.partition_broadcast(P)).then_inc(gout_landed, 16)
            for i in range(TT):
                drained(sp, ("hn2", i))
            for hf in range(2):
                sp.dma_start(hn2_dram[hf].rearrange("p (c t) -> p c t", c=DC), hnT[:, :, hf * HALF:(hf + 1) * HALF])\
                  .then_inc(hn2_stored, 16)
            sp.wait_ge(hn2_stored, 32)
            filled(sp, ("idx", 2))
            sp.wait_ge(h1_stored, 16 * TT)
            for hf in range(2):
                if hf:
                    sp.wait_ge(u_split, P + 2)
                sp.dma_start(hn_raw.rearrange("p c t -> p (c t)"), hn2_dram[hf]).then_inc(hn2_landed, 16)
                sp.wait_ge(hn2_split, hf + 1)
                half = hf * P

                def load_u(s, row, n):
                    sp.wait_ge(u_split, n + 1)
                    sp.dma_start(raw[:, s, :], expert_u[row].rearrange("a p n -> p (a n)")).then_inc(u_landed[s], 16)

                def load_v(s, row, n):
                    sp.wait_ge(v_split, n + 1)
                    sp.dma_start(raw[:, 2 + s, :], expert_v[row].rearrange("a p n -> p (a n)")).then_inc(v_landed[s], 16)

                for s in range(2):
                    load_u(s, slice(s, s + 1), half + s)
                sp.wait_ge(onehot_free, 8 + (hf + 1) * HALF)
                for s in range(2):
                    load_v(s, slice(s, s + 1), half + s)
                load_u(0, slice(2, 3), half + 2)
                with sp.Fori(0, P // 2 - 2) as it:
                    for s in range(2):
                        m = it * 2 + 2 + s
                        load_u(1 - s, bass.ds(m + 1, 1), m + 1 + half)
                        load_v(s, bass.ds(m, 1), m + half)
                load_u(1, slice(P - 1, P), half + P - 1)
                for s in range(2):
                    load_v(s, slice(P - 2 + s, P - 1 + s), half + P - 2 + s)

        @block.gpsimd
        def _(pool):
            steps = [0]

            def chain(ins):
                steps[0] += 1
                ins.then_inc(pool_step, 1)
                pool.wait_ge(pool_step, steps[0])
            chain(pool.memset(ident[:], 0.0))
            chain(pool.affine_select(out=ident[:], in_=ident[:], compare_op=ALU.not_equal, fill=1.0, base=0,
                                     pattern=[[-1, P]], channel_multiplier=1))
            chain(pool.tensor_copy(identb[:], ident[:]))
            chain(pool.memset(maskb[:], 0.0))
            chain(pool.affine_select(out=maskb[:], in_=maskb[:], compare_op=ALU.is_ge, fill=NEG, base=0,
                                     pattern=[[-1, P]], channel_multiplier=1))
            chain(pool.iota(iota[:], [[1, P]], base=0, channel_multiplier=0, allow_small_or_imprecise_dtypes=True))
            chain(pool.memset(zerob[:], 0.0))
            pool.memset(cd[:], 0.0).then_inc(consts_ready, 1)
            pool.memset(ecos[:, :, 0:1], 1.0)
            chain(pool.memset(esin[:, :, 0:1], 0.0))
            pool.wait_ge(sincos_ready, 1)
            ec, es = small[:, 10, :], small[:, 11, :]
            turn = [(small[:, 28, :], small[:, 29, :]), (small[:, 30, :], small[:, 31, :])]
            t1, t2 = small[:, 32, :], small[:, 33, :]
            n, lvl = 1, 0
            while n < L:
                m = min(n, L - n)
                cn, sn = turn[lvl % 2] if lvl else (ec, es)
                cn2, sn2 = turn[(lvl + 1) % 2]
                per = max(1, min(NT, SLOT // m))
                for a in range(0, NT, per):
                    b = a + per
                    tmp = ptmp[:, 0:per * m].rearrange("p (a b) -> p a b", a=per)
                    bc = cn[:, a:b].unsqueeze(2).to_broadcast([P, per, m])
                    bs = sn[:, a:b].unsqueeze(2).to_broadcast([P, per, m])
                    src_c, src_s = ecos[:, a:b, 0:m], esin[:, a:b, 0:m]
                    dst_c, dst_s = ecos[:, a:b, n:n + m], esin[:, a:b, n:n + m]
                    chain(pool.tensor_tensor(dst_c, src_c, bc, ALU.mult))
                    chain(pool.tensor_tensor(tmp, src_s, bs, ALU.mult))
                    chain(pool.tensor_tensor(dst_c, dst_c, tmp, ALU.subtract))
                    chain(pool.tensor_tensor(dst_s, src_s, bc, ALU.mult))
                    chain(pool.tensor_tensor(tmp, src_c, bs, ALU.mult))
                    chain(pool.tensor_tensor(dst_s, dst_s, tmp, ALU.add))
                chain(pool.tensor_tensor(t1, cn, cn, ALU.mult))
                chain(pool.tensor_tensor(t2, sn, sn, ALU.mult))
                chain(pool.tensor_tensor(cn2, t1, t2, ALU.subtract))
                chain(pool.tensor_tensor(t1, cn, sn, ALU.mult))
                chain(pool.tensor_tensor(sn2, t1, t1, ALU.add))
                n *= 2
                lvl += 1
            pool.memset(t1, 0.0).then_inc(table_ready, 1)
            pa, pb = ptmp[:, 0:SEQ], ptmp[:, SEQ:2 * SEQ]
            for i in range(NT):
                cx, sx = ecos[:, i, META:L], esin[:, i, META:L]
                yr, yi = y_real[i % 2][0][:, META:L], y_real[i % 2][1][:, META:L]
                pool.wait_ge(y_real_ready, i + 1)
                if i >= 1:
                    pool.wait_ge(state_ready, i)
                pool.tensor_tensor(pa, yr, cx, ALU.mult)
                chain(pool.tensor_tensor(pb, yi, sx, ALU.mult))
                if i >= 1:
                    filled(pool, ("y", i - 1))
                chain(pool.tensor_tensor(xs[0], pa, pb, ALU.subtract))
                pool.tensor_tensor(pa, yr, sx, ALU.mult)
                chain(pool.tensor_tensor(pb, yi, cx, ALU.mult))
                pool.tensor_tensor(xs[1], pa, pb, ALU.add).then_inc(state_ready, 1)
            for k in range(HK):
                pool.wait_ge(places_ready, k + 1)
                index = topf[:, k].unsqueeze(2).to_broadcast([P, TT, TOPK, TOPK])
                for i in range(TT):
                    ins = pool.tensor_tensor(pick[k % 2][:, i], pick[k % 2][:, i], index[:, i], ALU.mult)
                ins.then_inc(pick_done, 1)
            for p in range(3):
                drained(pool, ("idx", p))

            keys_and_gates = chosen[:, 1:3, :].rearrange("p a t -> p (a t)")

            def second_keys(hf):
                with pool.Fori(0, HALF // 8) as it:
                    for k in range(4):
                        step = it * 4 + k + hf * (HALF // 2)
                        pool.wait_ge(onehot_free, it * 8 + 2 * k + 1 + hf * HALF)
                        pool.wait_ge(second_ready, step + 1)
                        pool.wait_ge(oh2b_ready, step + 4)
                        pool.tensor_copy(second[:, (k + 1) % 4:(k + 1) % 4 + 1],
                                         keys_and_gates[:, bass.ds(it * 8 + 2 * k + 2 + hf * HALF, 1)])\
                            .then_inc(second_ready, 1)
                        pool.tensor_scalar(oh2[:, 2 * k, :], iota[:], second[:, k:k + 1], None, ALU.is_equal)\
                            .then_inc(oh2b_ready, 1)

            pool.tensor_copy(second[:, 0:1], keys_and_gates[:, 0:1]).then_inc(second_ready, 1)
            pool.sem_inc(oh2b_ready, 4)
            pool.wait_ge(hn2_stored, 32)
            pool.wait_ge(h1_stored, 16 * TT)
            second_keys(0)
            pool.wait_ge(h1_stored, 16 * TT)

            pool.dma_start(h1s[:], h1_dram[0]).then_inc(h1_landed, 16)
            pool.wait_ge(v_split, P + 2)
            second_keys(1)
            for g in range(TT):
                if g:
                    pool.wait_ge(out_stored, 16 * g)
                    pool.dma_start(h1s[:], h1_dram[g]).then_inc(h1_landed, 16)
                pool.wait_ge(out_ready, g + 1)
                pool.dma_start(out[g * P:(g + 1) * P, :], h1s[:]).then_inc(out_stored, 16)
            pool.wait_ge(out_stored, 16 * TT)

        @block.tensor
        def _(pe):
            pe.wait_ge(consts_ready, 1)
            pe.wait_ge(loaded, 13 * 16)

            def transposes(name, i, src, rows):
                vacant(pe, name)
                for c in range(DC):
                    mm = pe.transpose(pair(name)[:, c * P:c * P + rows], src[0:rows, c * P:(c + 1) * P], ident[0:rows, 0:rows])
                mm.then_inc(full_sem(name), 1)

            for i in range(TT + 1):
                pe.wait_ge(hn_ready, i + 1)
                o = 2 * D + (i % 2) * D
                transposes(("hn", i), i, temp[:, o:o + D], META if i == 0 else P)
            pe.wait_ge(bd_ready, 1)
            for a in range(2):
                vacant(pe, ("B", a))
                for q in range(4):
                    mm = pe.transpose(pair(("B", a))[:, q * P:(q + 1) * P],
                                      bd[:, a, 4 * q:4 * q + 4, :].rearrange("p a b -> p (a b)"), ident[:])
                mm.then_inc(full_sem(("B", a)), 1)
            for i in range(TT + 1):
                drained(pe, ("hn", i))

            def project(name, rhs, kc, cols):
                vacant(pe, name)
                s, v = wslot[name]
                pe.wait_ge(ring_landed[s], v)
                w = weights(name)
                for (dst, lo, hi) in cols:
                    for c in range(kc):
                        mm = pe.matmul(pair(name)[:, dst:dst + hi - lo], w[:, c, :], rhs[:, c, lo:hi],
                                       start=(c == 0), stop=(c == kc - 1))
                mm.then_inc(full_sem(name), 1)

            both = [(X0, 0, META), (512, META, L)]
            for c in range(SC):
                project(("u", c), hnT, DC, both)
            vacant(pe, ("f", 0))
            for dst, lo, hi in both:
                for c in range(DC):
                    mm = pe.matmul(pair(("f", 0))[0:HEADS, dst:dst + hi - lo], wf[:, c, :], hnT[:, c, lo:hi],
                                   start=(c == 0), stop=(c == DC - 1))
            mm.then_inc(full_sem(("f", 0)), 1)
            for c in range(AC):
                project(("k", c), hnT, DC, both)
            for c in range(AC):
                project(("q", c), hnT, DC, [(0, META, L)])
            pe.wait_ge(wv_landed, 16)
            for i in range(TT + 1):
                vacant(pe, ("v", i))
                lo, n = (0, META) if i == 0 else (META + (i - 1) * P, P)
                for c in range(DC):
                    mm = pe.matmul(pair(("v", i))[0:n, 0:AW], hnT[:, c, lo:lo + n], wv[:, c, :],
                                   start=(c == 0), stop=(c == DC - 1))
                mm.then_inc(full_sem(("v", i)), 1)

            for a in range(2):
                drained(pe, ("B", a))
            for c in range(SC):
                drained(pe, ("u", c))
            pe.wait_ge(dskip_ready, 1)

            def b_times_u(i):
                q = 32 * (i % 4)
                for a, kind in enumerate(("bu_re", "bu_im")):
                    name = (kind, i)
                    vacant(pe, name)
                    for dst, lo, hi in both:
                        mm = pe.matmul(pair(name)[:, dst:dst + hi - lo], bT[q:q + 32, a, i // 4, :],
                                       uT[q:q + 32, i // 4, lo:hi], start=True, stop=True)
                    mm.then_inc(full_sem(name), 1)

            def c_times_x(i):
                name = ("y", i)
                vacant(pe, name)
                q = 32 * (i % 4)
                y = pair(name)[q:q + 32, 0:SEQ]
                pe.matmul(y, dskip[q:q + 32, i // 4, :], uT[q:q + 32, i // 4, META:L], start=True, stop=False)
                pe.wait_ge(state_ready, i + 1)
                pe.matmul(y, cd[:, 0, i, :], xs[0], start=False, stop=False)
                pe.matmul(y, cd[:, 1, i, :], xs[1], start=False, stop=True).then_inc(full_sem(name), 1)

            def logits(j, hp):
                keys_x = (j + 1) * P
                for h in (2 * hp, 2 * hp + 1):
                    name = ("S", j, h)
                    vacant(pe, name)
                    b = 64 * (h % 2)
                    q = qT[b:b + 64, hp, j * P:(j + 1) * P]
                    eh = ident[0:HEADS, h:h + 1].to_broadcast([HEADS, P])
                    S = pair(name)
                    pe.matmul(S[:, X0:512], q, kT[b:b + 64, hp, 0:META], start=True, stop=False)
                    pe.matmul(S[:, X0:512], eh, ncum[:, 0:META], start=False, stop=True)
                    pe.matmul(S[:, 512:512 + keys_x], q, kT[b:b + 64, hp, META:META + keys_x], start=True, stop=False)
                    pe.matmul(S[:, 512:512 + keys_x], eh, ncum[:, META:META + keys_x], start=False, stop=False)
                    pe.matmul(S[:, 512 + keys_x - P:512 + keys_x], identb[:], maskb[:], start=False, stop=True)\
                      .then_inc(full_sem(name), 1)

            def times_v(j, hp):
                for h in (2 * hp, 2 * hp + 1):
                    name = ("PT", j, h)
                    vacant(pe, name)
                    pe.wait_ge(prob_ready, j * HEADS + h + 1)
                    pe.transpose(pair(name)[0:META, 4 * P:5 * P], prob[:, h % 2, 0:META], ident[:])
                    for s in range(j + 1):
                        mm = pe.transpose(pair(name)[:, s * P:(s + 1) * P],
                                          prob[:, h % 2, META + s * P:META + (s + 1) * P], ident[:])
                    mm.then_inc(full_sem(name), 1)
                o = ("O", j, hp)
                vacant(pe, o)
                for h in (2 * hp, 2 * hp + 1):
                    drained(pe, ("PT", j, h))
                    b = 64 * (h % 2)
                    pT = probT[h % 2]
                    O = pair(o)[b:b + 64, 0:P]
                    pe.matmul(O, vm[0:META, h * DH:(h + 1) * DH], pT[0:META, 4, :], start=True, stop=False)
                    for s in range(j + 1):
                        mm = pe.matmul(O, vx[:, s, h * DH:(h + 1) * DH], pT[:, s, :], start=False, stop=(s == j))
                mm.then_inc(full_sem(o), 1)

            pe.wait_ge(ncum_ready, 1)
            for c in range(AC):
                drained(pe, ("k", c))
                drained(pe, ("q", c))
            for i in range(TT + 1):
                drained(pe, ("v", i))
            x_cols = [(0, META, L)]
            t_cols = [(0, 0, SEQ)]
            b_times_u(0)
            for i in range(NT + 1):
                if i >= 1:
                    times_v(*units[i - 1])
                if i < NT:
                    logits(*units[i])
                if i >= 1:
                    project(("gate", i - 1), hnT, DC, x_cols)
                if i + 1 < NT:
                    b_times_u(i + 1)
                if i >= 1:
                    c_times_x(i - 1)

            for hp in range(AC):
                drained(pe, ("O", TT - 1, hp))
            pe.wait_ge(z_ready, SC)
            for c in range(DC):
                project(("att", c), attT, AC, t_cols)
                project(("gg", c), zT, SC, t_cols)
                project(("val", c), zT, SC, t_cols)
            pe.wait_ge(wout_landed, 16)
            pe.wait_ge(merged_ready, DC)
            for i in range(TT):
                name = ("wout", i)
                vacant(pe, name)
                for hf in range(2):
                    for c in range(DC):
                        mm = pe.matmul(pair(name)[:, hf * 512:(hf + 1) * 512], merged[:, c, i * P:(i + 1) * P],
                                       wout[:, c, hf * 512:(hf + 1) * 512], start=(c == 0), stop=(c == DC - 1))
                mm.then_inc(full_sem(name), 1)
                pe.wait_ge(hn_ready, TT + 2 + i)
                o = 2 * D + (i % 2) * D
                transposes(("hn2", i), i, temp[:, o:o + D], P)

            for i in range(TT):
                drained(pe, ("hn2", i))
            pe.wait_ge(keys_landed, 16)
            for n in range(HK):
                project(("qry", n), hnT, DC, t_cols)
                name = ("sc", n)
                vacant(pe, name)
                drained(pe, ("qry", n))
                for i in range(TT):
                    mm = pe.matmul(pair(name)[:, i * P:(i + 1) * P], temp[:, (n % 2) * 512 + i * P:(n % 2) * 512 + (i + 1) * P],
                                   keysT[:, n, :], start=True, stop=True)
                mm.then_inc(full_sem(name), 1)
            pe.wait_ge(chosen_ready, 1)
            for a in range(3):
                name = ("idx", a)
                vacant(pe, name)
                for i in range(TT):
                    mm = pe.transpose(pair(name)[:, i * P:(i + 1) * P],
                                      picked[:, a, i].rearrange("p h k -> p (h k)"), ident[:])
                mm.then_inc(full_sem(name), 1)

            for p in range(4):
                pe.wait_ge(psum_drained[p], held[p])
            pe.sem_inc(onehot_free, 8)
            pe.sem_inc(u_product, 2)
            pe.sem_inc(v_product, 2)

            def open_and_close(start):
                for p in range(2):
                    for b in range(2):
                        mm = pe.matmul(pairs[p][:, b * 512:(b + 1) * 512], zerob[:, 0:P], zerob[:], start=start,
                                       stop=not start, skip_group_check=True)
                return mm

            for hf in range(2):
                half = hf * P

                def u_part(s, n):
                    pe.wait_ge(u_hi_ready, n + half + 1)
                    out_a = pairs[2 + s][:, 0:HALF]
                    for c in range(DC):
                        for k, b in enumerate((hn_hi, hn_lo)):
                            pe.matmul(out_a, u_hi[:, s, c * P:(c + 1) * P], b[:, c, :], start=(c == 0 and k == 0), stop=False)
                    pe.wait_ge(u_split, n + half + 3)
                    for c in range(DC):
                        mm = pe.matmul(out_a, u_lo[:, c * P:(c + 1) * P], hn_hi[:, c, :], start=False, stop=(c == DC - 1))
                    mm.then_inc(u_product, 1)

                def v_part(s, n):
                    pe.wait_ge(v_hi_ready, (n + half) * 2 + 2)
                    pe.wait_ge(w_ready, n + half + 2)
                    for w, v in ((w_hi, v_hi), (w_lo, v_hi), (w_hi, v_lo)):
                        if v is v_lo:
                            pe.wait_ge(v_split, n + half + 3)
                        for i in range(2):
                            for b in range(2):
                                mm = pe.matmul(pairs[i][:, b * 512:(b + 1) * 512], w[:, s, i * P:(i + 1) * P],
                                               v[:, b * 512:(b + 1) * 512], start=False, stop=False,
                                               skip_group_check=True)
                    mm.then_inc(v_product, 1)

                with pe.Fori(0, HALF // 16) as it:
                    for s in range(4):
                        g = it * 4 + s + hf * (HALF // 4)
                        pe.wait_ge(gmat_free, g + 1)
                        for t in range(4):
                            pe.wait_ge(oh1_ready, g * 4 + t + 1)
                            if t % 2 == 0:
                                pe.wait_ge(oh2b_ready, g * 2 + t // 2 + 5)
                            else:
                                pe.wait_ge(oh2_ready, g * 2 + t // 2 + 1)
                            k = (s % 2) * 4 + t
                            pe.matmul(pairs[2 + s // 2][:, (s % 2) * 512 + t * P:(s % 2) * 512 + (t + 1) * P],
                                      oh2[:, k, :], oh1[:, k, :], start=True, stop=True).then_inc(onehot_free, 1)
                pe.wait_ge(gmat_free, 4 + (hf + 1) * HALF // 4)
                if hf:
                    pe.wait_ge(acc_drained, 2)
                open_and_close(True)
                u_part(0, 0)
                with pe.Fori(0, P // 2 - 1) as it:
                    for s in range(2):
                        n = it * 2 + s
                        pe.wait_ge(gelu_done, n + half + 1)
                        u_part(1 - s, n + 1)
                        v_part(s, n)
                pe.wait_ge(gelu_done, P - 2 + half + 1)
                u_part(1, P - 1)
                v_part(0, P - 2)
                v_part(1, P - 1)
                open_and_close(False).then_inc(acc_ready, 1)

        @block.scalar
        def _(ac):
            def final(g):
                ac.wait_ge(h2_ready, g + 1)
                ac.activation(pairs[g % 2][:, :], h1s[:], ACT.Square, accum_out=st[:, 9 + g:10 + g]).then_inc(acc_drained, 1)
                ac.wait_ge(acc_drained, g + 1)
                ac.activation(st[:, 25 + g:26 + g], st[:, 9 + g:10 + g], ACT.Sqrt, bias=epsc,
                              scale=1.0 / D).then_inc(root_ready, 1)

            def rms(tile, src, rows, junk):
                ac.activation(junk, src, ACT.Square, accum_out=st[0:rows, tile:tile + 1]).then_inc(act_step, 1)
                steps[0] += 1
                ac.wait_ge(act_step, steps[0])
                ac.activation(st[0:rows, 16 + tile:17 + tile], st[0:rows, tile:tile + 1], ACT.Sqrt,
                              bias=epsc[0:rows, :], scale=1.0 / D).then_inc(root_ready, 1)
            steps = [0]
            ac.wait_ge(dve_consts, 1)
            ac.wait_ge(loaded, 13 * 16)
            ac.activation(small[:, 3, :], small[:, 2, :], ACT.Exp).then_inc(dt_ready, 1)
            ac.wait_ge(adt_ready, 1)
            ac.activation(small[:, 5, :], small[:, 4, :], ACT.Exp).then_inc(mag_ready, 1)
            ac.wait_ge(angle_ready, 1)
            ac.activation(small[:, 11, :], small[:, 8, :], ACT.Sin)
            ac.activation(small[:, 10, :], small[:, 9, :], ACT.Sin).then_inc(sincos_ready, 1)
            for i in range(TT + 1):
                rows = META if i == 0 else P
                ac.wait_ge(x_landed[i % 2], 16 * (i // 2 + 1))
                if i >= 2:
                    filled(ac, ("hn", i - 2))
                o = (i % 2) * D
                rms(i, temp[0:rows, o:o + D], rows, temp[0:rows, 2 * D + o:3 * D + o])

            def evac(name, dst, cols, scale=1.0, rows=P):
                filled(ac, name)
                ac.activation(dst, pair(name)[0:rows, cols[0]:cols[1]], ACT.Copy, scale=scale).then_inc(free_sem(name), 1)

            ac.wait_ge(bd_ready, 1)
            for a in range(2):
                evac(("B", a), bT[:, a].rearrange("p q s -> p (q s)"), (0, 512))
            for c in range(SC):
                evac(("u", c), uT[:, c, :], (X0, X0 + L))
            ac.wait_ge(f_shifted, 1)
            ac.activation(fgate[0:HEADS, 1, :], fgate[0:HEADS, 1, :], ACT.Exp).then_inc(act_step, 1)
            steps[0] += 1
            ac.wait_ge(act_step, steps[0])
            ac.activation(fgate[0:HEADS, 1, :], fgate[0:HEADS, 1, :], ACT.Ln, bias=1.0).then_inc(f_logged, 1)
            for c in range(AC):
                evac(("k", c), kT[:, c, :], (X0, X0 + L))
            for c in range(AC):
                evac(("q", c), qT[:, c, :], (0, SEQ), scale=DH ** -0.5)
            evac(("v", 0), vm[0:META, :], (0, AW), rows=META)
            for i in range(1, TT + 1):
                evac(("v", i), vx[:, i - 1, :], (0, AW))
            for i in range(NT + 1):
                if i >= 1:
                    j, hp = units[i - 1]
                    for h in (2 * hp, 2 * hp + 1):
                        name = ("PT", j, h)
                        filled(ac, name)
                        if i >= 2:
                            filled(ac, ("O",) + units[i - 2])
                        ac.activation(probT[h % 2][0:META, 4, :], pair(name)[0:META, 4 * P:5 * P], ACT.Copy)
                        ac.activation(probT[h % 2][:, 0:j + 1, :].rearrange("p a b -> p (a b)"),
                                      pair(name)[:, 0:(j + 1) * P], ACT.Copy).then_inc(free_sem(name), 1)
                    evac(("O", j, hp), attT[:, hp, j * P:(j + 1) * P], (0, P))
                if i < NT:
                    j, hp = units[i]
                    n = META + (j + 1) * P
                    for h in (2 * hp, 2 * hp + 1):
                        k = j * HEADS + h
                        ac.wait_ge(rowmax_ready, k + 1)
                        name = ("S", j, h)
                        ac.activation(prob[:, h % 2, 0:n], pair(name)[:, X0:X0 + n], ACT.Exp,
                                      bias=negmax[:, h % 2:h % 2 + 1],
                                      accum_out=rowsum[:, h % 2:h % 2 + 1]).then_inc(free_sem(name), 1)
                if i >= 1:
                    ac.wait_ge(state_ready, i)
                    evac(("gate", i - 1), gates[:, i - 1, :], (0, SEQ))
                    name, q, c = ("y", i - 1), 32 * ((i - 1) % 4), (i - 1) // 4
                    filled(ac, name)
                    ac.activation(zT[q:q + 32, c, :], pair(name)[q:q + 32, 0:SEQ], ACT.Copy).then_inc(free_sem(name), 1)
            for i in range(NT - 4, NT):
                drained(ac, ("y", i))
            for c in range(SC):
                ac.activation(zT[:, c, :], zT[:, c, :], ACT.Gelu).then_inc(z_ready, 1)
            drained(ac, ("gate", 2 * DC - 1))
            drained(ac, ("gate", 2 * DC - 2))
            for c in range(DC):
                for n in (c, DC + c):
                    ac.activation(gates[:, n, :], gates[:, n, :], ACT.Sigmoid, bias=bgate[:, n:n + 1]).then_inc(gate_sig, 1)
                if c >= 2:
                    ac.wait_ge(merged_ready, c - 1)
                name, base = ("gg", c), (c % 2) * 1024
                filled(ac, name)
                ac.activation(temp[:, base:base + 512], pair(name)[:, 0:SEQ], ACT.Sigmoid).then_inc(free_sem(name), 1)
            for i in range(TT):
                ac.wait_ge(h1_ready, i + 1)
                if i < 2:
                    ac.wait_ge(merged_ready, DC)
                else:
                    filled(ac, ("hn2", i - 2))
                o = (i % 2) * D
                rms(TT + 1 + i, temp[:, o:o + D], P, temp[:, 2 * D + o:3 * D + o])
            ac.wait_ge(h1_stored, 16 * TT)
            for i in range(TT):
                drained(ac, ("hn2", i))
            for n in range(HK):
                if n >= 2:
                    filled(ac, ("sc", n - 2))
                evac(("qry", n), temp[:, (n % 2) * 512:(n % 2 + 1) * 512], (0, SEQ))
                evac(("sc", n), score[:, n, :, :].rearrange("p i k -> p (i k)"), (0, SEQ))
            ac.wait_ge(gates_raw, 1)
            ac.activation(gexp.rearrange("p h i k -> p (h i k)"), gexp.rearrange("p h i k -> p (h i k)"),
                          ACT.Exp).then_inc(gates_exp, 1)
            for a in range(3):
                evac(("idx", a), chosen[:, a, :], (0, SEQ))
            ac.sem_inc(gmat_free, 4)
            ac.sem_inc(gelu_done, 1)
            ac.sem_inc(w_full, 2)
            for hf in range(2):
                if hf:
                    ac.wait_ge(w_ready, P + 1)
                with ac.Fori(0, HALF // 16) as it:
                    for s in range(4):
                        g = it * 4 + s + hf * (HALF // 4)
                        ac.wait_ge(onehot_free, g * 4 + 12)
                        ac.activation(G[:, :, bass.ds(it * 16 + s * 4, 4)],
                                      pairs[2 + s // 2][:, (s % 2) * 512:(s % 2 + 1) * 512].rearrange("p (t e) -> p e t", t=4),
                                      ACT.Copy).then_inc(gmat_free, 1)
                if hf:
                    for i in range(2):
                        final(i)
                ac.wait_ge(hn2_landed, 16 * (hf + 1))
                ac.activation(hn_hi[:], hn_raw, ACT.Copy).then_inc(hn2_hi, 1)
                half = hf * P

                def round_u(s, n, k):
                    ac.wait_ge(u_landed[s], k * 16 + hf * P * 8)
                    ac.wait_ge(u_product, n + half + 1)
                    ac.activation(u_hi[:, s, :], raw[:, s, :], ACT.Copy).then_inc(u_hi_ready, 1)

                def round_v(s, n, k):
                    ac.wait_ge(v_landed[s], k * 16 + hf * P * 8)
                    ac.wait_ge(v_product, n + half + 2)
                    for b in range(2):
                        ac.activation(v_hi[:, b * 512:(b + 1) * 512], raw[:, 2 + s, b * 512:(b + 1) * 512],
                                      ACT.Copy).then_inc(v_hi_ready, 1)

                def gelu(s, n):
                    ac.wait_ge(u_product, n + half + 3)
                    ac.wait_ge(w_full, n + half + 1)
                    ac.activation(act[:, s, :], pairs[2 + s][:, 0:HALF], ACT.Gelu).then_inc(gelu_done, 1)

                ac.wait_ge(hn2_split, hf + 1)
                for s in range(2):
                    round_u(s, s, 1)
                with ac.Fori(0, P // 2 - 1) as it:
                    for s in range(2):
                        m = it * 2 + s
                        gelu(s, m)
                        round_u(s, m + 2, it + 2)
                        round_v(s, m, it + 1)
                for s in range(2):
                    gelu(s, P - 2 + s)
                    round_v(s, P - 2 + s, P // 2)
            for i in range(2, 4):
                final(i)

        @block.vector
        def _(dve):
            steps = [0]

            def chain(ins):
                steps[0] += 1
                ins.then_inc(dve_step, 1)
                dve.wait_ge(dve_step, steps[0])

            def mul(out, a, b):
                return dve.tensor_tensor(out, a, b, ALU.mult)

            dve.memset(bd.rearrange("p a n c -> p (a n c)"), 0.0)
            dve.memset(epsc, EPS).then_inc(dve_consts, 1)
            dve.wait_ge(dve_consts, 1)
            dve.wait_ge(loaded, 13 * 16)
            S = lambda k: small[:, k, :]
            are, aim, dt, adt, mag, th, kk, ang, cosarg, cosv, sinv = (S(0), S(1), S(3), S(4), S(5), S(6), S(7), S(8),
                                                                      S(9), S(10), S(11))
            abr, abi, numr, den, tm, rden, cr, ci = S(12), S(13), S(14), S(15), S(16), S(17), S(18), S(19)
            dve.wait_ge(dt_ready, 1)
            mul(adt, are, dt).then_inc(adt_ready, 1)
            chain(mul(th, aim, dt))
            chain(dve.tensor_scalar(kk, th, 1.0 / (2 * math.pi), ROUND, ALU.mult, ALU.add))
            chain(dve.tensor_scalar(kk, kk, -ROUND, None, ALU.add))
            chain(dve.scalar_tensor_tensor(out=ang, in0=kk, scalar=-TWO_PI_HI, in1=th, op0=ALU.mult, op1=ALU.add))
            chain(dve.scalar_tensor_tensor(out=ang, in0=kk, scalar=-TWO_PI_LO, in1=ang, op0=ALU.mult, op1=ALU.add))
            chain(dve.tensor_scalar(ang, ang, 3.1415925, -3.1415925, ALU.min, ALU.max))
            chain(dve.scalar_tensor_tensor(out=cosarg, in0=ang, scalar=-1.0, in1=ang, op0=ALU.mult, op1=ALU.min))
            dve.tensor_scalar(cosarg, cosarg, math.pi / 2, None, ALU.add).then_inc(angle_ready, 1)
            dve.wait_ge(sincos_ready, 1)
            dve.wait_ge(mag_ready, 1)
            mul(abr, mag, cosv)
            chain(mul(abi, mag, sinv))
            chain(dve.tensor_scalar(numr, abr, -1.0, None, ALU.add))
            mul(den, are, are)
            chain(mul(tm, aim, aim))
            chain(dve.tensor_tensor(den, den, tm, ALU.add))
            chain(dve.reciprocal(rden, den))
            mul(cr, numr, are)
            chain(mul(tm, abi, aim))
            chain(dve.tensor_tensor(cr, cr, tm, ALU.add))
            chain(mul(cr, cr, rden))
            mul(ci, abi, are)
            chain(mul(tm, numr, aim))
            chain(dve.tensor_tensor(ci, ci, tm, ALU.subtract))
            chain(mul(ci, ci, rden))
            crb = cr.unsqueeze(2).to_broadcast([P, NT, GCH])
            cib = ci.unsqueeze(2).to_broadcast([P, NT, GCH])
            for a, (p, q, op) in enumerate((((crb, 0), (cib, 1), ALU.subtract), ((crb, 1), (cib, 0), ALU.add))):
                mul(bprod[:, 0], braw[:, p[1]], p[0])
                chain(mul(bprod[:, 1], braw[:, q[1]], q[0]))
                dve.tensor_tensor(bd[0:64, a, :, 0:GCH], bprod[0:64, 0], bprod[0:64, 1], op)
                ins = dve.tensor_tensor(bd[64:P, a, :, GCH:32], bprod[64:P, 0], bprod[64:P, 1], op)
                chain(ins) if a == 0 else ins.then_inc(bd_ready, 1)
            dve.wait_ge(consts_ready, 1)
            for c in range(SC):
                for b in range(4):
                    r = slice(32 * b, 32 * b + 32)
                    ins = dve.tensor_scalar(dskip[r, c, :], ident[r, 32 * b:32 * b + 32], dsk[r, c:c + 1], None, ALU.mult)
            ins.then_inc(dskip_ready, 1)
            for g in range(2):
                r = slice(64 * g, 64 * g + 64)
                dve.tensor_copy(cd[r, 0, :, GCH * g:GCH * (g + 1)], braw[r, 2])
                dve.tensor_scalar(cd[r, 1, :, GCH * g:GCH * (g + 1)], braw[r, 3], -1.0, None, ALU.mult)

            def normalise(tile, src, dst, rows):
                dve.wait_ge(root_ready, tile + 1)
                chain(dve.reciprocal(st[0:rows, 32 + tile:33 + tile], st[0:rows, 16 + tile:17 + tile]))
                dve.tensor_scalar(dst, src, st[0:rows, 32 + tile:33 + tile], None, ALU.mult).then_inc(hn_ready, 1)

            def to_features(name, dst, rows, gain):
                filled(dve, name)
                mul(dst, pair(name).rearrange("p (c t) -> p c t", c=DC)[:, :, 0:rows],
                    gain[:, :].unsqueeze(2).to_broadcast([P, DC, rows])).then_inc(free_sem(name), 1)

            for i in range(TT + 1):
                rows = META if i == 0 else P
                o = (i % 2) * D
                normalise(i, temp[0:rows, o:o + D], temp[0:rows, 2 * D + o:3 * D + o], rows)
                lo = 0 if i == 0 else META + (i - 1) * P
                to_features(("hn", i), hnT[:, :, lo:lo + rows], rows, gmix)

            fx, fe = fgate[0:HEADS, 0, :], fgate[0:HEADS, 1, :]
            name = ("f", 0)
            filled(dve, name)
            dve.tensor_scalar(fx, pair(name)[0:HEADS, X0:X0 + L], bfg[:, 0:1], None, ALU.add).then_inc(free_sem(name), 1)
            drained(dve, name)
            dve.scalar_tensor_tensor(out=fe, in0=fx, scalar=-1.0, in1=fx, op0=ALU.mult, op1=ALU.min).then_inc(f_shifted, 1)
            dve.wait_ge(f_logged, 1)
            chain(dve.scalar_tensor_tensor(out=fe, in0=fx, scalar=0.0, in1=fe, op0=ALU.min, op1=ALU.subtract))
            chain(dve.tensor_scalar(fe, fe, -1.0, None, ALU.mult))
            chain(dve.memset(fx, 0.0))
            dve.tensor_tensor_scan(ncum, fe, fx, 0.0, ALU.add, ALU.add).then_inc(ncum_ready, 1)

            dve.wait_ge(table_ready, 1)
            m1, m3 = temp[:, 0:L], temp[:, L:2 * L]

            def recur(i):
                c, s = ecos[:, i, :], esin[:, i, :]
                re, im = ("bu_re", i), ("bu_im", i)
                yr, yi = y_real[i % 2]
                if i >= 2:
                    dve.wait_ge(state_ready, i - 1)
                filled(dve, re)
                bre, bim = pair(re)[:, X0:X0 + L], pair(im)[:, X0:X0 + L]
                mul(m1, bre, c)
                mul(yi, bre, s).then_inc(free_sem(re), 1)
                filled(dve, im)
                mul(yr, bim, s)
                mul(m3, bim, c).then_inc(free_sem(im), 1)
                drained(dve, re)
                drained(dve, im)
                dve.tensor_tensor(m1, m1, yr, ALU.add)
                chain(dve.tensor_tensor(m3, m3, yi, ALU.subtract))
                decay = mag[:, i:i + 1].to_broadcast([P, L])
                dve.tensor_tensor_scan(yr, decay, m1, 0.0, ALU.mult, ALU.add)
                dve.tensor_tensor_scan(yi, decay, m3, 0.0, ALU.mult, ALU.add).then_inc(y_real_ready, 1)
                dve.wait_ge(y_real_ready, i + 1)

            for i, (j, hp) in enumerate(units):
                n = META + (j + 1) * P
                for h in (2 * hp, 2 * hp + 1):
                    name = ("S", j, h)
                    filled(dve, name)
                    dve.tensor_reduce(negmax[:, h % 2:h % 2 + 1], pair(name)[:, X0:X0 + n], AX.X, ALU.max,
                                      negate=True).then_inc(rowmax_ready, 1)
                recur(i)
                for h in (2 * hp, 2 * hp + 1):
                    drained(dve, ("S", j, h))
                    chain(dve.reciprocal(rinv[:, h % 2:h % 2 + 1], rowsum[:, h % 2:h % 2 + 1]))
                    dve.tensor_scalar(prob[:, h % 2, 0:n], prob[:, h % 2, 0:n], rinv[:, h % 2:h % 2 + 1], None,
                                      ALU.mult).then_inc(prob_ready, 1)

            for c in range(DC):
                b = (c % 2) * 1024
                gg, t = temp[:, b:b + 512], temp[:, b + 512:b + 1024]
                name = ("att", c)
                filled(dve, name)
                dve.wait_ge(gate_sig, 2 * (c + 1))
                mul(merged[:, c, :], pair(name)[:, 0:SEQ], gates[:, c, :]).then_inc(free_sem(name), 1)
                name = ("val", c)
                filled(dve, name)
                drained(dve, ("gg", c))
                mul(t, pair(name)[:, 0:SEQ], gg).then_inc(free_sem(name), 1)
                drained(dve, name)
                chain(mul(t, t, gates[:, DC + c, :]))
                drained(dve, ("att", c))
                dve.tensor_tensor(merged[:, c, :], merged[:, c, :], t, ALU.add).then_inc(merged_ready, 1)

            for i in range(TT):
                name, o = ("wout", i), (i % 2) * D
                filled(dve, name)
                dve.wait_ge(x_landed[i % 2], 16 * ((TT + 2 - i % 2) // 2 + i // 2 + 1))
                h = temp[:, o:o + D]
                dve.tensor_tensor(h, h, pair(name), ALU.add).then_inc(h1_ready, 1)
                dve.wait_ge(h1_ready, i + 1)
                dve.engine_nop().then_inc(free_sem(name), 1)
                normalise(TT + 1 + i, h, temp[:, 2 * D + o:3 * D + o], P)
                to_features(("hn2", i), hnT[:, :, i * P:(i + 1) * P], P, gffn)

            def top16(vals, idx, src, scratch):
                chain(dve.max(vals[:, 0:8], src))
                dve.max_index(idx[:, 0:8], vals[:, 0:8], src)
                chain(dve.match_replace(scratch, vals[:, 0:8], src, -3.0e38))
                chain(dve.max(vals[:, 8:16], scratch))
                return dve.max_index(idx[:, 8:16], vals[:, 8:16], scratch)

            def sum_picks(h):
                for a in range(2):
                    dve.wait_ge(pick_done, 2 * h + a + 1)
                    chain(dve.tensor_reduce(picked[:, a, :, h, :], pick[a], AX.X, ALU.add))

            which = iota[:, 0:TOPK].unsqueeze(1).to_broadcast([P, TOPK, TOPK])
            for h in range(PH):
                for n in (2 * h, 2 * h + 1):
                    drained(dve, ("sc", n))
                    for i in range(TT):
                        chain(top16(topv[:, n, i, :], topi[:, n, i, :], score[:, n, i, :], work))
                dve.tensor_copy(topf[:, 2 * h:2 * h + 2].rearrange("p n i k -> p (n i k)"),
                                topi[:, 2 * h:2 * h + 2].rearrange("p n i k -> p (n i k)"))
                for i in range(TT):
                    a = topv[:, 2 * h, i, :].unsqueeze(2).to_broadcast([P, TOPK, TOPK])
                    b = topv[:, 2 * h + 1, i, :].unsqueeze(1).to_broadcast([P, TOPK, TOPK])
                    chain(dve.tensor_tensor(cand.rearrange("p (a b) -> p a b", a=TOPK), a, b, ALU.add))
                    chain(top16(best[:, h, i, :], posu[:, h, i, :], cand, cwork))
                dve.tensor_scalar(partu[:, 0], posu[:, h], 4, None, ALU.logical_shift_right)
                chain(dve.tensor_scalar(partu[:, 1], posu[:, h], 15, None, ALU.bitwise_and))
                chain(dve.tensor_copy(partf, partu))
                if h >= 1:
                    sum_picks(h - 1)
                for a in range(2):
                    for i in range(TT):
                        ins = dve.tensor_tensor(pick[a][:, i], partf[:, a, i].unsqueeze(2).to_broadcast([P, TOPK, TOPK]),
                                                which, ALU.is_equal)
                    ins.then_inc(places_ready, 1)
            dve.tensor_tensor(gexp, best, best[:, :, :, 0:1].to_broadcast([P, PH, TT, TOPK]), ALU.subtract)\
               .then_inc(gates_raw, 1)
            sum_picks(PH - 1)
            dve.wait_ge(gates_exp, 1)
            gflat = gexp.rearrange("p h i k -> p (h i) k")
            chain(dve.tensor_reduce(norm, gflat, AX.X, ALU.add))
            chain(dve.reciprocal(norm, norm))
            chain(mul(gflat, gflat, norm.unsqueeze(2).to_broadcast([P, PH * TT, TOPK])))
            dve.tensor_copy(picked[:, 2], gexp.rearrange("p h i k -> p i h k")).then_inc(chosen_ready, 1)

            for a in range(3):
                drained(dve, ("idx", a))

            def final(g):
                dve.wait_ge(h1_landed, 16 * (g + 1))
                dve.wait_ge(acc_ready, g // 2 + 1)
                dve.tensor_tensor(h1s[:], h1s[:], pairs[g % 2][:, :], ALU.add).then_inc(h2_ready, 1)
                dve.wait_ge(root_ready, 10 + g)
                chain(dve.reciprocal(st[:, 41 + g:42 + g], st[:, 25 + g:26 + g]))
                dve.scalar_tensor_tensor(out=h1s[:], in0=h1s[:], scalar=st[:, 41 + g:42 + g], in1=gout, op0=ALU.mult,
                                         op1=ALU.mult).then_inc(out_ready, 1)

            dve.wait_ge(gout_landed, 16)
            dve.wait_ge(hn2_stored, 32)
            dve.wait_ge(h1_stored, 16 * TT)
            dve.sem_inc(u_split, 2)
            dve.sem_inc(v_split, 2)
            dve.sem_inc(w_ready, 1)
            for hf in range(2):
                if hf:
                    dve.wait_ge(v_split, P + 2)
                with dve.Fori(0, HALF // 8) as it:
                    for k in range(8):
                        t = it * 8 + k + hf * HALF
                        dve.wait_ge(onehot_free, t + 1)
                        e1, e2, gate = (chosen[:, a, bass.ds(t, 1)] for a in range(3))
                        if k % 2:
                            dve.tensor_scalar(oh2[:, k, :], iota[:], e2, None, ALU.is_equal).then_inc(oh2_ready, 1)
                        dve.tensor_scalar(oh1[:, k, :], iota[:], e1, gate, ALU.is_equal, ALU.mult)\
                           .then_inc(oh1_ready, 1)
                if hf:
                    final(0)
                    final(1)
                dve.wait_ge(hn2_hi, hf + 1)
                dve.tensor_tensor(hn_lo[:], hn_raw, hn_hi[:].bitcast(F32), ALU.subtract).then_inc(hn2_split, 1)
                dve.wait_ge(gmat_free, 4 + (hf + 1) * HALF // 4)
                half = hf * P

                def split_u(s, n):
                    dve.wait_ge(u_hi_ready, n + half + 1)
                    dve.wait_ge(u_product, n + half + 2)
                    dve.tensor_tensor(u_lo[:], raw[:, s, :], u_hi[:, s, :].bitcast(F32), ALU.subtract).then_inc(u_split, 1)

                def split_v(s, n):
                    for b in range(2):
                        c = slice(b * 512, (b + 1) * 512)
                        dve.wait_ge(v_hi_ready, (n + half) * 2 + 1 + b)
                        ins = dve.tensor_tensor(v_lo[:, c], raw[:, 2 + s, c], v_hi[:, c].bitcast(F32), ALU.subtract)
                    ins.then_inc(v_split, 1)

                def weigh(s, n, row):
                    dve.wait_ge(gelu_done, n + half + 2)
                    dve.wait_ge(w_ready, n + half + 1)
                    dve.tensor_tensor(wfull[:], act[:, s, :], G[:, row, :].rearrange("p a t -> p (a t)"), ALU.mult)\
                       .then_inc(w_full, 1)
                    dve.wait_ge(w_full, n + half + 3)
                    dve.wait_ge(v_product, n + half + 1)
                    dve.tensor_copy(w_hi[:, s, :], wfull[:]).then_inc(w_rounded, 1)
                    dve.wait_ge(w_rounded, n + half + 1)
                    dve.tensor_tensor(w_lo[:, s, :], wfull[:], w_hi[:, s, :].bitcast(F32), ALU.subtract).then_inc(w_ready, 1)

                split_u(0, 0)
                with dve.Fori(0, P // 2 - 1) as it:
                    for s in range(2):
                        m = it * 2 + s
                        split_u(1 - s, m + 1)
                        weigh(s, m, bass.ds(m, 1))
                        split_v(s, m)
                for s in range(2):
                    if s == 0:
                        split_u(1, P - 1)
                    weigh(s, P - 2 + s, slice(P - 2 + s, P - 1 + s))
                    split_v(s, P - 2 + s)
            final(2)
            final(3)


def kernel(**inputs):
    import numpy as np
    import concourse.bacc as bacc
    from concourse.bass_utils import run_bass_kernel_spmd

    a = {k: np.asarray(v) for k, v in inputs.items()}

    def chunks(w):
        k, n = w.shape
        return w.reshape(k // P, P, n // P, P).transpose(2, 1, 0, 3).reshape(n // P, P, k)

    def rows(w):
        return w.reshape(w.shape[0] // P, P, -1).transpose(1, 0, 2)

    def states(w):
        return np.moveaxis(w.reshape((NT, 2 * ST) + w.shape[2:]), 1, 0)

    w_in = a["w_in"][0]
    s1, s2, s3 = AW, 2 * AW, 3 * AW
    s4, s5 = s3 + HEADS, s3 + HEADS + SW
    data = {
        "x": a["x"][0], "meta": a["meta_tokens"],
        "g_mix": a["mix_norm_g"].reshape(DC, P).T, "g_ffn": a["ffn_norm_g"].reshape(DC, P).T,
        "g_out": a["out_norm_g"],
        "w_u": chunks(w_in[:, s4:s5]), "w_k": chunks(w_in[:, s1:s2]), "w_q": chunks(w_in[:, 0:s1]),
        "w_v": rows(w_in[:, s2:s3]), "w_f": rows(w_in[:, s3:s4]), "w_g": chunks(w_in[:, s5:]),
        "b_f": a["b_forget"].reshape(HEADS, 1), "b_g": a["b_gate"].reshape(2 * DC, P).T,
        "w_att": chunks(a["w_att_branch"][0]), "w_val": chunks(a["w_glu_val"][0]), "w_gg": chunks(a["w_glu_gate"][0]),
        "w_out": rows(a["w_out"][0]),
        "a_re": states(a["ssm_a_re"][0]), "a_im": states(a["ssm_a_im"][0]),
        "log_dt": states(np.repeat(a["ssm_log_dt"][0][:, None], ST, axis=1)),
        "b_re": states(a["ssm_b_re"][0]), "b_im": states(a["ssm_b_im"][0]),
        "c_re": states(a["ssm_c_re"][0].transpose(0, 2, 1)), "c_im": states(a["ssm_c_im"][0].transpose(0, 2, 1)),
        "d_skip": a["ssm_d"].reshape(SC, P).T,
        "w_query": chunks(a["w_query"][0]),
        "keys": a["sub_keys"][0].reshape(HK, NKEY, P).transpose(2, 0, 1),
        "expert_u": a["expert_u"].reshape(P, P, DC, P).transpose(0, 3, 2, 1).reshape(P, P, D),
        "expert_v": a["expert_v"].reshape(P, P, D),
    }
    nc = bacc.Bacc("TRN2", target_bir_lowering=False, num_devices=1)
    arrays, args = {}, []
    for name, v in data.items():
        v = np.ascontiguousarray(v)
        arrays[f"in_{name}"] = v
        args.append(nc.dram_tensor(f"in_{name}", v.shape, mybir.dt.from_np(v.dtype), kind="ExternalInput").ap())
    args.append(nc.dram_tensor("out", (SEQ, D), F32, kind="ExternalOutput").ap())
    hybrid_program(nc, *args)
    r = run_bass_kernel_spmd(nc, [arrays], core_ids=[0])
    return r.results[0]["out"].reshape(1, SEQ, D)
```

```python
from contextlib import ExitStack
import math

import concourse.bass as bass
from concourse import mybir

ALU = mybir.AluOpType
ACT = mybir.ActivationFunctionType
AX = mybir.AxisListType
F32 = mybir.dt.float32
BF16 = mybir.dt.bfloat16
U32 = mybir.dt.uint32
F32R = mybir.dt.float32r

P = 128
D = 1024
DC = D // P
META = 16
SEQ = 512
L = META + SEQ
TT = SEQ // P
HEADS = 8
DH = 64
AW = HEADS * DH
AC = AW // P
SW = 512
SC = SW // P
GROUPS = 32
GCH = 16
ST = 64
NT = GROUPS * ST // P
PH = 8
HK = 2 * PH
NKEY = 128
TOPK = 16
HALF = SEQ // 2
EPS = 1e-6
NEG = -1e30
BANK = 512
X0 = BANK - L // 2
KEYS0 = [0 if META + (j + 1) * P <= BANK else X0 for j in range(TT)]
TWO_PI_HI = 6.28125
TWO_PI_LO = 2.0 * math.pi - 6.28125
ROUND = 1.5 * 2.0 ** 23

G_WORDS = P * HALF
RING = 8
SMALL_LOADS = 12
SLOT = 1024
O_COS, O_SIN = 0, NT * L
O_WOUT, O_SCORE = NT * L, 0
O_KT = 2 * NT * L
O_QT = O_KT + AC * L
O_MERGED = O_KT
O_VX = O_QT + AC * SEQ
O_VM = O_VX + TT * AW
O_ATT = O_VM + AW
O_WV = O_ATT + AC * SEQ
O_Z = O_WV
O_KEYS = O_Z + SC * SEQ
O_P = O_KEYS
O_PT = O_P + 2 * L
O_TOPK = O_KT
CAND = TOPK + 7 * 8 + 8
O_U = O_WV + DC * AW
O_SMALL = O_U + SC * L
TEMP = 6 * L + 2 * SEQ


def hybrid_program(nc, x, meta, g_mix, g_ffn, g_out, w_u, w_k, w_q, w_v, w_f, w_g, b_f, b_g, w_att, w_val,
                   w_gg, w_out, a_re, a_im, log_dt, b_re, b_im, c_re, c_im, d_skip, w_query, keys,
                   expert_u, expert_v, out):
    order = [("hn", i) for i in range(TT + 1)]
    order += [("u", c) for c in range(SC)] + [("B", 0), ("B", 1), ("f", 0)] + [("k", c) for c in range(AC)]
    order += [("q", c) for c in range(AC)] + [("v", i) for i in range(TT + 1)]
    alone = len(order)
    units = [(j, hp) for j in range(TT) for hp in range(AC)]
    order += [("bu_re", 0), ("bu_im", 0)]
    for i in range(NT + 1):
        if i >= 1:
            j, hp = units[i - 1]
            order += [("PT", j, 2 * hp), ("PT", j, 2 * hp + 1), ("O", j, hp)]
        if i < NT:
            j, hp = units[i]
            order += [("S", j, 2 * hp), ("S", j, 2 * hp + 1)]
        if i >= 1:
            order += [("gate", i - 1)]
        if i + 1 < NT:
            order += [("bu_re", i + 1), ("bu_im", i + 1)]
        if i >= 1:
            order += [("y", i - 1)]
    together = len(order)
    for c in range(DC):
        order += [("att", c), ("gg", c), ("val", c)]
    for i in range(TT + 1):
        order += ([("wout", i)] if i < TT else []) + ([("hn2", i - 1)] if i else [])
    query_steps = [(kind, m) for n in range(HK + 1)
                   for kind, m in ((("qry", n), ("sc", n - 1)) if n != HK - 1 else (("sc", n - 1), ("qry", n)))
                   if 0 <= m < HK]
    order += query_steps
    order += [("idx", a) for a in range(3)]
    place, held, turns = {}, [0] * 4, 0
    for n, name in enumerate(order):
        if name[0] in ("bu_re", "bu_im"):
            p = 2 if name[0] == "bu_re" else 3
        elif alone <= n < together:
            p, turns = turns % 2, turns + 1
        else:
            p = n % 4
        place[name] = (p, held[p])
        held[p] += 1

    with ExitStack() as ctx:
        sb = lambda name, shape, dt=F32: ctx.enter_context(nc.sbuf_tensor(name, shape, dt))
        sem = lambda name: ctx.enter_context(nc.semaphore(name))
        gate_all = sb("gate_all", [P, G_WORDS])
        chosen = sb("chosen", [P, 3, SEQ])
        cd = sb("cd", [P, 2, NT, 32])
        iota = sb("iota", [P, P])
        zerob = sb("zerob", [P, P], BF16)
        gmix = sb("gmix", [P, DC])
        gffn = sb("gffn", [P, DC])
        bgate = sb("bgate", [P, 2 * DC])
        dsk = sb("dsk", [P, SC])
        bfg = sb("bfg", [HEADS, 1])
        wf = sb("wf", [P, DC, HEADS])
        st = sb("st", [P, 64])
        with ExitStack() as mixer:
            hnT = mixer.enter_context(nc.sbuf_tensor("hnT", [P, DC, L], F32))
            ring = mixer.enter_context(nc.sbuf_tensor("ring", [P, RING, SLOT], F32))
            temp = mixer.enter_context(nc.sbuf_tensor("temp", [P, TEMP], F32))
            ident = mixer.enter_context(nc.sbuf_tensor("ident", [P, P], F32))
            identb = mixer.enter_context(nc.sbuf_tensor("identb", [P, P], BF16))
            maskb = mixer.enter_context(nc.sbuf_tensor("maskb", [P, P], BF16))
        raw = sb("raw", [P, 4, SLOT])
        h1s = sb("h1s", [P, 2, D])
        act = sb("act", [P, 2, HALF])
        wfull = sb("wfull", [P, HALF])
        hn_hi, hn_lo = sb("hn_hi", [P, DC, HALF], F32R), sb("hn_lo", [P, DC, HALF], F32R)
        u_hi, u_lo = sb("u_hi", [P, 2, SLOT], F32R), sb("u_lo", [P, SLOT], F32R)
        v_hi, v_lo = sb("v_hi", [P, SLOT], F32R), sb("v_lo", [P, SLOT], F32R)
        marks_more = sb("marks_more", [P, HALF])
        w_hi, w_lo = sb("w_hi", [P, 2, HALF], F32R), sb("w_lo", [P, 2, HALF], F32R)
        keys_chosen = chosen[:, 0, :].bitcast(BF16).rearrange("p (a t) -> p a t", a=2)
        numbers = chosen[:, 1, 0:HALF].bitcast(BF16).rearrange("p (e t) -> p e t", t=4)
        marks = [[v.bitcast(BF16).rearrange("p (e t) -> p e t", t=4) for v in pair_of]
                 for pair_of in ((wfull[:], marks_more[:]), (act[:, 0], act[:, 1]))]
        oh1 = raw[:, 2:4, :].rearrange("p s (b t e) -> p (s b) t e", b=2, t=4)
        oh2 = [v[:, b * 512:(b + 1) * 512].rearrange("p (t e) -> p t e", t=4) for v in (v_hi, v_lo) for b in range(2)]
        hn_raw = raw[:, 0:2, :].rearrange("p a (c t) -> p (a c) t", t=HALF)
        hn2_dram = nc.dram_tensor("hn2_dram", [2, P, DC * HALF], F32, kind="Internal").ap()
        h1_dram = nc.dram_tensor("h1_dram", [TT, P, D], F32, kind="Internal").ap()
        pairs = [ctx.enter_context(nc.psum_tensor(f"pair{p}", [P, 1024], F32)) for p in range(4)]

        def region(off, *shape):
            n = 1
            for s in shape:
                n *= s
            v = gate_all[:, off:off + n]
            if len(shape) == 1:
                return v
            if len(shape) == 2:
                return v.rearrange("p (a b) -> p a b", a=shape[0])
            if len(shape) == 3:
                return v.rearrange("p (a b c) -> p a b c", a=shape[0], b=shape[1])
            return v.rearrange("p (a b c d) -> p a b c d", a=shape[0], b=shape[1], c=shape[2])

        ecos, esin = region(O_COS, NT, L), region(O_SIN, NT, L)
        wout = region(O_WOUT, DC, D)
        score = region(O_SCORE, HK, TT, NKEY)
        kT, qT = region(O_KT, AC, L), region(O_QT, AC, SEQ)
        merged = region(O_MERGED, DC, SEQ)
        vx, vm = region(O_VX, TT, AW), region(O_VM, AW)
        attT, wv = region(O_ATT, AC, SEQ), region(O_WV, DC, AW)
        zT, keysT = region(O_Z, SC, SEQ), region(O_KEYS, HK, NKEY)
        prob = region(O_P, 2, L)
        probT = [region(O_PT, 5, P), ring[:, 5, 0:5 * P].rearrange("p (a b) -> p a b", a=5)]
        gates = ecos[:, :, 0:SEQ]
        uT = region(O_U, SC, L)
        fgate = region(O_ATT, 2, L)
        small = region(O_SMALL, 34, NT)
        G = region(0, P, HALF)
        x_first = region(O_KT, TT + 1, D)
        braw = region(O_ATT, 4, NT, GCH)
        bd = region(O_ATT + 4 * NT * GCH, 2, NT, 32)
        bprod = chosen[:, 0, :].rearrange("p (a b c) -> p a b c", a=2, b=NT)
        bT = chosen[:, 1:3, :].rearrange("p a (q s) -> p a q s", q=4)
        ptmp = ring[:, RING - 1, :]
        ncum = ring[0:HEADS, RING - 2, 0:L]
        xs = [temp[:, 6 * L + a * SEQ:6 * L + (a + 1) * SEQ] for a in range(2)]
        y_real = [[temp[:, (2 + 2 * b + a) * L:(3 + 2 * b + a) * L] for a in range(2)] for b in range(2)]
        gout = cd[:].rearrange("p a b c -> p (a b c)")

        loaded = sem("params_loaded")
        gmix_landed, first_landed = sem("gmix_landed"), [sem(f"first_landed{i}") for i in range(TT + 1)]
        x_landed = [sem(f"x_landed{i}") for i in range(2)]
        wv_landed = sem("wv_landed")
        wout_landed = sem("wout_landed")
        keys_landed = sem("keys_landed")
        ring_landed = [sem(f"ring_landed{i}") for i in range(RING)]
        psum_filled = [sem(f"psum_filled{p}") for p in range(4)]
        psum_drained = [sem(f"psum_drained{p}") for p in range(4)]
        pool_step, dve_step, act_step = sem("pool_step"), sem("dve_step"), sem("act_step")
        consts_ready = sem("consts_ready")
        root_ready = sem("root_ready")
        hn_ready = sem("hn_ready")
        dt_ready, mag_ready, adt_ready, angle_ready, sincos_ready = (
            sem("dt_ready"), sem("mag_ready"), sem("adt_ready"), sem("angle_ready"), sem("sincos_ready"))
        table_ready = sem("table_ready")
        bd_ready, skip_added = sem("bd_ready"), sem("skip_added")
        f_shifted, f_logged, ncum_ready = sem("f_shifted"), sem("f_logged"), sem("ncum_ready")
        state_ready = sem("state_ready")
        z_ready = sem("z_ready")
        rowmax_ready, prob_ready = sem("rowmax_ready"), sem("prob_ready")
        h1_ready, h1_stored = sem("h1_ready"), sem("h1_stored")
        h1_landed = [sem(f"h1_landed{i}") for i in range(2)]
        chosen_ready = sem("chosen_ready")
        merged_ready = sem("merged_ready")
        y_real_ready = sem("y_real_ready")
        places_ready, pick_done = sem("places_ready"), sem("pick_done")
        gate_sig = sem("gate_sigmoid_done")
        lists_ready, topf_ready, cand_ready = sem("lists_ready"), sem("topf_ready"), sem("cand_ready")
        eighths_ready, split_ready = sem("eighths_ready"), sem("split_ready")
        gates_raw, gates_exp = sem("gates_raw"), sem("gates_exp")
        numbers_ready = sem("numbers_ready")
        oh1_marked, oh2_marked, oh1_ready, oh2_ready, onehot_free = (
            sem("oh1_marked"), sem("oh2_marked"), sem("oh1_ready"), sem("oh2_ready"), sem("onehot_free"))
        gmat_free = sem("gmat_free")
        u_product, v_product = sem("u_product"), sem("v_product")
        hn2_stored, hn2_landed, hn2_hi, hn2_split = (sem("hn2_stored"), sem("hn2_landed"), sem("hn2_hi_ready"),
                                                     sem("hn2_split"))
        u_landed = [sem(f"u_landed{i}") for i in range(2)]
        v_landed = [sem(f"v_landed{i}") for i in range(2)]
        u_hi_ready, u_split, v_hi_ready, v_split = (sem("u_hi_ready"), sem("u_split"), sem("v_hi_ready"),
                                                    sem("v_split"))
        w_full, w_rounded = sem("w_full"), sem("w_rounded")
        gelu_done = sem("gelu_done")
        w_ready = sem("w_ready")
        acc_ready, squared = sem("acc_ready"), sem("squared")
        gout_landed = sem("gout_landed")
        out_ready, out_stored = sem("out_ready"), sem("out_stored")
        h2_ready = sem("h2_ready")

        negmax, rowsum, rinv, epsc = st[:, 48:50], st[:, 50:52], st[:, 52:54], st[:, 63:64]
        dve_consts = sem("dve_consts")
        topv, topi = region(O_TOPK, HK, TT, TOPK), region(O_TOPK + 1024, HK, TT, TOPK).bitcast(U32)
        topf = region(O_TOPK + 2048, HK, TT, TOPK)
        work, cwork = region(O_WOUT, TT, NKEY), region(O_WOUT + TT * NKEY, TT, CAND)
        cand = [region(O_WOUT + TT * (NKEY + (1 + k) * CAND), TT, CAND) for k in range(2)]
        best, posu = region(O_TOPK + 3712, PH, TT, TOPK), region(O_TOPK + 4224, PH, TT, TOPK).bitcast(U32)
        partu = region(O_TOPK + 4736, 2, TT, TOPK).bitcast(U32)
        partf = region(O_TOPK + 4864, 2, TT, TOPK)
        place_ab = region(O_WOUT + TT * (NKEY + 3 * CAND), TT * TOPK).bitcast(BF16).rearrange("p (a j) -> p a j", a=2)
        is9, is1, row8, rest = (region(O_WOUT + TT * (NKEY + 3 * CAND) + (1 + k) * TT * TOPK, TT, TOPK) for k in range(4))
        norm = region(O_TOPK + 5120, PH * TT)
        gexp = region(O_TOPK + 5152, PH, TT, TOPK)
        pick = [region(O_TOPK + 5664 + k * 512, 512).bitcast(BF16).rearrange("p (w j) -> p w j", w=TOPK) for k in range(2)]
        which = region(O_TOPK + 5664 + 1024, 512).bitcast(BF16).rearrange("p (w j) -> p w j", w=TOPK)
        picked = temp[:, 2048:2048 + 3 * SEQ].rearrange("p (a i h k) -> p a i h k", a=3, i=TT, h=PH)

        def vacant(eng, name):
            p, k = place[name]
            if k:
                eng.wait_ge(psum_drained[p], k)

        def filled(eng, name):
            p, k = place[name]
            eng.wait_ge(psum_filled[p], k + 1)

        def drained(eng, name):
            p, k = place[name]
            eng.wait_ge(psum_drained[p], k + 1)

        pair = lambda name: pairs[place[name][0]][:, :]
        full_sem = lambda name: psum_filled[place[name][0]]
        free_sem = lambda name: psum_drained[place[name][0]]

        wloads = [("u", c, w_u[c]) for c in range(SC)] + [("k", c, w_k[c]) for c in range(AC)]
        wloads += [("q", c, w_q[c]) for c in range(AC)] + [("gate", n, w_g[n]) for n in range(2 * DC)]
        merge_from = len(wloads)
        for c in range(DC):
            wloads += [("att", c, w_att[c]), ("gg", c, w_gg[c]), ("val", c, w_val[c])]
        query_from = len(wloads)
        wloads += [("qry", n, w_query[n]) for n in range(HK)]
        NW = 5
        wslot = {(a, b): (n % NW, 16 * (n // NW + 1)) for n, (a, b, _) in enumerate(wloads)}

        def weights(name):
            return ring[:, wslot[name][0], :].rearrange("p (k m) -> p k m", m=P)

        NLOAD = 15
        block = ctx.enter_context(nc.Block())

        @block.sync
        def _(sp):
            sp.dma_start(gmix[:], g_mix).then_inc(gmix_landed, 16)
            sp.dma_start(x_first[0:META, 0, :], meta).then_inc(first_landed[0], 16)
            for i in range(1, TT + 1):
                sp.dma_start(x_first[:, i, :], x[(i - 1) * P:i * P, :]).then_inc(first_landed[i], 16)
            small_loads = [(gffn[:], g_ffn), (bgate[:], b_g), (dsk[:], d_skip), (bfg[:], b_f),
                           (wf[:], w_f), (small[:, 0, :], a_re), (small[:, 1, :], a_im), (small[:, 2, :], log_dt),
                           (braw[:, 0], b_re), (braw[:, 1], b_im), (braw[:, 2], c_re), (braw[:, 3], c_im)]
            assert len(small_loads) == SMALL_LOADS
            for dst, src in small_loads:
                sp.dma_start(dst, src).then_inc(loaded, 16)

            def load_w(n):
                a, b, src = wloads[n]
                s = n % NW
                if n >= NW:
                    filled(sp, wloads[n - NW][:2])
                size = src.shape[1]
                sp.dma_start(ring[:, s, 0:size], src).then_inc(ring_landed[s], 16)
            for n in range(NW):
                load_w(n)
            sp.dma_start(wv, w_v).then_inc(wv_landed, 16)
            for n in range(NW, merge_from + NW - 2):
                load_w(n)
            sp.wait_ge(state_ready, NT)
            sp.dma_start(wout, w_out).then_inc(wout_landed, 16)
            for n in range(merge_from + NW - 2, query_from + 4):
                load_w(n)
                if n == merge_from + NW:
                    drained(sp, ("O", TT - 1, AC - 1))
                    sp.dma_start(keysT, keys).then_inc(keys_landed, 16)
            for i in range(TT):
                if i < 2:
                    sp.wait_ge(merged_ready, DC)
                else:
                    sp.wait_ge(h1_stored, 16 * (i - 1))
                    drained(sp, ("hn2", i - 2))
                o = (i % 2) * D
                sp.dma_start(temp[:, o:o + D], x[i * P:(i + 1) * P, :]).then_inc(x_landed[i % 2], 16)
                sp.wait_ge(h1_ready, i + 1)
                sp.dma_start(h1_dram[i], temp[:, o:o + D]).then_inc(h1_stored, 16)
            for n in range(query_from + 4, len(wloads)):
                load_w(n)
            sp.dma_start(gout, g_out.partition_broadcast(P)).then_inc(gout_landed, 16)
            for i in range(TT):
                drained(sp, ("hn2", i))
            for hf in range(2):
                sp.dma_start(hn2_dram[hf].rearrange("p (c t) -> p c t", c=DC), hnT[:, :, hf * HALF:(hf + 1) * HALF])\
                  .then_inc(hn2_stored, 16)
            sp.wait_ge(hn2_stored, 32)
            filled(sp, ("sc", HK - 1))
            sp.wait_ge(h1_stored, 16 * TT)
            for hf in range(2):
                if hf:
                    sp.wait_ge(u_split, P + 2)
                sp.dma_start(hn_raw.rearrange("p c t -> p (c t)"), hn2_dram[hf]).then_inc(hn2_landed, 16)
                sp.wait_ge(hn2_split, hf + 1)
                half = hf * P

                def load_u(s, row, n):
                    sp.wait_ge(u_split, n + 1)
                    sp.dma_start(raw[:, s, :], expert_u[row].rearrange("a p n -> p (a n)")).then_inc(u_landed[s], 16)

                def load_v(s, row, n):
                    sp.wait_ge(v_split, n + 1)
                    sp.dma_start(raw[:, 2 + s, :], expert_v[row].rearrange("a p n -> p (a n)")).then_inc(v_landed[s], 16)

                for s in range(2):
                    load_u(s, slice(s, s + 1), half + s)
                for s in range(2):
                    sp.wait_ge(onehot_free, 4 + (hf + 1) * (HALF // 4) - 2 + 2 * s)
                    load_v(s, slice(s, s + 1), half + s)
                load_u(0, slice(2, 3), half + 2)
                with sp.Fori(0, P // 2 - 2) as it:
                    for s in range(2):
                        m = it * 2 + 2 + s
                        load_u(1 - s, bass.ds(m + 1, 1), m + 1 + half)
                        load_v(s, bass.ds(m, 1), m + half)
                load_u(1, slice(P - 1, P), half + P - 1)
                for s in range(2):
                    load_v(s, slice(P - 2 + s, P - 1 + s), half + P - 2 + s)

        @block.gpsimd
        def _(pool):
            steps = [0]

            def chain(ins):
                steps[0] += 1
                ins.then_inc(pool_step, 1)
                pool.wait_ge(pool_step, steps[0])
            chain(pool.memset(ident[:], 0.0))
            chain(pool.affine_select(out=ident[:], in_=ident[:], compare_op=ALU.not_equal, fill=1.0, base=0,
                                     pattern=[[-1, P]], channel_multiplier=1))
            chain(pool.tensor_copy(identb[:], ident[:]))
            chain(pool.memset(maskb[:], 0.0))
            chain(pool.affine_select(out=maskb[:], in_=maskb[:], compare_op=ALU.is_ge, fill=NEG, base=0,
                                     pattern=[[-1, P]], channel_multiplier=1))
            chain(pool.iota(iota[:], [[1, P]], base=0, channel_multiplier=0, allow_small_or_imprecise_dtypes=True))
            chain(pool.memset(zerob[:], 0.0))
            pool.memset(cd[:], 0.0).then_inc(consts_ready, 1)
            pool.memset(ecos[:, :, 0:1], 1.0)
            chain(pool.memset(esin[:, :, 0:1], 0.0))
            pool.wait_ge(sincos_ready, 1)
            ec, es = small[:, 10, :], small[:, 11, :]
            turn = [(small[:, 28, :], small[:, 29, :]), (small[:, 30, :], small[:, 31, :])]
            t1, t2 = small[:, 32, :], small[:, 33, :]
            n, lvl = 1, 0
            while n < L:
                m = min(n, L - n)
                cn, sn = turn[lvl % 2] if lvl else (ec, es)
                cn2, sn2 = turn[(lvl + 1) % 2]
                per = max(1, min(NT, SLOT // m))
                for a in range(0, NT, per):
                    b = a + per
                    tmp = ptmp[:, 0:per * m].rearrange("p (a b) -> p a b", a=per)
                    bc = cn[:, a:b].unsqueeze(2).to_broadcast([P, per, m])
                    bs = sn[:, a:b].unsqueeze(2).to_broadcast([P, per, m])
                    src_c, src_s = ecos[:, a:b, 0:m], esin[:, a:b, 0:m]
                    dst_c, dst_s = ecos[:, a:b, n:n + m], esin[:, a:b, n:n + m]
                    chain(pool.tensor_tensor(dst_c, src_c, bc, ALU.mult))
                    chain(pool.tensor_tensor(tmp, src_s, bs, ALU.mult))
                    chain(pool.tensor_tensor(dst_c, dst_c, tmp, ALU.subtract))
                    chain(pool.tensor_tensor(dst_s, src_s, bc, ALU.mult))
                    chain(pool.tensor_tensor(tmp, src_c, bs, ALU.mult))
                    chain(pool.tensor_tensor(dst_s, dst_s, tmp, ALU.add))
                chain(pool.tensor_tensor(t1, cn, cn, ALU.mult))
                chain(pool.tensor_tensor(t2, sn, sn, ALU.mult))
                chain(pool.tensor_tensor(cn2, t1, t2, ALU.subtract))
                chain(pool.tensor_tensor(t1, cn, sn, ALU.mult))
                chain(pool.tensor_tensor(sn2, t1, t1, ALU.add))
                n *= 2
                lvl += 1
            pool.memset(t1, 0.0).then_inc(table_ready, 1)
            pa, pb = ptmp[:, 0:SEQ], ptmp[:, SEQ:2 * SEQ]
            for i in range(NT):
                cx, sx = ecos[:, i, META:L], esin[:, i, META:L]
                yr, yi = y_real[i % 2][0][:, META:L], y_real[i % 2][1][:, META:L]
                pool.wait_ge(y_real_ready, i + 1)
                if i >= 1:
                    pool.wait_ge(state_ready, i)
                pool.tensor_tensor(pa, yr, cx, ALU.mult)
                chain(pool.tensor_tensor(pb, yi, sx, ALU.mult))
                if i >= 1:
                    filled(pool, ("y", i - 1))
                chain(pool.tensor_tensor(xs[0], pa, pb, ALU.subtract))
                pool.tensor_tensor(pa, yr, sx, ALU.mult)
                chain(pool.tensor_tensor(pb, yi, cx, ALU.mult))
                pool.tensor_tensor(xs[1], pa, pb, ALU.add).then_inc(state_ready, 1)
            for h in range(PH + 1):
                if h >= 1:
                    pool.wait_ge(eighths_ready, h)
                    e, r = partf[:, 0], partf[:, 1]
                    pool.tensor_scalar(is9, e, float(CAND // 8 - 1), None, ALU.is_equal)
                    pool.tensor_scalar(row8, e, -1.0, 0.0, ALU.add, ALU.max)
                    chain(pool.tensor_scalar(is1, e, 1.0, 8.0, ALU.is_equal, ALU.mult))
                    chain(pool.tensor_tensor(is9, is9, r, ALU.mult))
                    flat = lambda v: v.rearrange("p i k -> p (i k)")
                    pool.tensor_tensor(place_ab[:, 0], flat(row8), flat(is9), ALU.add)
                    chain(pool.tensor_tensor(rest, r, is9, ALU.subtract))
                    pool.tensor_tensor(place_ab[:, 1], flat(rest), flat(is1), ALU.add).then_inc(split_ready, 1)
                if h < PH:
                    pool.wait_ge(lists_ready, h + 1)
                    a, b, c = topv[:, 2 * h], topv[:, 2 * h + 1], cand[h % 2]
                    pool.tensor_tensor(c[:, :, 0:TOPK], a[:, :, 0:1].to_broadcast([P, TT, TOPK]), b, ALU.add)
                    pool.tensor_tensor(c[:, :, TOPK:CAND - 8].rearrange("p i (a b) -> p i a b", a=7),
                                       a[:, :, 1:8].unsqueeze(3).to_broadcast([P, TT, 7, 8]),
                                       b[:, :, 0:8].unsqueeze(2).to_broadcast([P, TT, 7, 8]), ALU.add)
                    pool.tensor_tensor(c[:, :, CAND - 8:CAND], a[:, :, 8:16], b[:, :, 0:1].to_broadcast([P, TT, 8]),
                                       ALU.add).then_inc(cand_ready, 1)
                if h >= 1:
                    for a in range(2 if h < PH - 1 else 1):
                        k = 2 * (h - 1) + a
                        pool.wait_ge(places_ready, k + 1)
                        pool.wait_ge(topf_ready, h)
                        index = topf[:, k].rearrange("p i w -> p w i").unsqueeze(3).to_broadcast([P, TOPK, TT, TOPK])
                        by_tile = pick[a].rearrange("p w (i k) -> p w i k", i=TT)
                        chain(pool.tensor_tensor(by_tile, by_tile, index, ALU.mult))
                        chain(pool.tensor_tensor(pick[a][:, 0:8], pick[a][:, 0:8], pick[a][:, 8:16], ALU.add))
                        chain(pool.tensor_tensor(pick[a][:, 0:4], pick[a][:, 0:4], pick[a][:, 4:8], ALU.add))
                        chain(pool.tensor_tensor(pick[a][:, 0:2], pick[a][:, 0:2], pick[a][:, 2:4], ALU.add))
                        pool.tensor_tensor(picked[:, a, :, h - 1, :], pick[a][:, 0].rearrange("p (i k) -> p i k", i=TT),
                                           pick[a][:, 1].rearrange("p (i k) -> p i k", i=TT), ALU.add).then_inc(pick_done, 1)
            for p in range(3):
                drained(pool, ("idx", p))

            def gate_rows(hf):
                with pool.Fori(0, HALF // 16) as it:
                    for b in range(4):
                        g = it * 4 + b + hf * (HALF // 4)
                        pool.wait_ge(oh1_marked, g + 1)
                        pool.wait_ge(onehot_free, g + 1)
                        gate = chosen[:, 2, bass.ds(it * 16 + b * 4 + hf * HALF, 4)].unsqueeze(2).to_broadcast([P, 4, P])
                        pool.tensor_tensor(oh1[:, b], marks[0][b % 2].rearrange("p e t -> p t e"), gate, ALU.mult)\
                            .then_inc(oh1_ready, 1)

            pool.sem_inc(oh1_ready, 2)
            gate_rows(0)
            pool.wait_ge(h1_stored, 16 * TT)
            for hf in range(2):
                if hf:
                    pool.wait_ge(out_stored, 2 * 16)
                for i in range(2):
                    pool.dma_start(h1s[:, i], h1_dram[hf * 2 + i]).then_inc(h1_landed[i], 16)
                if hf == 0:
                    gate_rows(1)
                for i in range(2):
                    pool.wait_ge(out_ready, hf * 2 + i + 1)
                    pool.dma_start(out[(hf * 2 + i) * P:(hf * 2 + i + 1) * P, :], h1s[:, i]).then_inc(out_stored, 16)
            pool.wait_ge(out_stored, 16 * TT)

        @block.tensor
        def _(pe):
            pe.wait_ge(consts_ready, 1)

            def transposes(name, i, src, rows):
                vacant(pe, name)
                for c in range(DC):
                    mm = pe.transpose(pair(name)[:, c * P:c * P + rows], src[0:rows, c * P:(c + 1) * P], ident[0:rows, 0:rows])
                mm.then_inc(full_sem(name), 1)

            for i in range(TT + 1):
                pe.wait_ge(hn_ready, i + 1)
                o = 2 * D + (i % 2) * D
                transposes(("hn", i), i, temp[:, o:o + D], META if i == 0 else P)
            for i in range(TT + 1):
                drained(pe, ("hn", i))

            def project(name, rhs, kc, cols):
                vacant(pe, name)
                s, v = wslot[name]
                pe.wait_ge(ring_landed[s], v)
                w = weights(name)
                for (dst, lo, hi) in cols:
                    for c in range(kc):
                        mm = pe.matmul(pair(name)[:, dst:dst + hi - lo], w[:, c, :], rhs[:, c, lo:hi],
                                       start=(c == 0), stop=(c == kc - 1))
                mm.then_inc(full_sem(name), 1)

            both = [(X0, 0, BANK - X0), (BANK, BANK - X0, L)]
            for c in range(SC):
                project(("u", c), hnT, DC, both)
            pe.wait_ge(bd_ready, 1)
            for a in range(2):
                vacant(pe, ("B", a))
                for q in range(4):
                    mm = pe.transpose(pair(("B", a))[:, q * P:(q + 1) * P],
                                      bd[:, a, 4 * q:4 * q + 4, :].rearrange("p a b -> p (a b)"), ident[:])
                mm.then_inc(full_sem(("B", a)), 1)
            pe.wait_ge(loaded, 16 * SMALL_LOADS)
            vacant(pe, ("f", 0))
            for dst, lo, hi in both:
                for c in range(DC):
                    mm = pe.matmul(pair(("f", 0))[0:HEADS, dst:dst + hi - lo], wf[:, c, :], hnT[:, c, lo:hi],
                                   start=(c == 0), stop=(c == DC - 1))
            mm.then_inc(full_sem(("f", 0)), 1)
            for c in range(AC):
                project(("k", c), hnT, DC, both)
            for c in range(AC):
                project(("q", c), hnT, DC, [(0, META, L)])
            pe.wait_ge(wv_landed, 16)
            for i in range(TT + 1):
                vacant(pe, ("v", i))
                lo, n = (0, META) if i == 0 else (META + (i - 1) * P, P)
                for c in range(DC):
                    mm = pe.matmul(pair(("v", i))[0:n, 0:AW], hnT[:, c, lo:lo + n], wv[:, c, :],
                                   start=(c == 0), stop=(c == DC - 1))
                mm.then_inc(full_sem(("v", i)), 1)

            for a in range(2):
                drained(pe, ("B", a))
            for c in range(SC):
                drained(pe, ("u", c))

            def b_times_u(i):
                q = 32 * (i % 4)
                for a, kind in enumerate(("bu_re", "bu_im")):
                    name = (kind, i)
                    vacant(pe, name)
                    for dst, lo, hi in both:
                        mm = pe.matmul(pair(name)[:, dst:dst + hi - lo], bT[q:q + 32, a, i // 4, :],
                                       uT[q:q + 32, i // 4, lo:hi], start=True, stop=True)
                    mm.then_inc(full_sem(name), 1)

            def c_times_x(i):
                name = ("y", i)
                vacant(pe, name)
                q = 32 * (i % 4)
                y = pair(name)[q:q + 32, 0:SEQ]
                pe.wait_ge(state_ready, i + 1)
                pe.matmul(y, cd[:, 0, i, :], xs[0], start=True, stop=False)
                pe.matmul(y, cd[:, 1, i, :], xs[1], start=False, stop=True).then_inc(full_sem(name), 1)

            def logits(j, hp):
                n, at = META + (j + 1) * P, KEYS0[j]
                spans = [(0, n)] if at == 0 else [(0, BANK - at), (BANK - at, n)]
                for h in (2 * hp, 2 * hp + 1):
                    name = ("S", j, h)
                    vacant(pe, name)
                    b = 64 * (h % 2)
                    q = qT[b:b + 64, hp, j * P:(j + 1) * P]
                    eh = ident[0:HEADS, h:h + 1].to_broadcast([HEADS, P])
                    S = pair(name)
                    for lo, hi in spans:
                        pe.matmul(S[:, at + lo:at + hi], q, kT[b:b + 64, hp, lo:hi], start=True, stop=False)
                        pe.matmul(S[:, at + lo:at + hi], eh, ncum[:, lo:hi], start=False, stop=(hi < n))
                    pe.matmul(S[:, at + n - P:at + n], identb[:], maskb[:], start=False, stop=True)\
                      .then_inc(full_sem(name), 1)

            def times_v(j, hp):
                for h in (2 * hp, 2 * hp + 1):
                    name = ("PT", j, h)
                    vacant(pe, name)
                    pe.wait_ge(prob_ready, j * HEADS + h + 1)
                    pe.transpose(pair(name)[0:META, 4 * P:5 * P], prob[:, h % 2, 0:META], ident[:])
                    for s in range(j + 1):
                        mm = pe.transpose(pair(name)[:, s * P:(s + 1) * P],
                                          prob[:, h % 2, META + s * P:META + (s + 1) * P], ident[:])
                    mm.then_inc(full_sem(name), 1)
                o = ("O", j, hp)
                vacant(pe, o)
                for h in (2 * hp, 2 * hp + 1):
                    drained(pe, ("PT", j, h))
                    b = 64 * (h % 2)
                    pT = probT[h % 2]
                    O = pair(o)[b:b + 64, 0:P]
                    pe.matmul(O, vm[0:META, h * DH:(h + 1) * DH], pT[0:META, 4, :], start=True, stop=False)
                    for s in range(j + 1):
                        mm = pe.matmul(O, vx[:, s, h * DH:(h + 1) * DH], pT[:, s, :], start=False, stop=(s == j))
                mm.then_inc(full_sem(o), 1)

            pe.wait_ge(ncum_ready, 1)
            for c in range(AC):
                drained(pe, ("k", c))
                drained(pe, ("q", c))
            for i in range(TT + 1):
                drained(pe, ("v", i))
            x_cols = [(0, META, L)]
            t_cols = [(0, 0, SEQ)]
            b_times_u(0)
            for i in range(NT + 1):
                if i >= 1:
                    times_v(*units[i - 1])
                if i < NT:
                    logits(*units[i])
                if i >= 1:
                    project(("gate", i - 1), hnT, DC, x_cols)
                if i + 1 < NT:
                    b_times_u(i + 1)
                if i >= 1:
                    c_times_x(i - 1)

            for hp in range(AC):
                drained(pe, ("O", TT - 1, hp))
            for c in range(DC):
                project(("att", c), attT, AC, t_cols)
                if c == 0:
                    pe.wait_ge(z_ready, SC)
                project(("gg", c), zT, SC, t_cols)
                project(("val", c), zT, SC, t_cols)
            pe.wait_ge(wout_landed, 16)
            pe.wait_ge(merged_ready, DC)
            for i in range(TT + 1):
                if i < TT:
                    name = ("wout", i)
                    vacant(pe, name)
                    for hf in range(2):
                        for c in range(DC):
                            mm = pe.matmul(pair(name)[:, hf * 512:(hf + 1) * 512], merged[:, c, i * P:(i + 1) * P],
                                           wout[:, c, hf * 512:(hf + 1) * 512], start=(c == 0), stop=(c == DC - 1))
                    mm.then_inc(full_sem(name), 1)
                if i >= 1:
                    pe.wait_ge(hn_ready, TT + 1 + i)
                    o = 2 * D + ((i - 1) % 2) * D
                    transposes(("hn2", i - 1), i - 1, temp[:, o:o + D], P)

            for i in range(TT):
                drained(pe, ("hn2", i))
            pe.wait_ge(keys_landed, 16)
            for kind, n in query_steps:
                if kind == "qry":
                    project(("qry", n), hnT, DC, t_cols)
                    continue
                name = ("sc", n)
                vacant(pe, name)
                drained(pe, ("qry", n))
                o = (n % 2) * 512
                for i in range(TT):
                    mm = pe.matmul(pair(name)[:, i * P:(i + 1) * P], temp[:, o + i * P:o + (i + 1) * P],
                                   keysT[:, n, :], start=True, stop=True)
                mm.then_inc(full_sem(name), 1)
            pe.sem_inc(onehot_free, 4)
            pe.sem_inc(u_product, 2)
            pe.sem_inc(v_product, 2)
            pe.wait_ge(chosen_ready, 1)
            for a in range(3):
                name = ("idx", a)
                vacant(pe, name)
                for i in range(TT):
                    mm = pe.transpose(pair(name)[:, i * P:(i + 1) * P],
                                      picked[:, a, i].rearrange("p h k -> p (h k)"), ident[:])
                mm.then_inc(full_sem(name), 1)

            for p in range(4):
                pe.wait_ge(psum_drained[p], held[p])

            def open_and_close(start):
                for p in range(2):
                    for b in range(8):
                        mm = pe.matmul(pairs[p][:, b * P:(b + 1) * P], zerob[:], zerob[:], start=start,
                                       stop=not start, skip_group_check=True)
                return mm

            for hf in range(2):
                half = hf * P

                def u_part(s, n):
                    pe.wait_ge(u_hi_ready, n + half + 1)
                    out_a = pairs[2 + s][:, 0:HALF]
                    for c in range(DC):
                        for k, b in enumerate((hn_hi, hn_lo)):
                            pe.matmul(out_a, u_hi[:, s, c * P:(c + 1) * P], b[:, c, :], start=(c == 0 and k == 0), stop=False)
                    pe.wait_ge(u_split, n + half + 3)
                    for c in range(DC):
                        mm = pe.matmul(out_a, u_lo[:, c * P:(c + 1) * P], hn_hi[:, c, :], start=False, stop=(c == DC - 1))
                    mm.then_inc(u_product, 1)

                def v_part(s, n):
                    pe.wait_ge(v_hi_ready, (n + half) * 2 + 2)
                    pe.wait_ge(w_ready, n + half + 2)
                    for w, v in ((w_hi, v_hi), (w_lo, v_hi), (w_hi, v_lo)):
                        if v is v_lo:
                            pe.wait_ge(v_split, n + half + 3)
                        for i in range(2):
                            for b in range(2):
                                mm = pe.matmul(pairs[i][:, b * 512:(b + 1) * 512], w[:, s, i * P:(i + 1) * P],
                                               v[:, b * 512:(b + 1) * 512], start=False, stop=False,
                                               skip_group_check=True)
                    mm.then_inc(v_product, 1)

                with pe.Fori(0, HALF // 16) as it:
                    for s in range(4):
                        g = it * 4 + s + hf * (HALF // 4)
                        pe.wait_ge(gmat_free, g + 1)
                        pe.wait_ge(oh2_ready, g + 3)
                        pe.wait_ge(oh1_ready, g + 3)
                        for t in range(4):
                            mm = pe.matmul(pairs[2 + s // 2][:, (s % 2) * 512 + t * P:(s % 2) * 512 + (t + 1) * P],
                                           oh2[s][:, t].bitcast(F32), oh1[:, s, t], start=True, stop=True)
                        mm.then_inc(onehot_free, 1)
                pe.wait_ge(gmat_free, 4 + (hf + 1) * HALF // 4)
                u_part(0, 0)
                if hf:
                    pe.wait_ge(h2_ready, 2)
                open_and_close(True)
                with pe.Fori(0, P // 2 - 1) as it:
                    for s in range(2):
                        n = it * 2 + s
                        pe.wait_ge(gelu_done, n + half + 1)
                        u_part(1 - s, n + 1)
                        v_part(s, n)
                pe.wait_ge(gelu_done, P - 2 + half + 1)
                u_part(1, P - 1)
                v_part(0, P - 2)
                v_part(1, P - 1)
                open_and_close(False).then_inc(acc_ready, 1)

        @block.scalar
        def _(ac):
            def final(g):
                ac.wait_ge(h2_ready, g + 1)
                ac.activation(act[:].rearrange("p s t -> p (s t)").bitcast(BF16), h1s[:, g % 2], ACT.Square,
                              accum_out=st[:, 9 + g:10 + g]).then_inc(squared, 1)
                ac.wait_ge(squared, g + 1)
                ac.activation(st[:, 25 + g:26 + g], st[:, 9 + g:10 + g], ACT.Sqrt, bias=epsc,
                              scale=1.0 / D).then_inc(root_ready, 1)

            def rms(tile, src, rows, junk):
                ac.activation(junk, src, ACT.Square, accum_out=st[0:rows, tile:tile + 1]).then_inc(act_step, 1)
                steps[0] += 1
                ac.wait_ge(act_step, steps[0])
                ac.activation(st[0:rows, 16 + tile:17 + tile], st[0:rows, tile:tile + 1], ACT.Sqrt,
                              bias=epsc[0:rows, :], scale=1.0 / D).then_inc(root_ready, 1)
            steps = [0]
            ac.wait_ge(dve_consts, 1)
            for i in range(TT + 1):
                rows = META if i == 0 else P
                ac.wait_ge(first_landed[i], 16)
                rms(i, x_first[0:rows, i, :], rows, temp[0:rows, 0:D])
            ac.wait_ge(loaded, 16 * SMALL_LOADS)
            ac.activation(small[:, 3, :], small[:, 2, :], ACT.Exp).then_inc(dt_ready, 1)
            ac.wait_ge(adt_ready, 1)
            ac.activation(small[:, 5, :], small[:, 4, :], ACT.Exp).then_inc(mag_ready, 1)
            ac.wait_ge(angle_ready, 1)
            ac.activation(small[:, 11, :], small[:, 8, :], ACT.Sin)
            ac.activation(small[:, 10, :], small[:, 9, :], ACT.Sin).then_inc(sincos_ready, 1)

            def evac(name, dst, cols, scale=1.0, rows=P):
                filled(ac, name)
                ac.activation(dst, pair(name)[0:rows, cols[0]:cols[1]], ACT.Copy, scale=scale).then_inc(free_sem(name), 1)

            for c in range(SC):
                evac(("u", c), uT[:, c, :], (X0, X0 + L))
            ac.wait_ge(bd_ready, 1)
            for a in range(2):
                evac(("B", a), bT[:, a].rearrange("p q s -> p (q s)"), (0, 512))
            ac.wait_ge(f_shifted, 1)
            ac.activation(fgate[0:HEADS, 1, :], fgate[0:HEADS, 1, :], ACT.Exp).then_inc(act_step, 1)
            steps[0] += 1
            ac.wait_ge(act_step, steps[0])
            ac.activation(fgate[0:HEADS, 1, :], fgate[0:HEADS, 1, :], ACT.Ln, bias=1.0).then_inc(f_logged, 1)
            for c in range(AC):
                evac(("k", c), kT[:, c, :], (X0, X0 + L))
            for c in range(AC):
                evac(("q", c), qT[:, c, :], (0, SEQ), scale=DH ** -0.5)
            evac(("v", 0), vm[0:META, :], (0, AW), rows=META)
            for i in range(1, TT + 1):
                evac(("v", i), vx[:, i - 1, :], (0, AW))
            for i in range(NT + 1):
                if i >= 1:
                    j, hp = units[i - 1]
                    for h in (2 * hp, 2 * hp + 1):
                        name = ("PT", j, h)
                        filled(ac, name)
                        if i >= 2:
                            filled(ac, ("O",) + units[i - 2])
                        ac.activation(probT[h % 2][0:META, 4, :], pair(name)[0:META, 4 * P:5 * P], ACT.Copy)
                        ac.activation(probT[h % 2][:, 0:j + 1, :].rearrange("p a b -> p (a b)"),
                                      pair(name)[:, 0:(j + 1) * P], ACT.Copy).then_inc(free_sem(name), 1)
                    evac(("O", j, hp), attT[:, hp, j * P:(j + 1) * P], (0, P))
                if i < NT:
                    j, hp = units[i]
                    n = META + (j + 1) * P
                    for h in (2 * hp, 2 * hp + 1):
                        k = j * HEADS + h
                        ac.wait_ge(rowmax_ready, k + 1)
                        name = ("S", j, h)
                        ac.activation(prob[:, h % 2, 0:n], pair(name)[:, KEYS0[j]:KEYS0[j] + n], ACT.Exp,
                                      bias=negmax[:, h % 2:h % 2 + 1],
                                      accum_out=rowsum[:, h % 2:h % 2 + 1]).then_inc(free_sem(name), 1)
                if i >= 1:
                    ac.wait_ge(state_ready, i)
                    evac(("gate", i - 1), gates[:, i - 1, :], (0, SEQ))
                    name, q, c = ("y", i - 1), 32 * ((i - 1) % 4), (i - 1) // 4
                    filled(ac, name)
                    ac.activation(zT[q:q + 32, c, :], pair(name)[q:q + 32, 0:SEQ], ACT.Copy).then_inc(free_sem(name), 1)
            for c in range(SC):
                ac.wait_ge(skip_added, c + 1)
                ac.activation(zT[:, c, :], zT[:, c, :], ACT.Gelu).then_inc(z_ready, 1)
            drained(ac, ("gate", 2 * DC - 1))
            drained(ac, ("gate", 2 * DC - 2))
            for c in range(DC):
                for n in (c, DC + c):
                    ac.activation(gates[:, n, :], gates[:, n, :], ACT.Sigmoid, bias=bgate[:, n:n + 1]).then_inc(gate_sig, 1)
                if c >= 2:
                    ac.wait_ge(merged_ready, c - 1)
                name, base = ("gg", c), (c % 2) * 1024
                filled(ac, name)
                ac.activation(temp[:, base:base + 512], pair(name)[:, 0:SEQ], ACT.Sigmoid).then_inc(free_sem(name), 1)
            for i in range(TT):
                ac.wait_ge(h1_ready, i + 1)
                if i < 2:
                    ac.wait_ge(merged_ready, DC)
                else:
                    filled(ac, ("hn2", i - 2))
                o = (i % 2) * D
                rms(TT + 1 + i, temp[:, o:o + D], P, temp[:, 2 * D + o:3 * D + o])
            ac.wait_ge(h1_stored, 16 * TT)
            for i in range(TT):
                drained(ac, ("hn2", i))

            def places_to_float(h):
                ac.wait_ge(lists_ready, h + 1)
                ac.activation(topf[:, 2 * h:2 * h + 2].rearrange("p n i k -> p (n i k)"),
                              topi[:, 2 * h:2 * h + 2].rearrange("p n i k -> p (n i k)"), ACT.Copy).then_inc(topf_ready, 1)

            for kind, n in query_steps:
                if kind == "qry":
                    if n >= 2:
                        filled(ac, ("sc", n - 2))
                    evac(("qry", n), temp[:, (n % 2) * 512:(n % 2 + 1) * 512], (0, SEQ))
                else:
                    evac(("sc", n), score[:, n, :, :].rearrange("p i k -> p (i k)"), (0, SEQ))
                    if n >= 3 and n % 2:
                        places_to_float((n - 3) // 2)
            ac.sem_inc(gmat_free, 4)
            ac.sem_inc(oh2_ready, 2)
            ac.sem_inc(gelu_done, 1)
            ac.sem_inc(w_full, 2)
            for hf in range(2):
                if hf:
                    ac.wait_ge(u_product, P + 2)
                ac.wait_ge(hn2_landed, 16 * (hf + 1))
                ac.activation(hn_hi[:], hn_raw, ACT.Copy).then_inc(hn2_hi, 1)
                half = hf * P

                def round_u(s, n, k):
                    ac.wait_ge(u_landed[s], k * 16 + hf * P * 8)
                    ac.wait_ge(u_product, n + half + 1)
                    ac.activation(u_hi[:, s, :], raw[:, s, :], ACT.Copy).then_inc(u_hi_ready, 1)

                def round_v(s, n, k):
                    ac.wait_ge(v_landed[s], k * 16 + hf * P * 8)
                    ac.wait_ge(v_product, n + half + 2)
                    for b in range(2):
                        ac.activation(v_hi[:, b * 512:(b + 1) * 512], raw[:, 2 + s, b * 512:(b + 1) * 512],
                                      ACT.Copy).then_inc(v_hi_ready, 1)

                def gelu(s, n):
                    ac.wait_ge(u_product, n + half + 3)
                    ac.wait_ge(w_full, n + half + 1)
                    ac.activation(act[:, s, :], pairs[2 + s][:, 0:HALF], ACT.Gelu).then_inc(gelu_done, 1)

                if hf == 0:
                    places_to_float(PH - 1)
                    ac.wait_ge(gates_raw, 1)
                    ac.activation(gexp.rearrange("p h i k -> p (h i k)"), gexp.rearrange("p h i k -> p (h i k)"),
                                  ACT.Exp).then_inc(gates_exp, 1)
                    ac.activation(numbers, iota[:].unsqueeze(2).to_broadcast([P, P, 4]), ACT.Copy).then_inc(numbers_ready, 1)
                    for a in range(2):
                        evac(("idx", a), keys_chosen[:, a, :], (0, SEQ))
                    evac(("idx", 2), chosen[:, 2, :], (0, SEQ))
                else:
                    ac.wait_ge(w_ready, P + 1)

                def widen(g, b):
                    ac.wait_ge(oh2_marked, g + 1 + hf * (HALF // 4))
                    ac.wait_ge(onehot_free, g + 1 + hf * (HALF // 4))
                    ac.activation(oh2[b], marks[1][b % 2].rearrange("p e t -> p t e"), ACT.Copy).then_inc(oh2_ready, 1)

                def read_gates(g, b, place):
                    ac.wait_ge(onehot_free, g + 5 + hf * (HALF // 4))
                    ac.activation(G[:, :, place],
                                  pairs[2 + b // 2][:, (b % 2) * 512:(b % 2 + 1) * 512].rearrange("p (t e) -> p e t", t=4),
                                  ACT.Copy).then_inc(gmat_free, 1)

                widen(0, 0)
                widen(1, 1)
                for s in range(2):
                    round_u(s, s, 1)
                with ac.Fori(0, HALF // 16 - 1) as it:
                    for b in range(4):
                        widen(it * 4 + b + 2, (b + 2) % 4)
                        read_gates(it * 4 + b, b, bass.ds(it * 16 + b * 4, 4))
                for b in range(4):
                    g = HALF // 4 - 4 + b
                    if b < 2:
                        widen(g + 2, b + 2)
                    read_gates(g, b, slice(4 * g, 4 * g + 4))
                if hf:
                    final(0)
                    final(1)
                with ac.Fori(0, P // 2 - 1) as it:
                    for s in range(2):
                        m = it * 2 + s
                        gelu(s, m)
                        round_u(s, m + 2, it + 2)
                        round_v(s, m, it + 1)
                for s in range(2):
                    gelu(s, P - 2 + s)
                    round_v(s, P - 2 + s, P // 2)
            for i in range(2, 4):
                final(i)

        @block.vector
        def _(dve):
            steps = [0]

            def chain(ins):
                steps[0] += 1
                ins.then_inc(dve_step, 1)
                dve.wait_ge(dve_step, steps[0])

            def mul(out, a, b):
                return dve.tensor_tensor(out, a, b, ALU.mult)

            dve.memset(bd.rearrange("p a n c -> p (a n c)"), 0.0)
            dve.memset(epsc, EPS).then_inc(dve_consts, 1)
            dve.wait_ge(dve_consts, 1)
            def normalise(tile, src, dst, rows):
                dve.wait_ge(root_ready, tile + 1)
                chain(dve.reciprocal(st[0:rows, 32 + tile:33 + tile], st[0:rows, 16 + tile:17 + tile]))
                dve.tensor_scalar(dst, src, st[0:rows, 32 + tile:33 + tile], None, ALU.mult).then_inc(hn_ready, 1)

            def to_features(name, dst, rows, gain):
                filled(dve, name)
                mul(dst, pair(name).rearrange("p (c t) -> p c t", c=DC)[:, :, 0:rows],
                    gain[:, :].unsqueeze(2).to_broadcast([P, DC, rows])).then_inc(free_sem(name), 1)

            dve.wait_ge(gmix_landed, 16)
            for i in range(TT + 2):
                if i <= TT:
                    rows = META if i == 0 else P
                    o = 2 * D + (i % 2) * D
                    normalise(i, x_first[0:rows, i, :], temp[0:rows, o:o + D], rows)
                if i >= 1:
                    rows = META if i == 1 else P
                    lo = 0 if i == 1 else META + (i - 2) * P
                    to_features(("hn", i - 1), hnT[:, :, lo:lo + rows], rows, gmix)
            dve.wait_ge(loaded, 16 * SMALL_LOADS)
            S = lambda k: small[:, k, :]
            are, aim, dt, adt, mag, th, kk, ang, cosarg, cosv, sinv = (S(0), S(1), S(3), S(4), S(5), S(6), S(7), S(8),
                                                                      S(9), S(10), S(11))
            abr, abi, numr, den, tm, rden, cr, ci = S(12), S(13), S(14), S(15), S(16), S(17), S(18), S(19)
            dve.wait_ge(dt_ready, 1)
            mul(adt, are, dt).then_inc(adt_ready, 1)
            chain(mul(th, aim, dt))
            chain(dve.tensor_scalar(kk, th, 1.0 / (2 * math.pi), ROUND, ALU.mult, ALU.add))
            chain(dve.tensor_scalar(kk, kk, -ROUND, None, ALU.add))
            chain(dve.scalar_tensor_tensor(out=ang, in0=kk, scalar=-TWO_PI_HI, in1=th, op0=ALU.mult, op1=ALU.add))
            chain(dve.scalar_tensor_tensor(out=ang, in0=kk, scalar=-TWO_PI_LO, in1=ang, op0=ALU.mult, op1=ALU.add))
            chain(dve.tensor_scalar(ang, ang, 3.1415925, -3.1415925, ALU.min, ALU.max))
            chain(dve.scalar_tensor_tensor(out=cosarg, in0=ang, scalar=-1.0, in1=ang, op0=ALU.mult, op1=ALU.min))
            dve.tensor_scalar(cosarg, cosarg, math.pi / 2, None, ALU.add).then_inc(angle_ready, 1)
            dve.wait_ge(sincos_ready, 1)
            dve.wait_ge(mag_ready, 1)
            mul(abr, mag, cosv)
            chain(mul(abi, mag, sinv))
            chain(dve.tensor_scalar(numr, abr, -1.0, None, ALU.add))
            mul(den, are, are)
            chain(mul(tm, aim, aim))
            chain(dve.tensor_tensor(den, den, tm, ALU.add))
            chain(dve.reciprocal(rden, den))
            mul(cr, numr, are)
            chain(mul(tm, abi, aim))
            chain(dve.tensor_tensor(cr, cr, tm, ALU.add))
            chain(mul(cr, cr, rden))
            mul(ci, abi, are)
            chain(mul(tm, numr, aim))
            chain(dve.tensor_tensor(ci, ci, tm, ALU.subtract))
            chain(mul(ci, ci, rden))
            crb = cr.unsqueeze(2).to_broadcast([P, NT, GCH])
            cib = ci.unsqueeze(2).to_broadcast([P, NT, GCH])
            for a, (p, q, op) in enumerate((((crb, 0), (cib, 1), ALU.subtract), ((crb, 1), (cib, 0), ALU.add))):
                mul(bprod[:, 0], braw[:, p[1]], p[0])
                chain(mul(bprod[:, 1], braw[:, q[1]], q[0]))
                dve.tensor_tensor(bd[0:64, a, :, 0:GCH], bprod[0:64, 0], bprod[0:64, 1], op)
                ins = dve.tensor_tensor(bd[64:P, a, :, GCH:32], bprod[64:P, 0], bprod[64:P, 1], op)
                chain(ins) if a == 0 else ins.then_inc(bd_ready, 1)
            dve.wait_ge(consts_ready, 1)
            for g in range(2):
                r = slice(64 * g, 64 * g + 64)
                dve.tensor_copy(cd[r, 0, :, GCH * g:GCH * (g + 1)], braw[r, 2])
                ins = dve.tensor_scalar(cd[r, 1, :, GCH * g:GCH * (g + 1)], braw[r, 3], -1.0, None, ALU.mult)
            chain(ins)

            fx, fe = fgate[0:HEADS, 0, :], fgate[0:HEADS, 1, :]
            name = ("f", 0)
            filled(dve, name)
            dve.tensor_scalar(fx, pair(name)[0:HEADS, X0:X0 + L], bfg[:, 0:1], None, ALU.add).then_inc(free_sem(name), 1)
            drained(dve, name)
            dve.scalar_tensor_tensor(out=fe, in0=fx, scalar=-1.0, in1=fx, op0=ALU.mult, op1=ALU.min).then_inc(f_shifted, 1)
            dve.wait_ge(f_logged, 1)
            chain(dve.scalar_tensor_tensor(out=fe, in0=fx, scalar=0.0, in1=fe, op0=ALU.min, op1=ALU.subtract))
            chain(dve.tensor_scalar(fe, fe, -1.0, None, ALU.mult))
            chain(dve.memset(fx, 0.0))
            dve.tensor_tensor_scan(ncum, fe, fx, 0.0, ALU.add, ALU.add).then_inc(ncum_ready, 1)

            dve.wait_ge(table_ready, 1)
            m1, m3 = temp[:, 0:L], temp[:, L:2 * L]

            def recur(i):
                c, s = ecos[:, i, :], esin[:, i, :]
                re, im = ("bu_re", i), ("bu_im", i)
                yr, yi = y_real[i % 2]
                if i >= 2:
                    dve.wait_ge(state_ready, i - 1)
                filled(dve, re)
                bre, bim = pair(re)[:, X0:X0 + L], pair(im)[:, X0:X0 + L]
                mul(m1, bre, c)
                mul(yi, bre, s).then_inc(free_sem(re), 1)
                filled(dve, im)
                mul(yr, bim, s)
                mul(m3, bim, c).then_inc(free_sem(im), 1)
                drained(dve, re)
                drained(dve, im)
                dve.tensor_tensor(m1, m1, yr, ALU.add)
                chain(dve.tensor_tensor(m3, m3, yi, ALU.subtract))
                decay = mag[:, i:i + 1].to_broadcast([P, L])
                dve.tensor_tensor_scan(yr, decay, m1, 0.0, ALU.mult, ALU.add)
                dve.tensor_tensor_scan(yi, decay, m3, 0.0, ALU.mult, ALU.add).then_inc(y_real_ready, 1)
                dve.wait_ge(y_real_ready, i + 1)

            def add_skip(c):
                for i in range(4 * c, 4 * c + 4):
                    drained(dve, ("y", i))
                dve.scalar_tensor_tensor(out=zT[:, c, :], in0=uT[:, c, META:L], scalar=dsk[:, c:c + 1], in1=zT[:, c, :],
                                         op0=ALU.mult, op1=ALU.add).then_inc(skip_added, 1)

            for i, (j, hp) in enumerate(units):
                n = META + (j + 1) * P
                for h in (2 * hp, 2 * hp + 1):
                    name = ("S", j, h)
                    filled(dve, name)
                    dve.tensor_reduce(negmax[:, h % 2:h % 2 + 1], pair(name)[:, KEYS0[j]:KEYS0[j] + n], AX.X, ALU.max,
                                      negate=True).then_inc(rowmax_ready, 1)
                recur(i)
                for h in (2 * hp, 2 * hp + 1):
                    drained(dve, ("S", j, h))
                    chain(dve.reciprocal(rinv[:, h % 2:h % 2 + 1], rowsum[:, h % 2:h % 2 + 1]))
                    dve.tensor_scalar(prob[:, h % 2, 0:n], prob[:, h % 2, 0:n], rinv[:, h % 2:h % 2 + 1], None,
                                      ALU.mult).then_inc(prob_ready, 1)
                if i % 4 == 1 and i > 4:
                    add_skip(i // 4 - 1)
            add_skip(SC - 1)

            for c in range(DC):
                b = (c % 2) * 1024
                gg, t = temp[:, b:b + 512], temp[:, b + 512:b + 1024]
                name = ("att", c)
                filled(dve, name)
                dve.wait_ge(gate_sig, 2 * (c + 1))
                mul(merged[:, c, :], pair(name)[:, 0:SEQ], gates[:, c, :]).then_inc(free_sem(name), 1)
                name = ("val", c)
                filled(dve, name)
                drained(dve, ("gg", c))
                mul(t, pair(name)[:, 0:SEQ], gg).then_inc(free_sem(name), 1)
                drained(dve, name)
                chain(mul(t, t, gates[:, DC + c, :]))
                drained(dve, ("att", c))
                dve.tensor_tensor(merged[:, c, :], merged[:, c, :], t, ALU.add).then_inc(merged_ready, 1)

            for i in range(TT):
                name, o = ("wout", i), (i % 2) * D
                filled(dve, name)
                dve.wait_ge(x_landed[i % 2], 16 * (i // 2 + 1))
                h = temp[:, o:o + D]
                dve.tensor_tensor(h, h, pair(name), ALU.add).then_inc(h1_ready, 1)
                dve.wait_ge(h1_ready, i + 1)
                dve.engine_nop().then_inc(free_sem(name), 1)
                normalise(TT + 1 + i, h, temp[:, 2 * D + o:3 * D + o], P)
                to_features(("hn2", i), hnT[:, :, i * P:(i + 1) * P], P, gffn)

            def step(ins):
                steps[0] += 1
                ins.then_inc(dve_step, 1)
                return steps[0]

            def top16(lists):
                found = [step(dve.max(vals[:, 0:8], src)) for vals, idx, src, scratch in lists]
                for n, (vals, idx, src, scratch) in enumerate(lists):
                    dve.wait_ge(dve_step, found[n])
                    dve.max_index(idx[:, 0:8], vals[:, 0:8], src)
                    found[n] = step(dve.match_replace(scratch, vals[:, 0:8], src, -3.0e38))
                for n, (vals, idx, src, scratch) in enumerate(lists):
                    dve.wait_ge(dve_step, found[n])
                    found[n] = step(dve.max(vals[:, 8:16], scratch))
                for n, (vals, idx, src, scratch) in enumerate(lists):
                    dve.wait_ge(dve_step, found[n])
                    ins = dve.max_index(idx[:, 8:16], vals[:, 8:16], scratch)
                return ins

            picks_before = lambda h: 2 * h if h < PH - 2 else PH - 2 + h

            def pick_here(h):
                dve.wait_ge(places_ready, 2 * h + 2)
                dve.wait_ge(topf_ready, h + 1)
                by_tile = pick[1].rearrange("p w (i k) -> p w i k", i=TT)
                chain(mul(by_tile, by_tile,
                          topf[:, 2 * h + 1].rearrange("p i w -> p w i").unsqueeze(3).to_broadcast([P, TOPK, TT, TOPK])))
                chain(dve.tensor_reduce(picked[:, 1, :, h, :], pick[1].rearrange("p w (i k) -> p i k w", i=TT), AX.X, ALU.add))

            chain(dve.tensor_copy(which, iota[:, 0:TOPK].unsqueeze(2).to_broadcast([P, TOPK, TT * TOPK])))

            def key_lists(n):
                drained(dve, ("sc", n))
                chain(top16([(topv[:, n, i, :], topi[:, n, i, :], score[:, n, i, :], work[:, i]) for i in range(TT)]))
            for h in range(PH + 1):
                g = h - 1
                if h < PH:
                    key_lists(2 * h)
                if g >= 0:
                    dve.wait_ge(cand_ready, g + 1)
                    chain(top16([(best[:, g, i, :], posu[:, g, i, :], cand[g % 2][:, i], cwork[:, i]) for i in range(TT)]))
                    dve.tensor_scalar(partu[:, 0], posu[:, g], 3, None, ALU.logical_shift_right)
                    chain(dve.tensor_scalar(partu[:, 1], posu[:, g], 7, None, ALU.bitwise_and))
                    dve.tensor_copy(partf, partu).then_inc(eighths_ready, 1)
                if h < PH:
                    key_lists(2 * h + 1)
                    dve.engine_nop().then_inc(lists_ready, 1)
                if g == PH - 1:
                    dve.tensor_tensor(gexp, best, best[:, :, :, 0:1].to_broadcast([P, PH, TT, TOPK]), ALU.subtract)\
                       .then_inc(gates_raw, 1)
                    pick_here(g - 1)
                if g >= 0:
                    dve.wait_ge(split_ready, g + 1)
                    for a in range(2):
                        if g >= 1:
                            dve.wait_ge(pick_done, min(picks_before(g - 1) + a + 1, picks_before(g)))
                        dve.tensor_tensor(pick[a], place_ab[:, a].unsqueeze(1).to_broadcast([P, TOPK, TT * TOPK]), which,
                                          ALU.is_equal).then_inc(places_ready, 1)
            dve.sem_inc(u_split, 2)
            dve.sem_inc(v_split, 2)
            dve.sem_inc(w_ready, 1)

            def split_tokens(hf):
                dve.wait_ge(hn2_hi, hf + 1)
                dve.tensor_tensor(hn_lo[:], hn_raw, hn_hi[:].bitcast(F32), ALU.subtract).then_inc(hn2_split, 1)

            pick_here(PH - 1)
            dve.wait_ge(gates_exp, 1)
            gflat = gexp.rearrange("p h i k -> p (h i) k")
            chain(dve.tensor_reduce(norm, gflat, AX.X, ALU.add))
            chain(dve.reciprocal(norm, norm))
            chain(mul(gflat, gflat, norm.unsqueeze(2).to_broadcast([P, PH * TT, TOPK])))
            dve.wait_ge(pick_done, picks_before(PH))
            dve.tensor_copy(picked[:, 2], gexp.rearrange("p h i k -> p i h k")).then_inc(chosen_ready, 1)
            split_tokens(0)

            for a in range(3):
                drained(dve, ("idx", a))

            def add_residual(g):
                dve.wait_ge(h1_landed[g % 2], 16 * (g // 2 + 1))
                dve.wait_ge(acc_ready, g // 2 + 1)
                h = h1s[:, g % 2]
                dve.tensor_tensor(h, h, pairs[g % 2][:, :], ALU.add).then_inc(h2_ready, 1)

            def final(g):
                h = h1s[:, g % 2]
                dve.wait_ge(root_ready, 10 + g)
                chain(dve.reciprocal(st[:, 41 + g:42 + g], st[:, 25 + g:26 + g]))
                dve.scalar_tensor_tensor(out=h, in0=h, scalar=st[:, 41 + g:42 + g], in1=gout, op0=ALU.mult,
                                         op1=ALU.mult).then_inc(out_ready, 1)

            dve.wait_ge(numbers_ready, 1)
            dve.wait_ge(gout_landed, 16)
            dve.wait_ge(hn2_stored, 32)
            dve.wait_ge(h1_stored, 16 * TT)
            for hf in range(2):
                half = hf * P

                def split_u(s, n):
                    dve.wait_ge(u_hi_ready, n + half + 1)
                    dve.wait_ge(u_product, n + half + 2)
                    dve.tensor_tensor(u_lo[:], raw[:, s, :], u_hi[:, s, :].bitcast(F32), ALU.subtract).then_inc(u_split, 1)

                if hf:
                    split_tokens(1)
                    dve.wait_ge(v_product, P + 2)
                with dve.Fori(0, HALF // 16) as it:
                    for b in range(4):
                        g = it * 4 + b + hf * (HALF // 4)
                        for a, used, ready in ((0, oh1_ready, oh1_marked), (1, oh2_ready, oh2_marked)):
                            dve.wait_ge(used, g + 1)
                            key = keys_chosen[:, a, bass.ds(it * 16 + b * 4 + hf * HALF, 4)].unsqueeze(1)
                            dve.tensor_tensor(marks[a][b % 2], numbers, key.to_broadcast([P, P, 4]), ALU.is_equal)\
                               .then_inc(ready, 1)
                split_u(0, 0)
                if hf:
                    add_residual(0)
                    add_residual(1)
                    final(0)
                    final(1)
                dve.wait_ge(gmat_free, 4 + (hf + 1) * HALF // 4)

                def split_v(s, n):
                    for b in range(2):
                        c = slice(b * 512, (b + 1) * 512)
                        dve.wait_ge(v_hi_ready, (n + half) * 2 + 1 + b)
                        ins = dve.tensor_tensor(v_lo[:, c], raw[:, 2 + s, c], v_hi[:, c].bitcast(F32), ALU.subtract)
                    ins.then_inc(v_split, 1)

                def weigh(s, n, row):
                    dve.wait_ge(gelu_done, n + half + 2)
                    dve.wait_ge(w_ready, n + half + 1)
                    dve.tensor_tensor(wfull[:], act[:, s, :], G[:, row, :].rearrange("p a t -> p (a t)"), ALU.mult)\
                       .then_inc(w_full, 1)
                    dve.wait_ge(w_full, n + half + 3)
                    dve.wait_ge(v_product, n + half + 1)
                    dve.tensor_copy(w_hi[:, s, :], wfull[:]).then_inc(w_rounded, 1)
                    dve.wait_ge(w_rounded, n + half + 1)
                    dve.tensor_tensor(w_lo[:, s, :], wfull[:], w_hi[:, s, :].bitcast(F32), ALU.subtract).then_inc(w_ready, 1)

                with dve.Fori(0, P // 2 - 1) as it:
                    for s in range(2):
                        m = it * 2 + s
                        split_u(1 - s, m + 1)
                        weigh(s, m, bass.ds(m, 1))
                        split_v(s, m)
                for s in range(2):
                    if s == 0:
                        split_u(1, P - 1)
                    weigh(s, P - 2 + s, slice(P - 2 + s, P - 1 + s))
                    split_v(s, P - 2 + s)
            for g in (2, 3):
                add_residual(g)
            for g in (2, 3):
                final(g)


def kernel(**inputs):
    import numpy as np
    import concourse.bacc as bacc
    from concourse.bass_utils import run_bass_kernel_spmd

    a = {k: np.asarray(v) for k, v in inputs.items()}

    def chunks(w):
        k, n = w.shape
        return w.reshape(k // P, P, n // P, P).transpose(2, 1, 0, 3).reshape(n // P, P, k)

    def rows(w):
        return w.reshape(w.shape[0] // P, P, -1).transpose(1, 0, 2)

    def states(w):
        return np.moveaxis(w.reshape((NT, 2 * ST) + w.shape[2:]), 1, 0)

    w_in = a["w_in"][0]
    s1, s2, s3 = AW, 2 * AW, 3 * AW
    s4, s5 = s3 + HEADS, s3 + HEADS + SW
    data = {
        "x": a["x"][0], "meta": a["meta_tokens"],
        "g_mix": a["mix_norm_g"].reshape(DC, P).T, "g_ffn": a["ffn_norm_g"].reshape(DC, P).T,
        "g_out": a["out_norm_g"],
        "w_u": chunks(w_in[:, s4:s5]), "w_k": chunks(w_in[:, s1:s2]), "w_q": chunks(w_in[:, 0:s1]),
        "w_v": rows(w_in[:, s2:s3]), "w_f": rows(w_in[:, s3:s4]), "w_g": chunks(w_in[:, s5:]),
        "b_f": a["b_forget"].reshape(HEADS, 1), "b_g": a["b_gate"].reshape(2 * DC, P).T,
        "w_att": chunks(a["w_att_branch"][0]), "w_val": chunks(a["w_glu_val"][0]), "w_gg": chunks(a["w_glu_gate"][0]),
        "w_out": rows(a["w_out"][0]),
        "a_re": states(a["ssm_a_re"][0]), "a_im": states(a["ssm_a_im"][0]),
        "log_dt": states(np.repeat(a["ssm_log_dt"][0][:, None], ST, axis=1)),
        "b_re": states(a["ssm_b_re"][0]), "b_im": states(a["ssm_b_im"][0]),
        "c_re": states(a["ssm_c_re"][0].transpose(0, 2, 1)), "c_im": states(a["ssm_c_im"][0].transpose(0, 2, 1)),
        "d_skip": a["ssm_d"].reshape(SC, P).T,
        "w_query": chunks(a["w_query"][0]),
        "keys": a["sub_keys"][0].reshape(HK, NKEY, P).transpose(2, 0, 1),
        "expert_u": a["expert_u"].reshape(P, P, DC, P).transpose(0, 3, 2, 1).reshape(P, P, D),
        "expert_v": a["expert_v"].reshape(P, P, D),
    }
    nc = bacc.Bacc("TRN2", target_bir_lowering=False, num_devices=1)
    arrays, args = {}, []
    for name, v in data.items():
        v = np.ascontiguousarray(v)
        arrays[f"in_{name}"] = v
        args.append(nc.dram_tensor(f"in_{name}", v.shape, mybir.dt.from_np(v.dtype), kind="ExternalInput").ap())
    args.append(nc.dram_tensor("out", (SEQ, D), F32, kind="ExternalOutput").ap())
    hybrid_program(nc, *args)
    r = run_bass_kernel_spmd(nc, [arrays], core_ids=[0])
    return r.results[0]["out"].reshape(1, SEQ, D)
```
